# Optimizing a Trainium2 kernel written in Bass

```python
import math
import jax, jax.numpy as jnp
from jax import lax
import numpy as np

D_MODEL = 1024
BATCH = 1
SEQ = 512
DEPTH = 2
DEC_BATCH = 8
DEC_SEQ = 1
PAST_LEN = 512
PAGE_SIZE = 128

HEAD_DIM = 64
GROUP_W = D_MODEL // 2
H_A = GROUP_W // HEAD_DIM
H_B = GROUP_W // HEAD_DIM
H_C = GROUP_W // (2 * HEAD_DIM)
DV_C = 2 * HEAD_DIM
N_BLK_D = GROUP_W // HEAD_DIM
D_FF = 4 * D_MODEL
P_DIM = 256
RET_CHUNK = 64
Q_BLOCK = 128
CONV_W = 4
LRU_C = 8.0
RWKV_LORA_W = 64
RWKV_LORA_A = 64
RWKV_LORA_G = 128
N_NORMS = 8
ROPE_BASE = 10000.0
EPS = 1e-6
RWKV_GN_EPS = 64e-5

kernel_name = 'hybrid_retention_rwkv7_diffattn_rglru_step'

F32 = jnp.float32

def rmsnorm(x, g):
    x32 = x.astype(F32)
    y = x32 * lax.rsqrt(jnp.mean(x32 * x32, axis=-1, keepdims=True) + EPS)
    return (y * g.astype(F32)).astype(x.dtype)

def head_layernorm(x, eps):
    x = x.astype(F32)
    xc = x - jnp.mean(x, axis=-1, keepdims=True)
    return xc * lax.rsqrt(jnp.mean(xc * xc, axis=-1, keepdims=True) + eps)

def swiglu(x, w_in, w_out):
    gate, up = jnp.split(x @ w_in, 2, axis=-1)
    return (jax.nn.silu(gate) * up) @ w_out

def rotary(x, pos):
    half = x.shape[-1] // 2
    freq = 1.0 / (ROPE_BASE ** jnp.linspace(0.0, 1.0, half, dtype=F32))
    ang = pos[:, None] * freq[None, :]
    cos = jnp.cos(ang)[None, :, None, :]
    sin = jnp.sin(ang)[None, :, None, :]
    x32 = x.astype(F32)
    x1, x2 = x32[..., :half], x32[..., half:]
    return jnp.concatenate([x1 * cos - x2 * sin, x2 * cos + x1 * sin], axis=-1)

def retention_chunkwise(q, k, v, s0):
    B, L, H, _ = q.shape
    dv = v.shape[-1]
    c = math.gcd(L, RET_CHUNK)
    n = L // c
    lg = jnp.log1p(-jnp.exp2(-5.0 - jnp.arange(H, dtype=F32)))
    idx = jnp.arange(c, dtype=F32)
    rel = idx[:, None] - idx[None, :]
    dmask = jnp.where(rel[None] >= 0, jnp.exp(jnp.maximum(rel, 0.0)[None] * lg[:, None, None]), 0.0)
    q_dec = jnp.exp((idx[None, :] + 1.0) * lg[:, None])
    k_dec = jnp.exp((c - 1.0 - idx[None, :]) * lg[:, None])
    c_dec = jnp.exp(c * lg)

    def chunks(t):
        return t.reshape(B, n, c, H, t.shape[-1]).transpose(1, 0, 3, 2, 4)

    def step(s, inp):
        qc, kc, vc = inp
        att = jnp.einsum('bhid,bhjd->bhij', qc, kc) * dmask
        o = jnp.einsum('bhij,bhjv->bhiv', att, vc) + jnp.einsum('bhid,bhdv->bhiv', qc, s) * q_dec[..., None]
        s = s * c_dec[:, None, None] + jnp.einsum('bhjd,bhjv->bhdv', kc * k_dec[..., None], vc)
        return s, o

    s, o = lax.scan(step, s0.astype(F32), (chunks(q), chunks(k), chunks(v)))
    return o.transpose(1, 0, 3, 2, 4).reshape(B, L, H, dv), s

def rwkv7_scan(r, w, k, v, kk, a, s0):
    def step(s, inp):
        rt, wt, kt, vt, kkt, at = inp
        sa = jnp.einsum('bhvk,bhk->bhv', s, -kkt)
        s = s * wt[:, :, None, :] + sa[..., None] * (kkt * at)[:, :, None, :] + vt[..., None] * kt[:, :, None, :]
        return s, jnp.einsum('bhvk,bhk->bhv', s, rt)

    seq = tuple(t.transpose(1, 0, 2, 3) for t in (r, w, k, v, kk, a))
    s, o = lax.scan(step, s0.astype(F32), seq)
    return o.transpose(1, 0, 2, 3), s

def token_shift(u, buf):
    full = jnp.concatenate([buf.astype(u.dtype), u], axis=1)
    return full[:, :-1], full[:, -1:]

def mix_even(xn, pos, s_ret, s_rwkv, buf, prm, j):
    B, L, _ = xn.shape
    dt = xn.dtype
    u = xn @ prm['ab_w_in'][j]
    qa, ka, va, ga, rr, kr, vr, zr = jnp.split(u, 8, axis=-1)
    heads = lambda t, H: t.reshape(B, L, H, -1)
    q = rotary(heads(qa, H_A), pos)
    k = rotary(heads(ka, H_A), pos) * (HEAD_DIM ** -0.5)
    o_a, s_ret_new = retention_chunkwise(q, k, heads(va, H_A).astype(F32), s_ret)
    o_a = head_layernorm(o_a, EPS).reshape(B, L, GROUP_W).astype(dt) * jax.nn.silu(ga)
    cur = jnp.concatenate([rr, kr, vr, zr], axis=-1)
    prev, buf_new = token_shift(cur, buf)
    pr, pk, pv, pz = jnp.split(prev, 4, axis=-1)
    mu = prm['rwkv_mu'][j]
    lerp = lambda x, xp, m: x + (xp - x) * m
    r = lerp(rr, pr, mu[0])
    kx = lerp(kr, pk, mu[1])
    vx = lerp(vr, pv, mu[2])
    zw = lerp(zr, pz, mu[3])
    za = lerp(zr, pz, mu[4])
    zg = lerp(zr, pz, mu[5])
    wpre = (prm['rwkv_w0'][j] + jnp.tanh(zw @ prm['rwkv_w1'][j]) @ prm['rwkv_w2'][j]).astype(F32)
    decay = jnp.exp(-jnp.exp(-jax.nn.softplus(-wpre) - 0.5))
    a = jax.nn.sigmoid((prm['rwkv_a0'][j] + (za @ prm['rwkv_a1'][j]) @ prm['rwkv_a2'][j]).astype(F32))
    g = jax.nn.sigmoid(zg @ prm['rwkv_g1'][j]) @ prm['rwkv_g2'][j]
    k32 = kx.astype(F32)
    kk = heads(k32 * prm['rwkv_kk'][j].astype(F32), H_B)
    kk = kk / jnp.maximum(jnp.sqrt(jnp.sum(kk * kk, axis=-1, keepdims=True)), 1e-12)
    k32 = k32 * (1.0 + (a - 1.0) * prm['rwkv_ka'][j].astype(F32))
    r_h, k_h, v_h, a_h = heads(r.astype(F32), H_B), heads(k32, H_B), heads(vx.astype(F32), H_B), heads(a, H_B)
    o_b, s_rwkv_new = rwkv7_scan(r_h, heads(decay, H_B), k_h, v_h, kk, a_h, s_rwkv)
    ln = prm['rwkv_ln'][j].astype(F32).reshape(2, H_B, HEAD_DIM)
    o_b = head_layernorm(o_b, RWKV_GN_EPS) * ln[0] + ln[1]
    o_b = o_b + jnp.sum(r_h * k_h * prm['rwkv_rk'][j].astype(F32), axis=-1, keepdims=True) * v_h
    o_b = o_b.reshape(B, L, GROUP_W).astype(dt) * g
    out = jnp.concatenate([o_a, o_b], axis=-1) @ prm['ab_w_out'][j]
    return out, s_ret_new.astype(dt), s_rwkv_new.astype(dt), buf_new

def diff_attn_prompt(q, k, v, lam):
    B, L, H, _, dh = q.shape
    blk = math.gcd(L, Q_BLOCK)
    nb = L // blk
    scale = dh ** -0.5
    qb = q.reshape(B, nb, blk, H, 2, dh).transpose(1, 0, 2, 3, 4, 5)
    kpos = jnp.arange(L)

    def one(args):
        qi, q0 = args
        s = jnp.einsum('bqhmd,bkhmd->bhmqk', qi, k).astype(F32) * scale
        mask = kpos[None, :] <= (q0 + jnp.arange(blk))[:, None]
        pr = jax.nn.softmax(jnp.where(mask, s, -jnp.inf), axis=-1)
        wgt = pr[:, :, 0] - lam * pr[:, :, 1]
        return jnp.einsum('bhqk,bkhv->bqhv', wgt.astype(v.dtype), v)

    o = lax.map(one, (qb, jnp.arange(nb) * blk))
    return o.transpose(1, 0, 2, 3, 4).reshape(B, L, H, v.shape[-1])

def diff_attn_decode(q, k, v, kp, vp, lam):
    Ld, dh = q.shape[1], q.shape[-1]
    P = kp.shape[1]
    scale = dh ** -0.5
    s_past = jnp.einsum('bqhmd,bkhmd->bhmqk', q, kp).astype(F32) * scale
    s_new = jnp.einsum('bqhmd,bkhmd->bhmqk', q, k).astype(F32) * scale
    causal = jnp.arange(Ld)[None, :] <= jnp.arange(Ld)[:, None]
    s_new = jnp.where(causal, s_new, -jnp.inf)
    pr = jax.nn.softmax(jnp.concatenate([s_past, s_new], axis=-1), axis=-1)
    wgt = (pr[:, :, 0] - lam * pr[:, :, 1]).astype(v.dtype)
    return (jnp.einsum('bhqk,bkhv->bqhv', wgt[..., :P], vp)
            + jnp.einsum('bhqk,bkhv->bqhv', wgt[..., P:], v))

def causal_conv(x, buf, w, b):
    L = x.shape[1]
    full = jnp.concatenate([buf.astype(x.dtype), x], axis=1)
    y = sum(full[:, t:t + L] * w[t] for t in range(CONV_W)) + b
    return y, full[:, L:]

def rglru(x, h0, wa, ba, wi, bi, lam):
    B, L, C = x.shape
    x32 = x.astype(F32)
    xb = x32.reshape(B, L, N_BLK_D, -1)
    r = jax.nn.sigmoid(jnp.einsum('blnd,nde->blne', xb, wa.astype(F32)).reshape(B, L, C) + ba.astype(F32))
    ig = jax.nn.sigmoid(jnp.einsum('blnd,nde->blne', xb, wi.astype(F32)).reshape(B, L, C) + bi.astype(F32))
    log_a = -LRU_C * r * jax.nn.softplus(-lam.astype(F32))
    a = jnp.exp(log_a)
    bt = jnp.sqrt(-jnp.expm1(2.0 * log_a)) * (ig * x32)
    bt = bt.at[:, 0].add(a[:, 0] * h0.astype(F32))

    def comb(e1, e2):
        a1, b1 = e1
        a2, b2 = e2
        return a1 * a2, a2 * b1 + b2

    _, h = lax.associative_scan(comb, (a, bt), axis=1)
    return h, h[:, -1]

def mix_odd(xn, lru_h, lru_buf, past, prm, i, j):
    B, L, _ = xn.shape
    dt = xn.dtype
    u = xn @ prm['cd_w_in'][j]
    qc, kc, vc, xr, gr = jnp.split(u, 5, axis=-1)
    q = qc.reshape(B, L, H_C, 2, HEAD_DIM)
    k = kc.reshape(B, L, H_C, 2, HEAD_DIM)
    v = vc.reshape(B, L, H_C, DV_C)
    lp = prm['diff_lam'][j].astype(F32)
    lam_init = 0.8 - 0.6 * math.exp(-0.3 * i)
    lam = jnp.exp(jnp.sum(lp[0] * lp[1])) - jnp.exp(jnp.sum(lp[2] * lp[3])) + lam_init
    if past is None:
        o_c = diff_attn_prompt(q, k, v, lam)
    else:
        o_c = diff_attn_decode(q, k, v, past[0], past[1], lam)
    o_c = (rmsnorm(o_c, prm['diff_subln'][j]) * (1.0 - lam_init)).reshape(B, L, GROUP_W)
    xconv, buf_new = causal_conv(xr, lru_buf, prm['lru_conv_w'][j], prm['lru_conv_b'][j])
    hseq, h_last = rglru(xconv, lru_h, prm['lru_wa'][j], prm['lru_ba'][j], prm['lru_wi'][j],
                         prm['lru_bi'][j], prm['lru_lambda'][j])
    o_d = hseq.astype(dt) * jax.nn.gelu(gr)
    out = jnp.concatenate([o_c, o_d], axis=-1) @ prm['cd_w_out'][j]
    return out, k.reshape(B, L, H_C, 2 * HEAD_DIM), v, h_last.astype(dt), buf_new

def trunk(x, p, pos0, s_ret, s_rwkv, s_shift, s_lru_h, s_lru_conv, pages, prm):
    B, L, _ = x.shape
    pos = pos0 + jnp.arange(L, dtype=F32)
    ret_l, rwkv_l, shift_l, k_l, v_l, lh_l, lc_l = [], [], [], [], [], [], []
    h = x
    for i in range(DEPTH):
        j = i // 2
        g = prm['norm_g'][i]
        h = h + 0.5 * rmsnorm(swiglu(rmsnorm(h, g[0]), prm['ffn_w_in'][i, 0], prm['ffn_w_out'][i, 0]), g[1])
        xn = rmsnorm(h, g[2])
        if i % 2 == 0:
            mo, sr, sw, sb = mix_even(xn, pos, s_ret[j], s_rwkv[j], s_shift[j], prm, j)
            ret_l.append(sr)
            rwkv_l.append(sw)
            shift_l.append(sb)
        else:
            past = None
            if pages is not None:
                ck, cv, pt = pages
                past = (ck[j][pt].reshape(B, -1, H_C, 2, HEAD_DIM),
                        cv[j][pt].reshape(B, -1, H_C, DV_C))
            mo, kn, vn, lh, lc = mix_odd(xn, s_lru_h[j], s_lru_conv[j], past, prm, i, j)
            k_l.append(kn)
            v_l.append(vn)
            lh_l.append(lh)
            lc_l.append(lc)
        h = h + rmsnorm(mo, g[3])
        h = h + 0.5 * rmsnorm(swiglu(rmsnorm(h, g[4]), prm['ffn_w_in'][i, 1], prm['ffn_w_out'][i, 1]), g[5])
        gate = jax.nn.sigmoid(rmsnorm(h, g[6]) @ prm['ple_gate_w'][i])
        h = h + rmsnorm(gate * (p[i] @ prm['ple_w'][i]), g[7])
    st = lambda lst: jnp.stack(lst, axis=0)
    return h, st(k_l), st(v_l), st(ret_l), st(rwkv_l), st(shift_l), st(lh_l), st(lc_l)

def setup_inputs(seed: int = 0) -> dict:
    key = jax.random.key(seed)
    ks = iter(jax.random.split(key, 64))

    def nrm(shape, scale):
        return jax.random.normal(next(ks), shape, F32) * scale

    def unif(shape, lo, hi):
        return jax.random.uniform(next(ks), shape, F32, lo, hi)

    n_a = (DEPTH + 1) // 2
    n_c = DEPTH // 2
    n_pages = PAST_LEN // PAGE_SIZE
    n_pool = (5 * DEC_BATCH * n_pages + 3) // 4
    W = GROUP_W
    page_table = jax.random.permutation(next(ks), n_pool)[:DEC_BATCH * n_pages]
    page_table = page_table.reshape(DEC_BATCH, n_pages).astype(jnp.int32)
    s_lru = unif((n_c, W), 0.9, 0.999) ** (1.0 / LRU_C)
    return {
        'x_prompt': nrm((BATCH, SEQ, D_MODEL), 1.0),
        'x_sample': nrm((DEC_BATCH, DEC_SEQ, D_MODEL), 1.0),
        'cache_k': nrm((n_c, n_pool, PAGE_SIZE, H_C, 2 * HEAD_DIM), 1.0),
        'cache_v': nrm((n_c, n_pool, PAGE_SIZE, H_C, DV_C), 1.0),
        'state_ret': nrm((n_a, DEC_BATCH, H_A, HEAD_DIM, HEAD_DIM), 0.5),
        'state_rwkv': nrm((n_a, DEC_BATCH, H_B, HEAD_DIM, HEAD_DIM), 0.5),
        'state_rwkv_shift': nrm((n_a, DEC_BATCH, 1, 4 * W), 1.0),
        'state_lru_h': nrm((n_c, DEC_BATCH, W), 0.5),
        'state_lru_conv': nrm((n_c, DEC_BATCH, CONV_W - 1, W), 1.0),
        'page_table': page_table,
        'p_prompt': nrm((DEPTH, BATCH, SEQ, P_DIM), 1.0),
        'p_sample': nrm((DEPTH, DEC_BATCH, DEC_SEQ, P_DIM), 1.0),
        'norm_g': 1.0 + nrm((DEPTH, N_NORMS, D_MODEL), 0.05),
        'ffn_w_in': nrm((DEPTH, 2, D_MODEL, 2 * D_FF), D_MODEL ** -0.5),
        'ffn_w_out': nrm((DEPTH, 2, D_FF, D_MODEL), D_FF ** -0.5),
        'ple_w': nrm((DEPTH, P_DIM, D_MODEL), P_DIM ** -0.5),
        'ple_gate_w': nrm((DEPTH, D_MODEL, D_MODEL), D_MODEL ** -0.5),
        'ab_w_in': nrm((n_a, D_MODEL, 8 * W), D_MODEL ** -0.5),
        'ab_w_out': nrm((n_a, 2 * W, D_MODEL), (2 * W) ** -0.5),
        'rwkv_mu': unif((n_a, 6, W), 0.0, 1.0),
        'rwkv_w0': nrm((n_a, W), 0.5) - 0.5,
        'rwkv_w1': nrm((n_a, W, RWKV_LORA_W), W ** -0.5),
        'rwkv_w2': nrm((n_a, RWKV_LORA_W, W), 0.1 * RWKV_LORA_W ** -0.5),
        'rwkv_a0': nrm((n_a, W), 0.1),
        'rwkv_a1': nrm((n_a, W, RWKV_LORA_A), W ** -0.5),
        'rwkv_a2': nrm((n_a, RWKV_LORA_A, W), 0.1 * RWKV_LORA_A ** -0.5),
        'rwkv_g1': nrm((n_a, W, RWKV_LORA_G), W ** -0.5),
        'rwkv_g2': nrm((n_a, RWKV_LORA_G, W), RWKV_LORA_G ** -0.5),
        'rwkv_kk': 0.85 + nrm((n_a, W), 0.05),
        'rwkv_ka': 1.0 + nrm((n_a, W), 0.05),
        'rwkv_rk': nrm((n_a, H_B, HEAD_DIM), 0.1),
        'rwkv_ln': jnp.stack([1.0 + nrm((n_a, W), 0.05), nrm((n_a, W), 0.02)], axis=1),
        'cd_w_in': nrm((n_c, D_MODEL, 5 * W), D_MODEL ** -0.5),
        'cd_w_out': nrm((n_c, 2 * W, D_MODEL), (2 * W) ** -0.5),
        'diff_lam': nrm((n_c, 4, HEAD_DIM), 0.1),
        'diff_subln': 1.0 + nrm((n_c, DV_C), 0.05),
        'lru_conv_w': nrm((n_c, CONV_W, W), CONV_W ** -0.5),
        'lru_conv_b': nrm((n_c, W), 0.02),
        'lru_wa': nrm((n_c, N_BLK_D, HEAD_DIM, HEAD_DIM), HEAD_DIM ** -0.5),
        'lru_ba': nrm((n_c, W), 0.02),
        'lru_wi': nrm((n_c, N_BLK_D, HEAD_DIM, HEAD_DIM), HEAD_DIM ** -0.5),
        'lru_bi': nrm((n_c, W), 0.02),
        'lru_lambda': jnp.log(s_lru) - jnp.log1p(-s_lru),
    }

def reference(x_prompt, x_sample, cache_k, cache_v, state_ret, state_rwkv, state_rwkv_shift,
              state_lru_h, state_lru_conv, page_table, p_prompt, p_sample, norm_g, ffn_w_in,
              ffn_w_out, ple_w, ple_gate_w, ab_w_in, ab_w_out, rwkv_mu, rwkv_w0, rwkv_w1, rwkv_w2,
              rwkv_a0, rwkv_a1, rwkv_a2, rwkv_g1, rwkv_g2, rwkv_kk, rwkv_ka, rwkv_rk, rwkv_ln,
              cd_w_in, cd_w_out, diff_lam, diff_subln, lru_conv_w, lru_conv_b, lru_wa, lru_ba,
              lru_wi, lru_bi, lru_lambda):
    prm = dict(norm_g=norm_g, ffn_w_in=ffn_w_in, ffn_w_out=ffn_w_out, ple_w=ple_w,
               ple_gate_w=ple_gate_w, ab_w_in=ab_w_in, ab_w_out=ab_w_out, rwkv_mu=rwkv_mu,
               rwkv_w0=rwkv_w0, rwkv_w1=rwkv_w1, rwkv_w2=rwkv_w2, rwkv_a0=rwkv_a0,
               rwkv_a1=rwkv_a1, rwkv_a2=rwkv_a2, rwkv_g1=rwkv_g1, rwkv_g2=rwkv_g2,
               rwkv_kk=rwkv_kk, rwkv_ka=rwkv_ka, rwkv_rk=rwkv_rk, rwkv_ln=rwkv_ln,
               cd_w_in=cd_w_in, cd_w_out=cd_w_out, diff_lam=diff_lam, diff_subln=diff_subln,
               lru_conv_w=lru_conv_w, lru_conv_b=lru_conv_b, lru_wa=lru_wa, lru_ba=lru_ba,
               lru_wi=lru_wi, lru_bi=lru_bi, lru_lambda=lru_lambda)
    dt = x_prompt.dtype
    bp = x_prompt.shape[0]
    n_a = state_ret.shape[0]
    n_c = state_lru_h.shape[0]
    yp, kp, vp, rp, wp, sp, hp, cp = trunk(
        x_prompt, p_prompt, 0,
        jnp.zeros((n_a, bp, H_A, HEAD_DIM, HEAD_DIM), dt),
        jnp.zeros((n_a, bp, H_B, HEAD_DIM, HEAD_DIM), dt),
        jnp.zeros((n_a, bp, 1, 4 * GROUP_W), dt),
        jnp.zeros((n_c, bp, GROUP_W), dt),
        jnp.zeros((n_c, bp, CONV_W - 1, GROUP_W), dt),
        None, prm)
    ys, ks_, vs, rs, ws, ss, hs, cs = trunk(
        x_sample, p_sample, PAST_LEN, state_ret, state_rwkv, state_rwkv_shift,
        state_lru_h, state_lru_conv, (cache_k, cache_v, page_table), prm)
    return (yp, ys, kp, vp, rp, wp, sp, hp, cp, ks_, vs, rs, ws, ss, hs, cs)


_drawn_inputs = setup_inputs


def setup_inputs(seed=0):
    import zlib

    import numpy as np

    out = dict(_drawn_inputs(seed))
    spreads = {}
    factors = {'rwkv_w1': 4.931,
     'rwkv_w2': 4.585,
     'rwkv_kk': 20.437,
     'diff_subln': 8.083,
     'lru_ba': 8.0,
     'lru_bi': 7.455}
    for name, (base, spread) in spreads.items():
        noise = np.random.default_rng([zlib.crc32(name.encode()), seed]).standard_normal(out[name].shape)
        drawn = base * np.exp(spread * noise) if base else spread * noise
        out[name] = __import__('jax').numpy.asarray(drawn.astype(out[name].dtype))
    for name, factor in factors.items():
        out[name] = (out[name] * factor).astype(out[name].dtype)
    return out
```

```python
import math
from contextlib import ExitStack

import numpy as np

import concourse.bass as bass
from concourse import mybir
from concourse.alu_op_type import AluOpType as ALU

ACT = mybir.ActivationFunctionType
AX = mybir.AxisListType
F32 = mybir.dt.float32
F32R = mybir.dt.float32r
I32 = mybir.dt.int32

P = 128
SEQ = 512
NS = 8
T = SEQ + NS
TH = T // 2
D = 1024
KT = D // P
GW = 512
GT = GW // P
HD = 64
EPS = 1e-6
GN_EPS = 64e-5
CH = 64
NCH = SEQ // CH
TOK_TILES = [0, 128, 256, 384, T - P]
NEG = -1e30
LAM_INIT = 0.8 - 0.6 * math.exp(-0.3 * 1)
PAGES = 4

CONST = {}
_at = 0
for _n, _w in [("ident", 128), ("bones", 128), ("center", 128), ("rot", 128), ("causal_t", 128),
               ("causal_add", 128), ("m_a", 128), ("m_at", 128), ("m_e", 128), ("m_s", 128),
               ("m_i", 128), ("stack", 64), ("hsel", 2), ("ones2", 2), ("g511", 4), ("gam", 4),
               ("bsel", 2)]:
    CONST[_n] = (_at, _w)
    _at += _w
NCONST = _at

VEC = {}
_at = 0
for _n, _w in [("mu", 24), ("w0", 4), ("a0", 4), ("kk", 4), ("ka", 4), ("rk", 4), ("ln", 8),
               ("conv_w", 16), ("conv_b", 4), ("ba", 4), ("bi", 4), ("lam", 4), ("subln", 1)]:
    VEC[_n] = (_at, _w)
    _at += _w
NVEC = _at


def host_constants():
    c = np.zeros((P, NCONST), np.float32)

    def put(name, a):
        s, w = CONST[name]
        c[:, s:s + w] = a

    i = np.arange(P)
    blk = (i[:, None] // HD) == (i[None, :] // HD)
    r, q = i[:, None] % HD, i[None, :] % HD
    same16 = (r // 16) == (q // 16)
    put("ident", np.eye(P))
    put("bones", blk)
    put("center", np.eye(P) - blk / HD)
    rot = np.zeros((P, P))
    for m in range(P):
        if m % HD < 32:
            rot[m + 32, m] = -1
        else:
            rot[m - 32, m] = 1
    put("rot", rot)
    put("causal_t", i[:, None] <= i[None, :])
    put("causal_add", np.where(i[None, :] > i[:, None], NEG, 0.0))
    put("m_a", -1.0 * (blk & (q < r) & same16))
    put("m_at", -1.0 * (blk & (r < q) & same16))
    put("m_e", 1.0 * (blk & (q < r) & ~same16))
    put("m_s", 1.0 * (blk & (r < q)))
    put("m_i", 1.0 * (blk & (r <= q)))
    put("stack", np.vstack([np.eye(HD)] * 2))
    put("hsel", np.stack([i < HD, i >= HD], 1) / HD)
    put("ones2", np.ones((P, 2)))
    put("bsel", np.stack([i < HD, i >= HD], 1))
    head = np.arange(8)
    lg = np.log1p(-np.exp2(-5.0 - head))
    hp = 2 * np.arange(GT)[None, :] + (i[:, None] // HD)
    put("g511", np.exp((SEQ - 1) * lg[hp]))
    put("gam", np.exp(lg[hp]))
    pos = np.concatenate([np.arange(SEQ), np.full(NS, SEQ)]).astype(np.float64)
    freq = 1.0 / (10000.0 ** np.linspace(0.0, 1.0, 32))
    ang = pos[None, :].astype(np.float32) * freq[i % 32].astype(np.float32)[:, None]
    rope = np.stack([np.cos(ang), np.sin(ang)], 1).astype(np.float32)
    t = np.concatenate([np.arange(SEQ), np.zeros(NS)])
    sample = (np.arange(T) >= SEQ)
    dq = np.exp(t[None, None, :] * lg[hp][:, :, None])
    dk = np.exp(-t[None, None, :] * lg[hp][:, :, None]) * HD ** -0.5
    decay = np.stack([dq, dk], 1).astype(np.float32)
    reset = (np.arange(SEQ) % CH != 0).astype(np.float32)[None].repeat(P, 0)
    return c, rope.reshape(P, 2 * T), decay.reshape(P, 2 * GT * T), reset


class Steps:

    def __init__(self, eng, sem):
        self.eng, self.sem, self.n = eng, sem, 0

    def __call__(self, ins):
        self.n += 1
        ins.then_inc(self.sem, 1)
        return ins

    def settle(self):
        self.eng.wait_ge(self.sem, self.n)


def build(nc, I, O):
    ctx = ExitStack()
    with ctx:
        sems = {}

        def sem(name):
            if name not in sems:
                sems[name] = ctx.enter_context(nc.semaphore(name))
            return sems[name]

        base = (nc.sbuf_base + 63) // 64 * 64
        top = [base]

        def at(name, shape, offset, dt=F32):
            return nc.alloc_sbuf_tensor_at(name, shape, dt, offset=offset)

        def new(name, shape, dt=F32):
            n = int(np.prod(shape[1:])) * 4
            o = top[0]
            top[0] += (n + 31) // 32 * 32
            assert top[0] <= nc.sbuf_usable_end, (name, top[0])
            return at(name, shape, o, dt), o

        UNIT = KT * P
        raw = [new(f"raw{s}", [P, UNIT])[0] for s in range(4)]
        whi = [new(f"whi{s}", [P, UNIT], F32R)[0] for s in range(4)]
        wlo = [new(f"wlo{s}", [P, UNIT], F32R)[0] for s in range(4)]
        h, _ = new("h", [P, KT, T])
        f, F_AT = new("f", [P, KT, T])
        xhi, X_AT = new("xhi", [P, KT, T], F32R)
        xlo, _ = new("xlo", [P, KT, T], F32R)
        ghi, A_AT = new("ghi", [P, 16, T], F32R)
        glo, _ = new("glo", [P, 16, T], F32R)
        sgt, SG_AT = new("sgt", [P, 4, T])
        sq, SQ_AT = new("sq", [P, 2, T])
        cst, _ = new("cst", [P, NCONST])
        gcol, _ = new("gcol", [P, P])
        vcol, _ = new("vcol", [P, 96])
        shcol, _ = new("shcol", [P, P])
        lrucol, _ = new("lrucol", [P, P])
        small, _ = new("small", [P, 192])
        rs5, rs5b, eps_col, gn_eps_col = small[:, 0:5], small[:, 8:13], small[:, 14:15], small[:, 15:16]
        st_in, st_sd, st_rs = small[:, 16:56], small[:, 56:96], small[:, 96:136]
        omka, lru_sp, lru_nsp, lt = small[:, 136:140], small[:, 140:144], small[:, 144:148], small[:, 148:168]
        neglam, mx2, nb2, l2, rl2 = small[:, 168:169], small[:, 170:172], small[:, 172:174], small[:, 174:176], small[:, 176:178]
        lamt, mxn, pn2, wn2 = small[:, 178:182], small[:, 182:184], small[:, 184:186], small[:, 186:188]
        EXTRA = top[0]
        assert EXTRA + 6144 <= nc.sbuf_usable_end, EXTRA
        AR = GT * T * 4
        u = at("u", [P, 32, T], A_AT)
        A = [u[:, 4 * n:4 * n + 4, :] for n in range(8)]
        FA = [at(f"FA{n}", [P, GT, T], F_AT + n * AR) for n in range(2)]
        X = [at(f"X{n}", [P, GT, T], X_AT + n * AR) for n in range(4)]
        stage = at("stage", [P, 4, D], A_AT)
        stage_s = at("stage_s", [NS, D], A_AT + 4 * D * 4)
        phi = at("phi", [P, 2, T], A_AT, F32R)
        plo = at("plo", [P, 2, T], A_AT + 2 * T * 4, F32R)
        pst = at("pst", [P, 4, 256], EXTRA)
        pss = at("pss", [NS, 256], EXTRA + 4096)

        rope = at("rope", [P, 2, T], SG_AT)
        decay = at("decay", [P, 2, GT, T], F_AT)
        shst = at("shst", [9, 16, P], X_AT + 3 * AR)
        ktok = at("ktok", [P, GT, P], X_AT)
        vtok = at("vtok", [P, GT, P], X_AT + 2048)
        ubd = at("ubd", [P, GT, P], X_AT + 4096)
        uout = at("uout", [P, GT, HD], X_AT + 6144)
        vs8 = at("vs8", [NS, GW], SQ_AT)
        att = at("att", [P, 2, GT, P], X_AT + AR)
        kvt = at("kvt", [P, NS, HD], SQ_AT + 2048)
        s_ret = at("s_ret", [P, GT, NS, HD], X_AT + 2 * AR)

        lw1 = at("lw1", [P, GT, HD], A_AT + 3 * AR)
        la1 = at("la1", [P, GT, HD], A_AT + 3 * AR + 1024)
        lg1 = at("lg1", [P, GT, P], A_AT + 3 * AR + 2048)
        lw2 = at("lw2", [HD, GW], A_AT + 3 * AR + 4096)
        la2 = at("la2", [HD, GW], A_AT + 3 * AR + 6144)
        lg2 = at("lg2", [P, GW], EXTRA)
        tw = at("tw", [HD, T], SQ_AT)
        ta = at("ta", [HD, T], SQ_AT + T * 4)
        tg = at("tg", [P, T], SG_AT)
        reset = at("reset", [P, SEQ], SG_AT + T * 4)
        rows8 = [at(f"rows8_{n}", [NS, GW], A_AT + 6 * AR + 2048 * n) for n in range(4)] + [at("rows8_4", [NS, GW], SQ_AT)]
        s_rw = at("s_rw", [P, GT, NS, HD], A_AT + AR)
        swt = [at(f"swt{n}", [P, NS, HD], EXTRA + 2048 * (n + 1)) for n in range(2)]
        sa8 = at("sa8", [P, NS], EXTRA)

        def slots(names, o):
            return {x: at(f"c_{x}", [P, GT, P], o + 2048 * n) for n, x in enumerate(names)}

        c = {**slots(["al", "be", "ka", "rh"], A_AT + 4 * AR), **slots(["vb", "ob", "wt", "bt"], SG_AT),
             **slots(["akt", "rbt", "rkt", "kt"], A_AT + 6 * AR), **slots(["s1", "s2", "s3", "s4"], A_AT + AR),
             **slots(["s5", "s6"], SQ_AT), **slots(["s7"], EXTRA)}
        vc, zc, rc, uc = [at(f"c_{x}", [P, GT, HD], EXTRA + 2048 + 1024 * n) for n, x in enumerate(["vc", "zc", "rc", "uc"])]
        rwst = at("rwst", [HD, GT, P], SG_AT + 4096)

        wabd = at("wabd", [P, GT, P], A_AT + 5 * AR)
        wibd = at("wibd", [P, GT, P], A_AT + 5 * AR + 2048)
        lcst = at("lcst", [11, GW], A_AT + 7 * AR)
        lhst = at("lhst", [9, GW], A_AT + 7 * AR + 2048)
        vtm = at("vtm", [P, GT, GW], A_AT + 5 * AR)
        ktm = at("ktm", [P, GT, GW], A_AT + 6 * AR)
        ks8 = at("ks8", [NS, GW], EXTRA)
        vs8o = at("vs8o", [NS, GW], EXTRA + 2048)
        qs8 = at("qs8", [NS, GW], EXTRA + 4096)
        dlam = at("dlam", [P, 4, HD], SG_AT)
        pages = at("pages", [1, NS * PAGES], SG_AT + 1024, I32)
        probs = at("probs", [P, 2, 2, SEQ], X_AT)
        wtp = at("wtp", [P, 2, SEQ], X_AT + AR)
        sdec = at("sdec", [P, 2, PAGES, NS, 4], X_AT + AR + 4096)
        kd = [at(f"kd{n}", [P, PAGES, GW], X_AT + (2 + n) * AR) for n in range(2)]
        vd = [at(f"vd{n}", [P, PAGES, GW], F_AT + n * AR) for n in range(2)]
        kprod = at("kprod", [P, PAGES, GW], A_AT + 7 * AR)
        pdec = at("pdec", [32, 2, SEQ], SG_AT + 2048)
        wtd = at("wtd", [P, PAGES, 32], SG_AT + 2048 + 4096)
        prodn = at("prodn", [P, NS, 4], SG_AT + 2048 + 4096 + 512)
        wdiag = at("wdiag", [32, 32], SG_AT + 2048 + 4096 + 512 + 128)
        assert SG_AT + 2048 + 4096 + 512 + 256 <= SG_AT + 4 * T * 4

        row_g = at("row_g", [P, P], A_AT + 5 * AR)
        row_v = at("row_v", [NVEC, P], A_AT + 5 * AR + 512)
        row_s = at("row_s", [P, P], A_AT + 5 * AR + 1024)
        row_l = at("row_l", [P, P], A_AT + 5 * AR + 1536)
        row_tables = [(gcol, row_g), (vcol, row_v), (shcol, row_s), (lrucol, row_l)]

        psum = ctx.enter_context(nc.psum_tensor("psum", [P, 8, 512], F32))
        flat = psum[:, :, :].rearrange("p b n -> p (b n)")

        def bank(b, n=512):
            return psum[:, b, 0:n]

        def halves(b):
            return psum[:, b:b + 2, 0:TH]

        def tok(x):
            return x.rearrange("p (h t) -> p h t", h=2)

        def C(name):
            s, w = CONST[name]
            return cst[:, s:s + w]

        def V(name, j=0):
            s, _ = VEC[name]
            return vcol[:, s + j:s + j + 1]

        ident = C("ident")

        w_in, w_out = I["ffn_w_in"], I["ffn_w_out"]
        PHASES = []

        def ffn_phases(i, a):
            for r in range(2):
                PHASES.append((("in", i, a, r), 32, 16))
                PHASES.append((("out", i, a, r), 16, 8))

        for i in range(2):
            ffn_phases(i, 0)
            PHASES.append((("mix_in", i), 32 if i == 0 else 20, 32 if i == 0 else 20))
            PHASES.append((("mix_out", i), 8, 8))
            ffn_phases(i, 1)
            PHASES.append((("gate", i), 8, 8))
            PHASES.append((("ple", i), 4, 8))
        UB, TB = {}, {}
        ub = tb = 0
        for name, nu, nt in PHASES:
            UB[name], TB[name] = ub, tb
            ub, tb = ub + nu, tb + nt
        NU = ub

        raw_loaded = [sem(f"raw_loaded{s}") for s in range(4)]
        hi_ready, lo_ready, unit_used = sem("hi_ready"), sem("lo_ready"), sem("unit_used")
        psum_free = [sem(f"psum_free{s}") for s in range(2)]
        sg_ready, hid_ready, hhi_ready = sem("sg_ready"), sem("hid_ready"), sem("hhi_ready")
        sq_ready, sq_used = sem("sq_ready"), sem("sq_used")
        sd_ready, rs_ready, rb_ready = sem("sd_ready"), sem("rs_ready"), sem("rb_ready")
        h_ready, xt_ready, xh_ready, xn_ready = sem("h_ready"), sem("xt_ready"), sem("xh_ready"), sem("xn_ready")

        def free_count(t):
            return t // 2

        NORM = {}
        for i in range(2):
            for k in range(8):
                NORM[(i, k)] = 8 * i + k

        PAIRS = {}
        n = 0
        for name, _, nt in PHASES:
            if name[0] == "in":
                PAIRS[name] = n
                n += nt

        block = ctx.enter_context(nc.Block())

        cen_ready, cen_copied = sem("centred"), sem("centred_copied")
        stat_summed, stat_rooted, stat_ready = sem("stat_summed"), sem("stat_rooted"), sem("stat_ready")
        stat_spread, stat_used = sem("stat_spread"), sem("stat_used")
        cath_ready, cat_ready = sem("cat_hi_ready"), sem("cat_ready")

        def raw_cols(u):
            small_u = isinstance(u, int) and any(UB[("ple", i)] <= u < UB[("ple", i)] + 4 for i in range(2))
            return 512 if small_u else UNIT

        def one(x, m):
            return x[:, m, :] if isinstance(m, int) else x[:, bass.ds(m, 1), :].rearrange("p a t -> p (a t)")

        def one2(x, m):
            return x[:, bass.ds(m, 1), :].rearrange("p a (h t) -> p (a h) t", h=2)

        def row128(a):
            return a.rearrange("(k p) -> k p", p=P)

        def vrow(name):
            s, w = VEC[name]
            return row_v[s:s + w, :]

        ROWS = [
            (row_g[:, :], I["norm_g"].rearrange("i n (k p) -> (i n k) p", p=P)),
            (vrow("mu"), I["rwkv_mu"][0].rearrange("m (k p) -> (m k) p", p=P)),
            (vrow("w0"), row128(I["rwkv_w0"][0])), (vrow("a0"), row128(I["rwkv_a0"][0])),
            (vrow("kk"), row128(I["rwkv_kk"][0])), (vrow("ka"), row128(I["rwkv_ka"][0])),
            (vrow("rk"), I["rwkv_rk"][0].rearrange("(k h) d -> k (h d)", h=2)),
            (vrow("ln"), I["rwkv_ln"][0].rearrange("m (k p) -> (m k) p", p=P)),
            (vrow("conv_w"), I["lru_conv_w"][0].rearrange("m (k p) -> (m k) p", p=P)),
            (vrow("conv_b"), row128(I["lru_conv_b"][0])), (vrow("ba"), row128(I["lru_ba"][0])),
            (vrow("bi"), row128(I["lru_bi"][0])), (vrow("lam"), row128(I["lru_lambda"][0])),
            (vrow("subln"), I["diff_subln"]),
            (row_s[:, :], I["state_rwkv_shift"][0, :, 0, :].rearrange("b (k p) -> (b k) p", p=P)),
            (row_l[0:96, :], I["state_lru_conv"][0].rearrange("b t (k p) -> (b t k) p", p=P)),
            (row_l[96:128, :], I["state_lru_h"][0].rearrange("b (k p) -> (b k) p", p=P)),
        ]
        NROWS = len(ROWS)

        lin = I["ab_w_in"][0], I["cd_w_in"][0]
        lout = I["ab_w_out"][0], I["cd_w_out"][0]
        DC = math.exp(-0.5)

        PE_STEPS = ["mats", "rhs", "a2", "a4", "a8", "x8", "f", "f2", "hh", "w", "z", "out", "turn"]
        ACT_STEPS = ["bt", "kt", "vc", "rc", "a2t", "a4", "a4t", "a8", "f", "ft", "dinv", "hh", "w", "o0", "o1", "turn"]
        DVE_STEPS = ["stage", "a", "at", "e", "x1", "akt", "a2", "rbt", "rkt", "x2", "x4", "x8", "imf", "if2", "zc", "u0", "u1"]
        ch_pe, ch_act, ch_dve = sem("chunk_pe_steps"), sem("chunk_act_steps"), sem("chunk_dve_steps")

        def in_chunk(eng, it, who, step):
            s, names = {"pe": (ch_pe, PE_STEPS), "act": (ch_act, ACT_STEPS), "dve": (ch_dve, DVE_STEPS)}[who]
            eng.wait_ge(s, it * len(names) + (0 if step is None else names.index(step) + 1))

        @block.sync
        def _(sp):
            def load(u, r, src, width=P, nk=KT):
                if not isinstance(u, int) or u >= 4:
                    sp.wait_ge(lo_ready, u - 3)
                s = r % 4
                dst = raw[s][:, 0:nk * width].rearrange("p (k c) -> p k c", k=nk)
                sp.dma_start(dst, src.rearrange("(k p) c -> p k c", p=P)).then_inc(raw_loaded[s], 16)

            def ffn(i, a):
                win, wout = w_in[i, a, :, :], w_out[i, a, :, :]
                for r in range(2):
                    u0 = UB[("in", i, a, r)]
                    first = 1 if u0 == 0 else 0
                    c0 = r * 16 * P
                    for p in range(2 * first):
                        load(2 * p, 2 * p, win[:, c0 + p * P:c0 + (p + 1) * P])
                        load(2 * p + 1, 2 * p + 1, win[:, 4096 + c0 + p * P:4096 + c0 + (p + 1) * P])
                    with sp.Fori(first, 8) as it:
                        for p in range(2):
                            col = it * (2 * P) + (c0 + p * P)
                            load(it * 4 + (u0 + 2 * p), 2 * p, win[:, bass.ds(col, P)])
                            load(it * 4 + (u0 + 2 * p + 1), 2 * p + 1, win[:, bass.ds(col + 4096, P)])
                    u0 = UB[("out", i, a, r)]
                    with sp.Fori(0, 4) as it:
                        for m in range(2):
                            for g in range(2):
                                row = (r * 2 + g) * D
                                load(it * 4 + (u0 + 2 * m + g), 2 * m + g,
                                     wout[row:row + D, bass.ds(it * (2 * P) + m * P, P)])

            def proj(name, w):
                u0, nt = UB[name], w.shape[1] // P
                with sp.Fori(0, nt // 4) as it:
                    for m in range(4):
                        load(it * 4 + (u0 + m), m, w[:, bass.ds(it * (4 * P) + m * P, P)])

            for i in range(2):
                ffn(i, 0)
                proj(("mix_in", i), lin[i])
                proj(("mix_out", i), lout[i])
                ffn(i, 1)
                proj(("gate", i), I["ple_gate_w"][i])
                for e in range(4):
                    load(UB[("ple", i)] + e, e, I["ple_w"][i][:, e * 256:(e + 1) * 256], 256, 2)

        NT = {name: nt for name, _, nt in PHASES}

        @block.tensor
        def _(pe):
            mm = nc.tensor.matmul

            def turn(out, in_):
                return nc.tensor.transpose(out, in_, ident[0:in_.shape[0], 0:in_.shape[0]])

            def unit(u, r, out, xh, xl, nk=KT, start=True, stop=True, width=P, c0=0, k0=0, last=True, paced=None):
                pe.wait_ge(lo_ready, u + 1)
                s = r % 4
                hi = whi[s][:, 0:nk * width].rearrange("p (k c) -> p k c", k=nk)
                lo = wlo[s][:, 0:nk * width].rearrange("p (k c) -> p k c", k=nk)
                for k in range(nk):
                    if paced is not None:
                        pe.wait_ge(xn_ready, paced + k + 1)
                    for e in range(2):
                        for n, (w, x) in enumerate(((hi, xh), (hi, xl), (lo, xh))):
                            ins = mm(out[:, e, :], w[:, k, c0:c0 + P], x[:, k0 + k, e * TH:(e + 1) * TH],
                                     start=start and k == 0 and n == 0, stop=stop and k == nk - 1 and n == 2)
                if last:
                    ins.then_inc(unit_used, 1)

            def free(s, count):
                if not isinstance(count, int) or count > 0:
                    pe.wait_ge(psum_free[s], count)

            def ffn(i, a):
                nx = 8 * (NORM[(i, 0 if a == 0 else 4)] // 2)
                for r in range(2):
                    name = ("in", i, a, r)
                    u0, t0 = UB[name], TB[name] // 2

                    def body(it, lead):
                        for p in range(2):
                            free(p, it + t0)
                            for g in range(2):
                                if lead and p == 0 and g == 1:
                                    pe.wait_ge(xn_ready, nx + 8)
                                unit(it * 4 + (u0 + 2 * p + g), 2 * p + g, halves(4 * p + 2 * g), xhi, xlo,
                                     paced=nx if lead and p == 0 and g == 0 else None)

                    if r == 0:
                        body(0, True)
                    with pe.Fori(1 - r, 8) as it:
                        body(it, False)
                    name = ("out", i, a, r)
                    uo, to = UB[name], TB[name] // 2

                    def obody(it, lead):
                        for m in range(2):
                            if lead and m == 0:
                                pe.wait_ge(psum_free[1], to - 4)
                                pe.wait_ge(psum_free[0], to)
                            else:
                                free(m, it + to)
                            unit(it * 4 + (uo + 2 * m), 2 * m, halves(4 * m), ghi, glo, stop=False)
                            if lead and m == 0:
                                pe.wait_ge(psum_free[1], to)
                            unit(it * 4 + (uo + 2 * m + 1), 2 * m + 1, halves(4 * m), ghi, glo, start=False, k0=KT)

                    obody(0, True)
                    with pe.Fori(1, 4) as it:
                        obody(it, False)

            def proj(name, nx, cat=None):
                u0, t0 = UB[name], TB[name] // 2
                if cat is None:
                    pe.wait_ge(xn_ready, nx)
                else:
                    pe.wait_ge(cat_ready, cat)
                with pe.Fori(0, NT[name] // 4) as it:
                    for m in range(4):
                        free(m % 2, it * 2 + (t0 + m // 2))
                        unit(it * 4 + (u0 + m), m, halves(4 * (m % 2)), xhi, xlo)

            def spread(b, r5, signal):
                heads = r5.shape[2]
                for x in range(5):
                    w = P if x < 4 else NS
                    for g in range(heads):
                        n = P // heads
                        last = mm(flat[g * n:(g + 1) * n, b * 512 + x * P:b * 512 + x * P + w], r5[:, x, g:g + 1].to_broadcast([P, n]),
                                  ident[:, P - w:P], start=True, stop=True)
                last.then_inc(signal, 1)

            def norm(n):
                for k in range(KT):
                    pe.wait_ge(sq_ready, 8 * n + k + 1)
                    for x, t0 in enumerate(TOK_TILES):
                        last = mm(psum[:, 7, x:x + 1], sq[:, k % 2, t0:t0 + P], C("ones2")[:, 0:1],
                                  start=(k == 0 and x == 0), stop=(k == KT - 1), skip_group_check=True)
                    last.then_inc(sq_used, 1)
                pe.wait_ge(rs_ready, n + 1)
                spread(2, rs5b.rearrange("p (x o) -> p x o", o=1), rb_ready)

            def centre(g, src):
                for j in range(GT):
                    if 4 * g + j >= 2:
                        pe.wait_ge(cen_copied, 2 * (4 * g + j - 1))
                    for e in range(2):
                        last = mm(halves(4 * (j % 2))[:, e, :], C("center"), src[:, j, e * TH:(e + 1) * TH], start=True, stop=True)
                    last.then_inc(cen_ready, 1)

            def even_mix():
                q, k, v = A[0], A[1], A[2]
                for s in range(2):
                    pe.wait_ge(psum_free[s], TB[("mix_in", 0)] // 2 + 16)
                for n in range(16):
                    last = turn(psum[0:9, n // 4, (n % 4) * P:(n % 4 + 1) * P], u[:, 16 + n, SEQ - 1:T])
                last.then_inc(sem("shift_turned"), 1)
                pe.wait_ge(sem("shift_copied"), 4)
                for n in range(8):
                    if n >= 2:
                        pe.wait_ge(sem("rot_used"), n - 1)
                    for e in range(2):
                        last = mm(halves(4 * (n % 2))[:, e, :], C("rot"), A[n // 4][:, n % 4, e * TH:(e + 1) * TH], start=True, stop=True)
                    last.then_inc(sem("rot_ready"), 1)
                pe.wait_ge(sem("qk_ready"), 8)
                for i in range(4):
                    ts = slice(i * P, (i + 1) * P)
                    if i:
                        pe.wait_ge(sem("tk_copied"), 2 * i)
                    for j in range(GT):
                        turn(bank(0)[:, j * P:(j + 1) * P], k[:, j, ts])
                        last = turn(bank(1)[:, j * P:(j + 1) * P], v[:, j, ts])
                    last.then_inc(sem("tk_turned"), 1)
                    if i:
                        pe.wait_ge(sem("att_ready"), 2 * i)
                    for hh in range(2):
                        hp = slice(hh * HD, (hh + 1) * HD)
                        for j in range(GT):
                            last = mm(bank(2 + hh)[:, j * P:(j + 1) * P], k[hp, j, ts], q[hp, j, ts], start=True, stop=True)
                    last.then_inc(sem("sc_ready"), 1)
                    pe.wait_ge(sem("tk_copied"), 2 * (i + 1))
                    pe.wait_ge(sem("att_ready"), 2 * (i + 1))
                    pe.wait_ge(sem("ubd_ready"), i + 1)
                    if i:
                        pe.wait_ge(sem("o_copied"), i)
                    for j in range(GT):
                        js = slice(j * P, (j + 1) * P)
                        mm(bank(4)[:, js], ubd[:, j, :], q[:, j, ts], start=True, stop=False, skip_group_check=True)
                        for hh in range(2):
                            hp = slice(hh * HD, (hh + 1) * HD)
                            mm(bank(4)[hp, js], vtok[:, j, hp], att[:, hh, j, :], start=False, stop=True, skip_group_check=True)
                    for j in range(GT):
                        last = mm(bank(5)[:, j * P:(j + 1) * P], ktok[:, j, :], vtok[:, j, :], start=True, stop=True)
                    last.then_inc(sem("pv_done"), 1)
                for j in range(GT):
                    last = turn(psum[0:NS, 6, j * P:(j + 1) * P], v[:, j, SEQ:T])
                last.then_inc(sem("vs_turned"), 1)
                pe.wait_ge(sem("vs8_ready"), 1)
                for j in range(GT):
                    if j >= 2:
                        pe.wait_ge(sem("vb_used"), j - 1)
                    for hh in range(2):
                        for b in range(NS):
                            last = mm(psum[hh * HD:(hh + 1) * HD, j % 2, b * HD:(b + 1) * HD], ident[0:NS, b:b + 1].to_broadcast([NS, HD]),
                                      vs8[:, (2 * j + hh) * HD:(2 * j + hh + 1) * HD], start=True, stop=True)
                    last.then_inc(sem("vb_ready"), 1)
                for j in range(GT):
                    pe.wait_ge(sem("sret_ready"), j + 1)
                    for hh in range(2):
                        hp = slice(hh * HD, (hh + 1) * HD)
                        for b in range(NS):
                            last = mm(psum[hp, 2 + hh, j * NS + b:j * NS + b + 1], s_ret[hp, j, b, :], q[hp, j, SEQ + b:SEQ + b + 1], start=True, stop=True)
                last.then_inc(sem("os_ready"), 1)
                pe.wait_ge(sem("o_copied"), 6)
                centre(0, A[0])
                head_stat0(0)
                pe.wait_ge(sem("lora_loaded"), 96)
                pe.wait_ge(sem("z_ready"), 12)
                pe.wait_ge(stat_used, 4)
                for n, (w, x, b, m) in enumerate(((lw1, FA[1], 0, HD), (la1, X[3], 2, HD), (lg1, A[1], 4, P))):
                    for e in range(2):
                        for j in range(GT):
                            last = mm(halves(b)[0:m, e, :], w[:, j, :], x[:, j, e * TH:(e + 1) * TH], start=(j == 0), stop=(j == GT - 1))
                    last.then_inc(sem("l1_ready"), 1)
                for n in range(12):
                    w, x = ((lw2, tw), (la2, ta), (lg2, tg))[n // 4]
                    if n % 4 == 0:
                        pe.wait_ge(sem("l1_copied"), 3)
                    if n >= 2:
                        pe.wait_ge(sem("l2_copied"), n - 1)
                    j = n % 4
                    for e in range(2):
                        last = mm(halves(4 * (n % 2))[:, e, :], w[:, j * P:(j + 1) * P], x[:, e * TH:(e + 1) * TH], start=True, stop=True)
                    last.then_inc(sem("l2_ready"), 1)
                pe.wait_ge(sem("l2_copied"), 12)
                pe.wait_ge(sem("kk_sq"), 4)
                stat_body(1, X[3], C("bsel"))
                pe.wait_ge(sem("rw_ready"), 1)
                for n, x in enumerate((FA[0], A[5], FA[1], X[1], X[0])):
                    for j in range(GT):
                        last = turn(psum[0:NS, n, j * P:(j + 1) * P], x[:, j, SEQ:T])
                last.then_inc(sem("rw_turned"), 1)
                pe.wait_ge(sem("rows8_ready"), 5)
                for n in range(20):
                    j, x = n // 5, n % 5
                    if n >= 6:
                        pe.wait_ge(sem("bc_used"), n - 5)
                    for hh in range(2):
                        for b in range(NS):
                            last = mm(psum[hh * HD:(hh + 1) * HD, n % 6, b * HD:(b + 1) * HD], ident[0:NS, b:b + 1].to_broadcast([NS, HD]),
                                      rows8[x][:, (2 * j + hh) * HD:(2 * j + hh + 1) * HD], start=True, stop=True)
                    last.then_inc(sem("bc_ready"), 1)
                pe.wait_ge(sem("bc_used"), 20)
                stack = C("stack")

                def pairs(b, lhs, rhs, n=P, more=None):
                    terms = [(lhs, rhs)] + (more or [])
                    for j in range(GT):
                        for x, (l, r) in enumerate(terms):
                            last = mm(bank(b)[:, j * n:(j + 1) * n], l[:, j, :], r if len(r.shape) == 2 else r[:, j, :],
                                      start=(x == 0), stop=(x == len(terms) - 1))
                    return last

                with pe.Fori(0, NCH) as it:
                    W = lambda who, step: in_chunk(pe, it, who, step)
                    W("act", None)
                    W("dve", "stage")
                    pairs(0, c["al"], c["be"])
                    pairs(1, c["be"], c["al"])
                    pairs(7, c["vb"], stack, HD)
                    pairs(2, c["ka"], c["al"])
                    pairs(3, c["be"], c["rh"])
                    pairs(4, c["ka"], c["rh"])
                    pairs(5, c["be"], ident)
                    pairs(6, c["ka"], ident).then_inc(ch_pe, 1)
                    W("dve", "akt")
                    W("act", "vc")
                    pairs(7, c["al"], uc, HD, [(c["akt"], vc)]).then_inc(ch_pe, 1)
                    pairs(0, c["s2"], c["s1"])
                    pairs(1, c["s1"], c["s2"]).then_inc(ch_pe, 1)
                    W("dve", "a2")
                    W("act", "a2t")
                    pairs(0, c["s4"], c["s3"])
                    pairs(1, c["s3"], c["s4"])
                    pairs(2, c["s3"], c["s6"]).then_inc(ch_pe, 1)
                    W("act", "a4t")
                    W("dve", "x2")
                    pairs(0, c["s2"], c["s1"])
                    pairs(2, c["s1"], c["s7"]).then_inc(ch_pe, 1)
                    W("act", "a8")
                    W("dve", "x4")
                    pairs(2, c["s3"], c["s6"]).then_inc(ch_pe, 1)
                    W("dve", "x8")
                    pairs(0, c["s7"], c["s5"])
                    pairs(1, c["s5"], c["s7"])
                    pairs(2, c["s7"], ident).then_inc(ch_pe, 1)
                    W("act", "ft")
                    pairs(0, c["s2"], c["s1"]).then_inc(ch_pe, 1)
                    W("dve", "if2")
                    pairs(1, c["s3"], c["s6"]).then_inc(ch_pe, 1)
                    W("act", "hh")
                    pairs(2, c["s4"], c["s5"]).then_inc(ch_pe, 1)
                    W("act", "w")
                    W("dve", "rkt")
                    pairs(3, c["wt"], rc, HD).then_inc(ch_pe, 1)
                    W("dve", "zc")
                    pairs(4, c["rh"], uc, HD, [(c["rbt"], zc), (c["rkt"], vc)])
                    pairs(5, c["bt"], zc, HD, [(c["kt"], vc)]).then_inc(ch_pe, 1)
                    W("act", "o1")
                    pairs(6, c["ob"], stack, HD).then_inc(ch_pe, 1)
                pe.wait_ge(ch_dve, NCH * len(DVE_STEPS))
                pe.wait_ge(ch_act, NCH * len(ACT_STEPS))
                for j in range(GT):
                    last = turn(psum[0:HD, 6, j * P:(j + 1) * P], uc[:, j, :])
                last.then_inc(sem("state_turned"), 1)
                centre(1, X[3])
                head_stat0(2)
                pe.wait_ge(sem("rkk_ready"), 1)
                for j in range(GT):
                    pe.wait_ge(stat_used, 12)
                    if j >= 2:
                        pe.wait_ge(sem("bonus_used"), j - 1)
                    for e in range(2):
                        last = mm(halves(4 * (j % 2))[:, e, :], C("bones"), X[0][:, j, e * TH:(e + 1) * TH], start=True, stop=True)
                    last.then_inc(sem("bonus_ready"), 1)

            def head_stat0(g):
                pe.wait_ge(cen_copied, 8 * (g // 2 + 1))
                stat_body(g, X[1] if g == 0 else FA[1], C("hsel"))

            def stat_body(g, src, sel):
                w = sel.shape[1]
                for j in range(GT):
                    for x, t0 in enumerate(TOK_TILES):
                        last = mm(psum[:, 7, (x * GT + j) * w:(x * GT + j + 1) * w], src[:, j, t0:t0 + P], sel,
                                  start=(j == 0 and x == 0), stop=(j == GT - 1), skip_group_check=True)
                last.then_inc(stat_summed, 1)
                pe.wait_ge(stat_ready, g + 1)
                r = st_rs[:, 0:20 * w].rearrange("p (x j s) -> p x j s", j=GT, s=w)
                for j in range(GT):
                    if 4 * g + j >= 2:
                        pe.wait_ge(stat_used, 4 * g + j - 1)
                    spread(4 * (j % 2), r[:, :, j, :], stat_spread)

            def odd_mix():
                q, k, v = A[0], A[1], A[2]
                for s in range(2):
                    pe.wait_ge(psum_free[s], TB[("mix_in", 1)] // 2 + 10)
                for j in range(GT):
                    last = turn(psum[0:11, 6, j * P:(j + 1) * P], A[3][:, j, SEQ - 3:T])
                last.then_inc(sem("lconv_turned"), 1)
                pe.wait_ge(sem("lruw_loaded"), 16 * 16)
                pe.wait_ge(sem("xc_ready"), 1)
                for n in range(8):
                    if n >= 2:
                        pe.wait_ge(sem("gates_copied"), n - 1)
                    for e in range(2):
                        last = mm(halves(4 * (n % 2))[:, e, :], (wabd, wibd)[n // 4][:, n % 4, :], X[0][:, n % 4, e * TH:(e + 1) * TH], start=True, stop=True)
                    last.then_inc(sem("gates_ready"), 1)
                pe.wait_ge(sem("gates_copied"), 8)
                for x in range(5):
                    w = P if x < 4 else NS
                    if x >= 2:
                        pe.wait_ge(sem("kv_copied"), 2 * (x - 1))
                    for n, a in enumerate((v, k)):
                        for j in range(GT):
                            last = turn(psum[0:w, 2 * (x % 2) + n, j * P:(j + 1) * P], a[:, j, x * P:x * P + w])
                    last.then_inc(sem("kv_turned"), 1)
                for j in range(GT):
                    last = turn(psum[0:NS, 4, j * P:(j + 1) * P], q[:, j, SEQ:T])
                last.then_inc(sem("qs_turned"), 1)
                pe.wait_ge(sem("lruh_ready"), 1)
                for j in range(GT):
                    last = turn(psum[0:9, 5, j * P:(j + 1) * P], FA[0][:, j, SEQ - 1:T])
                last.then_inc(sem("lruh_turned"), 1)
                pe.wait_ge(sem("qs_copied"), 1)
                pe.wait_ge(sem("lruh_copied"), 1)
                pe.wait_ge(sem("kv_copied"), 10)

                def scores(n):
                    i, j = n // 4, n % 4
                    if n >= 2:
                        pe.wait_ge(sem("exp_done"), 2 * (n - 1))
                    for m in range(2):
                        hp = slice(m * HD, (m + 1) * HD)
                        last = mm(psum[:, 2 * (n % 2) + m, 0:(i + 1) * P], q[hp, j, i * P:(i + 1) * P], k[hp, j, 0:(i + 1) * P], start=True, stop=True)
                    last.then_inc(sem("qk2_ready"), 1)

                scores(0)
                for n in range(16):
                    i, j = n // 4, n % 4
                    if n < 15:
                        scores(n + 1)
                    pe.wait_ge(sem("w_ready"), n + 1)
                    if n >= 2:
                        pe.wait_ge(sem("wt_copied"), n - 1)
                    for x in range(i + 1):
                        last = turn(psum[:, 4 + n % 2, x * P:(x + 1) * P], probs[:, n % 2, 0, x * P:(x + 1) * P])
                    last.then_inc(sem("wt_turned"), 1)
                    pe.wait_ge(sem("wt_copied"), n + 1)
                    if n >= 2:
                        pe.wait_ge(sem("oc_copied"), n - 1)
                    for x in range(i + 1):
                        last = mm(psum[:, 6 + n % 2, 0:P], vtm[:, x, j * P:(j + 1) * P], wtp[:, n % 2, x * P:(x + 1) * P], start=(x == 0), stop=(x == i))
                    last.then_inc(sem("pv2_done"), 1)
                pe.wait_ge(sem("oc_copied"), 16)
                for b in range(NS):
                    if b >= 2:
                        pe.wait_ge(sem("qb_used"), b - 1)
                    mm(bank(b % 2), ident[0:NS, b:b + 1].to_broadcast([NS, P]), qs8[:, :], start=True, stop=True).then_inc(sem("qb_ready"), 1)
                pe.wait_ge(sem("sdec_ready"), NS + 1)
                for m in range(2):
                    for x in range(PAGES):
                        turn(psum[0:32, 2 + m, x * P:(x + 1) * P], sdec[:, m, x, :, :].rearrange("p b h -> p (b h)"))
                mm(psum[0:32, 4, 0:2], prodn[:, :, :].rearrange("p b h -> p (b h)"), C("bsel"), start=True, stop=True).then_inc(sem("sd_turned"), 1)
                pe.wait_ge(sem("wd_ready"), 1)
                for x in range(PAGES):
                    turn(psum[:, 5, x * 32:(x + 1) * 32], pdec[:, 0, x * P:(x + 1) * P])
                mm(psum[:, 6, 0:32], C("ones2")[0:32, 0:1].to_broadcast([32, P]), wdiag[:, :], start=True, stop=True).then_inc(sem("wd_turned"), 1)
                pe.wait_ge(sem("wtd_copied"), 1)
                for b in range(NS):
                    pe.wait_ge(sem(f"vd_loaded{b % 2}"), 64 * (b // 2 + 1))
                    for j in range(4):
                        for x in range(PAGES):
                            last = mm(psum[:, 7, b * 4 + j:b * 4 + j + 1], vd[b % 2][:, x, j * P:(j + 1) * P], wtd[:, x, b * 4 + j:b * 4 + j + 1],
                                      start=(x == 0), stop=(x == PAGES - 1))
                    last.then_inc(sem("vd_used"), 1)
                pe.wait_ge(sem("oc_sq"), 1)
                stat_body(3, X[1], C("ones2")[:, 0:1])

            pe.wait_ge(sem("inputs_loaded"), 16 * (NROWS + 3))
            for n, (dst, rows) in enumerate(row_tables):
                last = turn(psum[:, 6, n * P:n * P + rows.shape[0]], rows[:, :])
            last.then_inc(sem("rows_turned"), 1)
            for k in range(KT):
                b = 4 * (k % 2)
                if k >= 2:
                    pe.wait_ge(h_ready, k - 1)
                for x in range(4):
                    turn(psum[:, b, x * P:(x + 1) * P], stage[:, x, k * P:(k + 1) * P])
                turn(psum[:, b + 1, 0:NS], stage_s[:, k * P:(k + 1) * P]).then_inc(sem("xt_turned"), 1)
            for i in range(2):
                norm(NORM[(i, 0)])
                ffn(i, 0)
                norm(NORM[(i, 1)])
                norm(NORM[(i, 2)])
                proj(("mix_in", i), 8 * (NORM[(i, 2)] // 2 + 1))
                (even_mix if i == 0 else odd_mix)()
                proj(("mix_out", i), None, 8 * (i + 1))
                norm(NORM[(i, 3)])
                norm(NORM[(i, 4)])
                ffn(i, 1)
                norm(NORM[(i, 5)])
                norm(NORM[(i, 6)])
                proj(("gate", i), 8 * (NORM[(i, 6)] // 2 + 1))
                pe.wait_ge(psum_free[1], TB[("ple", i)] // 2)
                pe.wait_ge(psum_free[0], TB[("ple", i)] // 2)
                pe.wait_ge(sem("p_loaded"), 32 * (i + 1))
                for k in range(2):
                    for x in range(4):
                        turn(psum[:, 2 + 4 * k, x * P:(x + 1) * P], pst[:, x, k * P:(k + 1) * P])
                    last = turn(psum[:, 3 + 4 * k, 0:NS], pss[:, k * P:(k + 1) * P])
                last.then_inc(sem("p_turned"), 1)
                pe.wait_ge(sem("plo_ready"), 2 * (i + 1))
                for e in range(4):
                    for m in range(2):
                        free(m, TB[("ple", i)] // 2 + e)
                        unit(UB[("ple", i)] + e, e, halves(4 * m), phi, plo, nk=2, width=256, c0=m * P, last=(m == 1))
                norm(NORM[(i, 7)])
            pe.wait_ge(h_ready, 8 * 9)
            for x in range(5):
                w = P if x < 4 else NS
                if x >= 2:
                    pe.wait_ge(sem("y_copied"), x - 1)
                for k in range(KT):
                    last = turn(psum[0:w, 4 * (x % 2) + k // 4, (k % 4) * P:(k % 4 + 1) * P], h[:, k, x * P:x * P + w])
                last.then_inc(sem("y_turned"), 1)

        @block.scalar
        def _(act):
            own = Steps(act, sem("act_steps"))
            fn = nc.scalar.activation

            def ahead(u, r, lead=3):
                u, r = u + lead, r + lead
                if isinstance(u, int) and u >= NU:
                    return
                s = r % 4
                act.wait_ge(raw_loaded[s], 16 * (u // 4 + 1) if isinstance(u, int) else (u - s) * 4 + 16)
                if not isinstance(u, int) or u >= 4:
                    act.wait_ge(unit_used, u - 3)
                fn(whi[s][:, 0:raw_cols(u)], raw[s][:, 0:raw_cols(u)], ACT.Copy).then_inc(hi_ready, 1)

            def ffn(i, a):
                for r in range(2):
                    name = ("in", i, a, r)
                    u0, p0 = UB[name], PAIRS[name]

                    def body(it):
                        for p in range(2):
                            for g in range(2):
                                ahead(it * 4 + (u0 + 2 * p + g), 2 * p + g)
                            pr = it * 2 + (p0 + p)
                            act.wait_ge(unit_used, it * 4 + (u0 + 2 * p + 2))
                            if not isinstance(pr, int) or pr >= 2:
                                act.wait_ge(hid_ready, pr - 1)
                            fn(tok(sgt[:, p, :]), halves(4 * p), ACT.Silu).then_inc(sg_ready, 1)
                            act.wait_ge(hid_ready, pr + 1)
                            fn(one(ghi, it * 2 + p), sgt[:, 2 + p, :], ACT.Copy).then_inc(hhi_ready, 1)

                    if u0 == 0:
                        body(0)
                    with act.Fori(1 if u0 == 0 else 0, 8) as it:
                        body(it)
                    uo = UB[("out", i, a, r)]
                    with act.Fori(0, 4) as it:
                        for m in range(4):
                            ahead(it * 4 + (uo + m), m)

            def norm(n, src, ready, pre):
                for k in range(KT):
                    ready(k)
                    if 8 * n + k >= 2:
                        act.wait_ge(sq_used, 8 * n + k - 1)
                    fn(sq[:, k % 2, :], src[:, k, :], ACT.Square).then_inc(sq_ready, 1)
                act.wait_ge(sq_used, 8 * (n + 1))
                fn(rs5, psum[:, 7, 0:5], ACT.Sqrt, scale=1.0 / D, bias=eps_col).then_inc(sd_ready, 1)
                if pre:
                    for k in range(KT):
                        act.wait_ge(xt_ready, 8 * (n // 2) + k + 1)
                        fn(xhi[:, k, :], sgt[:, 2 + k % 2, :], ACT.Copy).then_inc(xh_ready, 1)

            def pre(n):
                norm(n, h, lambda k: act.wait_ge(h_ready, 8 * (n // 2) + k + 1), True)

            def post(n, name):
                norm(n, f, lambda k: act.wait_ge(psum_free[k % 2], TB[name] // 2 + k // 2 + 1), False)

            def stat_root(g, n, scale, eps):
                act.wait_ge(stat_summed, g + 1)
                fn(st_sd[:, 0:n], psum[:, 7, 0:n], ACT.Sqrt, scale=scale, bias=eps).then_inc(stat_rooted, 1)

            def centred(g, xc, xs):
                for j in range(GT):
                    act.wait_ge(cen_ready, 4 * g + j + 1)
                    fn(tok(xc[:, j, :]), halves(4 * (j % 2)), ACT.Copy).then_inc(cen_copied, 1)
                    fn(tok(xs[:, j, :]), halves(4 * (j % 2)), ACT.Square).then_inc(cen_copied, 1)

            def cat(i, parts):
                for k in range(KT):
                    fn(xhi[:, k, :], parts[k // 4][:, k % 4, :], ACT.Copy).then_inc(cath_ready, 1)

            def even_mix():
                act.wait_ge(sem("shift_turned"), 1)
                for n in range(4):
                    fn(shst[:, 4 * n:4 * n + 4, :].rearrange("p a b -> p (a b)"), psum[0:9, n, :], ACT.Copy).then_inc(sem("shift_copied"), 1)
                for i in range(4):
                    act.wait_ge(sem("tk_turned"), i + 1)
                    if i:
                        act.wait_ge(sem("pv_done"), i)
                    for n, x in enumerate((ktok, vtok)):
                        fn(x[:, :, :].rearrange("p a b -> p (a b)"), bank(n), ACT.Copy).then_inc(sem("tk_copied"), 1)
                    act.wait_ge(sem("pv_done"), i + 1)
                    fn(A[0][:, :, i * P:(i + 1) * P], psum[:, 4, :].rearrange("p (a b) -> p a b", a=GT), ACT.Copy).then_inc(sem("o_copied"), 1)
                act.wait_ge(sem("vs_turned"), 1)
                fn(vs8[:, :], psum[0:NS, 6, :], ACT.Copy).then_inc(sem("vs8_ready"), 1)
                act.wait_ge(sem("os_ready"), 1)
                for hh in range(2):
                    hp = slice(hh * HD, (hh + 1) * HD)
                    fn(A[0][hp, :, SEQ:T], psum[hp, 2 + hh, 0:GT * NS].rearrange("p (a b) -> p a b", a=GT), ACT.Copy).then_inc(sem("o_copied"), 1)
                act.wait_ge(sem("rows_stored"), 48)
                centred(0, X[0], X[1])
                stat_root(0, 40, 1.0, eps_col)
                fn(A[3][:, :, :], A[3][:, :, :], ACT.Silu).then_inc(sem("silu_ready"), 1)
                act.wait_ge(sem("l1_ready"), 1)
                fn(tok(tw[:, :]), halves(0)[0:HD], ACT.Tanh).then_inc(sem("l1_copied"), 1)
                act.wait_ge(sem("l1_ready"), 2)
                fn(tok(ta[:, :]), halves(2)[0:HD], ACT.Copy).then_inc(sem("l1_copied"), 1)
                act.wait_ge(sem("l1_ready"), 3)
                fn(tok(tg[:, :]), halves(4), ACT.Sigmoid).then_inc(sem("l1_copied"), 1)
                act.wait_ge(sem("rkv_ready"), 3)
                for n in range(12):
                    j, kind = n % 4, n // 4
                    act.wait_ge(sem("l2_ready"), n + 1)
                    src = halves(4 * (n % 2))
                    if kind == 0:
                        ins = fn(tok(A[2][:, j, :]), src, ACT.Sigmoid, bias=V("w0", j))
                    elif kind == 1:
                        ins = fn(tok(FA[1][:, j, :]), src, ACT.Sigmoid, bias=V("a0", j))
                    else:
                        ins = fn(tok(A[7][:, j, :]), src, ACT.Copy)
                    ins.then_inc(sem("l2_copied"), 1)
                for j in range(GT):
                    act.wait_ge(sem("kk_raw"), j + 1)
                    fn(X[3][:, j, :], FA[0][:, j, :], ACT.Square).then_inc(sem("kk_sq"), 1)
                act.wait_ge(sem("kk_clamped"), 1)
                fn(st_sd[:, 0:40], st_in[:, 0:40], ACT.Sqrt).then_inc(stat_rooted, 1)
                act.wait_ge(sem("cs_ready"), 1)
                fn(A[3][:, :, :], A[5][:, :, :], ACT.Exp, scale=DC).then_inc(sem("dec_ready"), 1)
                fn(A[2][:, :, :], A[2][:, :, :], ACT.Exp, scale=-DC).then_inc(sem("dec_ready"), 1)
                act.wait_ge(sem("dec_ready"), 2)
                fn(A[5][:, :, :], A[5][:, :, :], ACT.Exp, scale=-DC).then_inc(sem("dec_ready"), 1)
                act.wait_ge(sem("rw_turned"), 1)
                for n in range(5):
                    fn(rows8[n][:, :], psum[0:NS, n, :], ACT.Copy).then_inc(sem("rows8_ready"), 1)

                with act.Fori(0, NCH) as it:
                    W = lambda who, step: in_chunk(act, it, who, step)
                    full = lambda x: x[:, :, :].rearrange("p a b -> p (a b)")

                    def copy(dst, b, n=512, scale=1.0):
                        fn(full(dst), bank(b, n), ACT.Copy, scale=scale).then_inc(ch_act, 1)

                    W("pe", "mats")
                    copy(c["bt"], 5)
                    copy(c["kt"], 6)
                    copy(vc, 7, 256)
                    W("pe", "rhs")
                    copy(rc, 7, 256)
                    W("pe", "a2")
                    copy(c["s4"], 1)
                    W("pe", "a4")
                    copy(c["s1"], 0)
                    copy(c["s2"], 1)
                    W("pe", "a8")
                    copy(c["s3"], 0)
                    W("pe", "f")
                    copy(c["s1"], 0)
                    copy(c["s2"], 1)
                    copy(c["s4"], 2)
                    W("pe", "hh")
                    copy(c["s5"], 1)
                    W("pe", "w")
                    copy(c["wt"], 2, 512, -1.0)
                    W("pe", "out")
                    for hh in range(2):
                        hp = slice(hh * HD, (hh + 1) * HD)
                        fn(c["ob"][hp, :, hp], psum[hp, 4, 0:256].rearrange("p (a b) -> p a b", a=GT), ACT.Copy).then_inc(ch_act, 1)
                    W("pe", "turn")
                    fn(X[3][:, :, bass.ds(it * CH, CH)], psum[:, 6, 0:256].rearrange("p (a b) -> p a b", a=GT), ACT.Copy).then_inc(ch_act, 1)
                act.wait_ge(sem("state_turned"), 1)
                fn(rwst[:, :, :].rearrange("p a b -> p (a b)"), psum[0:HD, 6, :], ACT.Copy).then_inc(sem("rwst_ready"), 1)
                centred(1, FA[0], FA[1])
                stat_root(2, 40, 1.0, gn_eps_col)
                act.wait_ge(sem("ob_ready"), 4)
                cat(0, (A[0], A[7]))

            def odd_mix():
                act.wait_ge(sem("lconv_turned"), 1)
                fn(lcst[:, :], psum[0:11, 6, :], ACT.Copy).then_inc(sem("lconv_copied"), 1)
                act.wait_ge(sem("lam_abs"), 1)
                fn(lt[:, 4:8], lt[:, 0:4], ACT.Exp, scale=-1.0).then_inc(sem("lam_exp"), 1)
                act.wait_ge(sem("lam_exp"), 1)
                fn(lt[:, 8:12], lt[:, 4:8], ACT.Ln, bias=1.0).then_inc(sem("lam_ln"), 1)
                act.wait_ge(sem("dlam_sums"), 2)
                fn(lamt[:, 2:4], lamt[:, 0:2], ACT.Exp).then_inc(sem("dlam_exp"), 1)
                for n in range(8):
                    j = n % 4
                    act.wait_ge(sem("gates_ready"), n + 1)
                    fn(tok(X[1 + n // 4][:, j, :]), halves(4 * (n % 2)), ACT.Sigmoid, bias=V("ba" if n < 4 else "bi", j)).then_inc(sem("gates_copied"), 1)
                act.wait_ge(sem("lru_sp_ready"), 1)
                act.wait_ge(sem("gates_copied"), 8)
                for j in range(GT):
                    fn(X[3][:, j, :], X[1][:, j, :], ACT.Tanh, scale=lru_sp[:, j:j + 1]).then_inc(sem("lru_decays"), 1)
                for j in range(GT):
                    fn(X[1][:, j, :], X[1][:, j, :], ACT.Exp, scale=lru_nsp[:, j:j + 1]).then_inc(sem("lru_decays"), 1)
                act.wait_ge(sem("lru_v"), 1)
                fn(X[3][:, :, :], X[3][:, :, :], ACT.Sqrt).then_inc(sem("lru_root"), 1)
                fn(A[4][:, :, :], A[4][:, :, :], ACT.Gelu_apprx_tanh).then_inc(sem("gelu_ready"), 1)
                for x in range(5):
                    w = P if x < 4 else NS
                    act.wait_ge(sem("kv_turned"), x + 1)
                    for n in range(2):
                        dst = (vtm, ktm)[n][:, x, :] if x < 4 else (vs8o, ks8)[n][:, :]
                        fn(dst, psum[0:w, 2 * (x % 2) + n, :], ACT.Copy).then_inc(sem("kv_copied"), 1)
                act.wait_ge(sem("qs_turned"), 1)
                fn(qs8[:, :], psum[0:NS, 4, :], ACT.Copy).then_inc(sem("qs_copied"), 1)
                act.wait_ge(sem("lruh_turned"), 1)
                fn(lhst[:, :], psum[0:9, 5, :], ACT.Copy).then_inc(sem("lruh_copied"), 1)
                act.wait_ge(sem("lru_done"), 1)
                for n in range(16):
                    i, j = n // 4, n % 4
                    nk = (i + 1) * P
                    act.wait_ge(sem("mx_ready"), n + 1)
                    if n >= 2:
                        act.wait_ge(sem("wt_turned"), n - 1)
                    for m in range(2):
                        fn(probs[:, n % 2, m, 0:nk], psum[:, 2 * (n % 2) + m, 0:nk], ACT.Exp, bias=nb2[:, m:m + 1], scale=HD ** -0.5,
                           accum_out=l2[:, m:m + 1]).then_inc(sem("exp_done"), 1)
                    act.wait_ge(sem("wt_turned"), n + 1)
                    if n >= 2:
                        act.wait_ge(sem("pv2_done"), n - 1)
                    fn(wtp[:, n % 2, 0:nk], psum[:, 4 + n % 2, 0:nk], ACT.Copy).then_inc(sem("wt_copied"), 1)
                    act.wait_ge(sem("pv2_done"), n + 1)
                    fn(A[0][:, j, i * P:(i + 1) * P], psum[:, 6 + n % 2, 0:P], ACT.Copy).then_inc(sem("oc_copied"), 1)
                act.wait_ge(sem("mxn_ready"), 1)
                for m in range(2):
                    fn(pdec[:, m, :], psum[0:32, 2 + m, :], ACT.Exp, bias=mxn[0:32, m:m + 1], scale=HD ** -0.5,
                       accum_out=l2[0:32, m:m + 1]).then_inc(sem("expd_done"), 1)
                    fn(pn2[0:32, m:m + 1], psum[0:32, 4, m:m + 1], ACT.Exp, bias=mxn[0:32, m:m + 1], scale=HD ** -0.5).then_inc(sem("expd_done"), 1)
                act.wait_ge(sem("wd_turned"), 1)
                fn(wtd[:, :, :].rearrange("p a b -> p (a b)"), psum[:, 5, 0:128], ACT.Copy).then_inc(sem("wtd_copied"), 1)
                act.wait_ge(sem("os2_ready"), 1)
                fn(X[1][:, :, :], A[0][:, :, :], ACT.Square).then_inc(sem("oc_sq"), 1)
                stat_root(3, 20, 1.0 / P, eps_col)
                act.wait_ge(sem("ob_ready"), 8)
                cat(1, (A[0], A[4]))

            def mix_in(i):
                name = ("mix_in", i)
                u0, t0 = UB[name], TB[name]
                with act.Fori(0, NT[name] // 4) as it:
                    for m in range(4):
                        ahead(it * 4 + (u0 + m), m)
                        if m % 2 == 0:
                            continue
                        act.wait_ge(unit_used, it * 4 + (u0 + m))
                        fn(one2(u, it * 4 + (m - 1)), halves(0), ACT.Copy).then_inc(psum_free[0], 1)

            def just_ahead(name, n):
                with act.Fori(0, n) as it:
                    for m in range(4):
                        ahead(it * 4 + (UB[name] + m), m)

            def gate(i):
                name = ("gate", i)
                u0 = UB[name]
                with act.Fori(0, 2) as it:
                    for m in range(4):
                        ahead(it * 4 + (u0 + m), m)
                        act.wait_ge(unit_used, it * 4 + (u0 + m + 1))
                        fn(one2(f, it * 4 + m), halves(4 * (m % 2)), ACT.Sigmoid).then_inc(psum_free[m % 2], 1)

            for r in range(3):
                ahead(r, r, 0)
            act.wait_ge(sem("eps_set"), 2)
            for i in range(2):
                pre(NORM[(i, 0)])
                ffn(i, 0)
                post(NORM[(i, 1)], ("out", i, 0, 1))
                pre(NORM[(i, 2)])
                mix_in(i)
                (even_mix if i == 0 else odd_mix)()
                just_ahead(("mix_out", i), 2)
                post(NORM[(i, 3)], ("mix_out", i))
                pre(NORM[(i, 4)])
                ffn(i, 1)
                post(NORM[(i, 5)], ("out", i, 1, 1))
                pre(NORM[(i, 6)])
                gate(i)
                act.wait_ge(sem("p_turned"), i + 1)
                for k in range(2):
                    b = (2 + 4 * k) * 512
                    fn(phi[:, k, :], flat[:, b:b + T], ACT.Copy).then_inc(sem("phi_ready"), 1)
                for e in range(4):
                    ahead(UB[("ple", i)] + e, e)
                post(NORM[(i, 7)], ("ple", i))

        @block.vector
        def _(dve):
            own = Steps(dve, sem("dve_steps"))
            tt, ts, stt = nc.vector.tensor_tensor, nc.vector.tensor_scalar, nc.vector.scalar_tensor_tensor

            def ahead(u, r, lead=3):
                u, r = u + lead, r + lead
                if isinstance(u, int) and u >= NU:
                    return
                s, w = r % 4, raw_cols(u)
                dve.wait_ge(hi_ready, u + 1)
                tt(wlo[s][:, 0:w], raw[s][:, 0:w], whi[s][:, 0:w].bitcast(F32), ALU.subtract).then_inc(lo_ready, 1)

            def ffn(i, a):
                for r in range(2):
                    name = ("in", i, a, r)
                    u0, p0 = UB[name], PAIRS[name]
                    with dve.Fori(0, 8) as it:
                        for p in range(2):
                            for g in range(2):
                                ahead(it * 4 + (u0 + 2 * p + g), 2 * p + g)
                            pr = it * 2 + (p0 + p)
                            dve.wait_ge(sg_ready, pr + 1)
                            tt(tok(sgt[:, 2 + p, :]), tok(sgt[:, p, :]), halves(4 * p + 2), ALU.mult).then_inc(hid_ready, 1)
                            dve.wait_ge(hhi_ready, pr + 1)
                            tt(one(glo, it * 2 + p), sgt[:, 2 + p, :], one(ghi, it * 2 + p).bitcast(F32), ALU.subtract).then_inc(psum_free[p], 1)
                    name = ("out", i, a, r)
                    uo = UB[name]
                    with dve.Fori(0, 4) as it:
                        for m in range(2):
                            for g in range(2):
                                ahead(it * 4 + (uo + 2 * m + g), 2 * m + g)
                            dve.wait_ge(unit_used, it * 4 + (uo + 2 * m + 2))
                            dst = one2(f, it * 2 + m)
                            if r == 0:
                                ins = nc.vector.tensor_copy(dst, halves(4 * m))
                            else:
                                ins = tt(dst, halves(4 * m), dst, ALU.add)
                            ins.then_inc(psum_free[m], 1)

            RB = flat[:, 1024:1024 + T]

            def rstd(n):
                dve.wait_ge(sd_ready, n + 1)
                nc.vector.reciprocal(rs5b, rs5).then_inc(rs_ready, 1)
                dve.wait_ge(rb_ready, n + 1)

            def pre(n):
                rstd(n)
                for k in range(KT + 1):
                    if k < KT:
                        if k >= 2:
                            dve.wait_ge(xn_ready, 8 * (n // 2) + k - 1)
                        stt(sgt[:, 2 + k % 2, :], h[:, k, :], gcol[:, n * 8 + k:n * 8 + k + 1], RB, ALU.mult, ALU.mult).then_inc(xt_ready, 1)
                    if k >= 1:
                        j = k - 1
                        dve.wait_ge(xh_ready, 8 * (n // 2) + j + 1)
                        tt(xlo[:, j, :], sgt[:, 2 + j % 2, :], xhi[:, j, :].bitcast(F32), ALU.subtract).then_inc(xn_ready, 1)

            def post(n):
                rstd(n)
                for k in range(KT + 1):
                    if k < KT:
                        own(stt(f[:, k, :], f[:, k, :], gcol[:, n * 8 + k:n * 8 + k + 1], RB, ALU.mult, ALU.mult))
                    if k >= 1:
                        j = k - 1
                        dve.wait_ge(own.sem, own.n - (1 if k < KT else 0))
                        tt(h[:, j, :], h[:, j, :], f[:, j, :], ALU.add).then_inc(h_ready, 1)

            def stat_rate(g, n):
                dve.wait_ge(stat_rooted, g + 1)
                nc.vector.reciprocal(st_rs[:, 0:n], st_sd[:, 0:n]).then_inc(stat_ready, 1)

            def spread_mul(g, dst, src, gain=None):
                for j in range(GT):
                    dve.wait_ge(stat_spread, 4 * g + j + 1)
                    rb = flat[:, 4 * (j % 2) * 512:4 * (j % 2) * 512 + T]
                    if gain is None:
                        tt(dst[:, j, :], src[:, j, :], rb, ALU.mult).then_inc(stat_used, 1)
                    else:
                        stt(dst[:, j, :], src[:, j, :], gain, rb, ALU.mult, ALU.mult).then_inc(stat_used, 1)
                dve.wait_ge(stat_used, 4 * (g + 1))

            def cat(i, parts):
                for k in range(KT):
                    dve.wait_ge(cath_ready, 8 * i + k + 1)
                    tt(xlo[:, k, :], parts[k // 4][:, k % 4, :], xhi[:, k, :].bitcast(F32), ALU.subtract).then_inc(cat_ready, 1)

            def even_mix():
                q, k, v = A[0], A[1], A[2]
                dve.wait_ge(sem("tables_loaded"), 32)
                for n in range(8):
                    j, x = n % 4, A[n // 4]
                    dve.wait_ge(sem("rot_ready"), n + 1)
                    tt(tok(X[1][:, j, :]), halves(4 * (n % 2)), tok(rope[:, 1, :]), ALU.mult).then_inc(sem("rot_used"), 1)
                    own(tt(x[:, j, :], x[:, j, :], rope[:, 0, :], ALU.mult))
                    own.settle()
                    dve.wait_ge(sem("rot_used"), n + 1)
                    own(tt(x[:, j, :], x[:, j, :], X[1][:, j, :], ALU.add))
                    own.settle()
                    tt(x[:, j, :], x[:, j, :], decay[:, n // 4, j, :], ALU.mult).then_inc(sem("qk_ready"), 1)
                for i in range(4):
                    dve.wait_ge(sem("sc_ready"), i + 1)
                    if i:
                        dve.wait_ge(sem("pv_done"), i)
                    else:
                        dve.wait_ge(sem("qk_ready"), 8)
                    for hh in range(2):
                        tt(att[:, hh, :, :], psum[:, 2 + hh, :].rearrange("p (a b) -> p a b", a=GT),
                           C("causal_t").rearrange("p (o b) -> p o b", o=1).to_broadcast([P, GT, P]), ALU.mult).then_inc(sem("att_ready"), 1)
                    dve.wait_ge(sem("pv_done"), i + 1)
                    dve.wait_ge(sem("ubd_ready"), i + 1)
                    for hh in range(2):
                        hp = slice(hh * HD, (hh + 1) * HD)
                        ins = tt(ubd[hp, :, hp], ubd[hp, :, hp], psum[hp, 5, :].rearrange("p (a b) -> p a b", a=GT)[:, :, hp], ALU.add)
                        own(ins) if hh == 0 else ins.then_inc(sem("ubd_ready"), 1)
                    own.settle()
                dve.wait_ge(sem("ubd_ready"), 5)
                for hh in range(2):
                    hp = slice(hh * HD, (hh + 1) * HD)
                    tt(uout[hp, :, :], ubd[hp, :, hp], C("g511")[hp].rearrange("p (a o) -> p a o", o=1).to_broadcast([HD, GT, HD]), ALU.mult).then_inc(sem("uout_ready"), 1)
                dve.wait_ge(sem("sret_loaded"), 16 * GT)
                for j in range(GT):
                    dve.wait_ge(sem("vb_ready"), j + 1)
                    if j:
                        dve.wait_ge(sem("sret_ready"), j)
                    tt(kvt[:, :, :], psum[:, j % 2, :].rearrange("p (b v) -> p b v", b=NS),
                       k[:, j, SEQ:T].rearrange("p (b o) -> p b o", o=1).to_broadcast([P, NS, HD]), ALU.mult).then_inc(sem("vb_used"), 1)
                    dve.wait_ge(sem("vb_used"), j + 1)
                    stt(s_ret[:, j, :, :], s_ret[:, j, :, :], C("gam")[:, j:j + 1], kvt[:, :, :], ALU.mult, ALU.add).then_inc(sem("sret_ready"), 1)
                r_, k_, v_, z_ = A[4], A[5], A[6], A[7]

                def shift(x, n, d):
                    own(ts(d[:, :, 0:1], x[:, :, 0:1], -1.0, None, ALU.mult))
                    own(tt(d[:, :, 1:SEQ], x[:, :, 0:SEQ - 1], x[:, :, 1:SEQ], ALU.subtract))
                    own(tt(d[:, :, SEQ:T], shcol[:, :].rearrange("p (b j) -> p j b", b=NS)[:, 4 * n:4 * n + 4, :], x[:, :, SEQ:T], ALU.subtract))
                    own.settle()

                def lerp(dst, x, d, mu, signal):
                    for j in range(GT):
                        stt(dst[:, j, :], d[:, j, :], V("mu", 4 * mu + j), x[:, j, :], ALU.mult, ALU.add).then_inc(signal, 1)

                stat_rate(0, 40)
                spread_mul(0, X[0], X[0])
                dve.wait_ge(sem("silu_ready"), 1)
                tt(A[0][:, :, :], X[0][:, :, :], A[3][:, :, :], ALU.mult).then_inc(sem("oa_ready"), 1)
                dve.wait_ge(sem("oa_ready"), 1)
                dve.wait_ge(sem("sret_stored"), 64)
                dve.wait_ge(sem("rows_stored"), 48)
                shift(z_, 3, FA[0])
                lerp(FA[1], z_, FA[0], 3, sem("z_ready"))
                lerp(X[3], z_, FA[0], 4, sem("z_ready"))
                lerp(A[1], z_, FA[0], 5, sem("z_ready"))
                for n, (x, dst) in enumerate(((r_, X[0]), (k_, X[1]), (v_, X[2]))):
                    shift(x, n, A[2])
                    for j in range(GT):
                        own(stt(dst[:, j, :], A[2][:, j, :], V("mu", 4 * n + j), x[:, j, :], ALU.mult, ALU.add))
                    own.settle()
                nc.vector.memset(small[:, 190:191], 0.0).then_inc(sem("rkv_ready"), 3)
                for j in range(GT):
                    dve.wait_ge(sem("z_ready"), 12)
                    ts(FA[0][:, j, :], X[1][:, j, :], V("kk", j), None, ALU.mult).then_inc(sem("kk_raw"), 1)
                dve.wait_ge(stat_summed, 2)
                own(ts(st_in[:, 0:40], psum[:, 7, 0:40], 1e-24, None, ALU.max))
                own.settle()
                nc.vector.memset(small[:, 190:191], 0.0).then_inc(sem("kk_clamped"), 1)
                own(ts(omka, vcol[:, VEC["ka"][0]:VEC["ka"][0] + 4], -1.0, 1.0, ALU.mult, ALU.add))
                own.settle()
                dve.wait_ge(sem("l2_copied"), 8)
                for j in range(GT):
                    own(ts(A[4][:, j, :], FA[1][:, j, :], V("ka", j), omka[:, j:j + 1], ALU.mult, ALU.add))
                own.settle()
                own(tt(X[1][:, :, :], X[1][:, :, :], A[4][:, :, :], ALU.mult))
                stat_rate(1, 40)
                spread_mul(1, FA[0], FA[0])
                own(tt(FA[1][:, :, :], FA[1][:, :, :], FA[0][:, :, :], ALU.mult))
                dve.wait_ge(sem("tables_loaded"), 48)
                for j in range(GT):
                    own(nc.vector.tensor_tensor_scan(A[5][:, j, 0:SEQ], reset[:, :], A[2][:, j, 0:SEQ], 0.0, ALU.mult, ALU.add))
                own(nc.vector.tensor_copy(A[5][:, :, SEQ:T], A[2][:, :, SEQ:T]))
                own.settle()
                own(tt(A[2][:, :, :], A[5][:, :, :], A[2][:, :, :], ALU.subtract))
                own.settle()
                dve.wait_ge(sem("l2_copied"), 12)
                nc.vector.memset(small[:, 190:191], 0.0).then_inc(sem("cs_ready"), 1)
                dve.wait_ge(sem("dec_ready"), 3)
                nc.vector.memset(small[:, 190:191], 0.0).then_inc(sem("rw_ready"), 1)
                dve.wait_ge(sem("srw_loaded"), 16 * GT)
                bcn = [0]

                def bc():
                    bcn[0] += 1
                    dve.wait_ge(sem("bc_ready"), bcn[0])
                    return psum[:, (bcn[0] - 1) % 6, :].rearrange("p (b k) -> p b k", b=NS)

                def col(x):
                    return x.rearrange("p (b o) -> p b o", o=1).to_broadcast([P, NS, HD])

                for j in range(GT):
                    S = s_rw[:, j, :, :]
                    t0, t1 = swt[0][:, :, :], swt[1][:, :, :]

                    def step(ins):
                        ins.then_inc(sem("bc_used"), 1)
                        dve.wait_ge(sem("bc_used"), bcn[0])

                    def mine(ins):
                        own(ins)
                        own.settle()

                    step(tt(t0, S, bc(), ALU.mult))
                    mine(nc.vector.tensor_reduce(sa8[:, :], t0, axis=AX.X, op=ALU.add))
                    step(tt(S, S, bc(), ALU.mult))
                    step(tt(t1, bc(), col(sa8[:, :]), ALU.mult))
                    mine(tt(S, S, t1, ALU.subtract))
                    step(tt(t0, bc(), col(X[2][:, j, SEQ:T]), ALU.mult))
                    mine(tt(S, S, t0, ALU.add))
                    step(tt(t1, S, bc(), ALU.mult))
                    mine(nc.vector.tensor_reduce(X[3][:, j, SEQ:T], t1, axis=AX.X, op=ALU.add))
                nc.vector.memset(small[:, 190:191], 0.0).then_inc(sem("srw_ready"), 1)
                own(nc.vector.memset(uc[:, :, :], 0.0))
                own.settle()
                dve.wait_ge(sem("srw_stored"), 16 * GT)
                dve.wait_ge(sem("bd_zeroed"), 6)

                with dve.Fori(0, NCH) as it:
                    W = lambda who, step: in_chunk(dve, it, who, step)
                    cols = bass.ds(it * CH, CH)
                    four = lambda x, n=P: x.rearrange("p (a b) -> p a b", a=GT)
                    mask = lambda name: C(name).rearrange("p (o b) -> p o b", o=1).to_broadcast([P, GT, P])

                    def done(ins):
                        ins.then_inc(ch_dve, 1)

                    W("pe", None)
                    for hh in range(2):
                        hp = slice(hh * HD, (hh + 1) * HD)
                        tt(c["al"][hp, :, hp], FA[0][hp, :, cols], A[2][hp, :, cols], ALU.mult)
                        tt(c["be"][hp, :, hp], FA[1][hp, :, cols], A[3][hp, :, cols], ALU.mult)
                        tt(c["ka"][hp, :, hp], X[1][hp, :, cols], A[3][hp, :, cols], ALU.mult)
                        tt(c["rh"][hp, :, hp], X[0][hp, :, cols], A[5][hp, :, cols], ALU.mult)
                        last = nc.vector.tensor_copy(c["vb"][hp, :, hp], X[2][hp, :, cols])
                    done(last)
                    W("pe", "mats")
                    done(tt(c["s1"][:, :, :], four(bank(0)), mask("m_a"), ALU.mult))
                    done(tt(c["s2"][:, :, :], four(bank(1)), mask("m_at"), ALU.mult))
                    done(tt(c["s5"][:, :, :], four(bank(0)), mask("m_e"), ALU.mult))
                    W("dve", "at")
                    done(tt(c["s6"][:, :, :], c["s2"][:, :, :], mask("ident"), ALU.add))
                    done(tt(c["akt"][:, :, :], four(bank(2)), mask("m_s"), ALU.mult))
                    W("pe", "a2")
                    done(nc.vector.tensor_copy(c["s3"][:, :, :], four(bank(0))))
                    done(tt(c["rbt"][:, :, :], four(bank(3)), mask("m_i"), ALU.mult))
                    done(tt(c["rkt"][:, :, :], four(bank(4)), mask("m_i"), ALU.mult))
                    W("pe", "a4")
                    done(tt(c["s7"][:, :, :], four(bank(2)), c["s6"][:, :, :], ALU.add))
                    W("pe", "a8")
                    W("dve", "x2")
                    done(tt(c["s6"][:, :, :], four(bank(2)), c["s7"][:, :, :], ALU.add))
                    W("pe", "x8")
                    W("dve", "x4")
                    done(tt(c["s7"][:, :, :], four(bank(2)), c["s6"][:, :, :], ALU.add))
                    W("act", "ft")
                    done(tt(c["s6"][:, :, :], mask("ident"), c["s2"][:, :, :], ALU.subtract))
                    W("pe", "f2")
                    done(tt(c["s3"][:, :, :], four(bank(0)), mask("ident"), ALU.add))
                    W("pe", "z")
                    done(nc.vector.tensor_copy(zc[:, :, :], bank(3, 256).rearrange("p (a b) -> p a b", a=GT)))
                    W("pe", "out")
                    done(tt(uc[:, :, :], uc[:, :, :], bank(5, 256).rearrange("p (a b) -> p a b", a=GT), ALU.add))
                    W("dve", "u0")
                    done(tt(uc[:, :, :], uc[:, :, :], A[5][:, :, bass.ds(it * CH + (CH - 1), 1)].to_broadcast([P, GT, HD]), ALU.mult))
                dve.wait_ge(ch_pe, NCH * len(PE_STEPS))
                own(tt(X[0][:, :, :], X[0][:, :, :], X[1][:, :, :], ALU.mult))
                own.settle()
                for j in range(GT):
                    own(ts(X[0][:, j, :], X[0][:, j, :], V("rk", j), None, ALU.mult))
                own.settle()
                nc.vector.memset(small[:, 190:191], 0.0).then_inc(sem("rkk_ready"), 1)
                stat_rate(2, 40)
                spread_mul(2, X[3], FA[0])
                for j in range(GT):
                    own(ts(X[3][:, j, :], X[3][:, j, :], V("ln", j), V("ln", 4 + j), ALU.mult, ALU.add))
                for j in range(GT):
                    dve.wait_ge(sem("bonus_ready"), j + 1)
                    tt(tok(X[2][:, j, :]), tok(X[2][:, j, :]), halves(4 * (j % 2)), ALU.mult).then_inc(sem("bonus_used"), 1)
                dve.wait_ge(sem("bonus_used"), 4)
                own.settle()
                own(tt(X[3][:, :, :], X[3][:, :, :], X[2][:, :, :], ALU.add))
                own.settle()
                tt(A[7][:, :, :], A[7][:, :, :], X[3][:, :, :], ALU.mult).then_inc(sem("ob_ready"), 4)
                cat(0, (A[0], A[7]))
                dve.wait_ge(sem("rows_stored"), 64)

            def odd_mix():
                xr, xc = A[3], X[0]
                lam = vcol[:, VEC["lam"][0]:VEC["lam"][0] + 4]

                def mine(ins):
                    own(ins)
                    own.settle()

                mine(ts(lt[:, 16:20], lam, -1.0, None, ALU.mult))
                tt(lt[:, 0:4], lt[:, 16:20], lam, ALU.max).then_inc(sem("lam_abs"), 1)
                dve.wait_ge(sem("lam_pages_loaded"), 32)
                mine(tt(dlam[:, 0, :], dlam[:, 0, :], dlam[:, 1, :], ALU.mult))
                nc.vector.tensor_reduce(lamt[:, 0:1], dlam[:, 0, :], axis=AX.X, op=ALU.add).then_inc(sem("dlam_sums"), 1)
                mine(tt(dlam[:, 2, :], dlam[:, 2, :], dlam[:, 3, :], ALU.mult))
                nc.vector.tensor_reduce(lamt[:, 1:2], dlam[:, 2, :], axis=AX.X, op=ALU.add).then_inc(sem("dlam_sums"), 1)
                dve.wait_ge(psum_free[0], TB[("mix_in", 1)] // 2 + 10)
                own.settle()
                for j in range(GT):
                    own(ts(xc[:, j, :], xr[:, j, :], V("conv_w", 12 + j), V("conv_b", j), ALU.mult, ALU.add))
                own.settle()
                buf = lrucol[:, 0:96].rearrange("p (b t j) -> p j t b", b=NS, t=3)
                for d in range(1, 4):
                    for j in range(GT):
                        w = V("conv_w", 4 * (3 - d) + j)
                        own(stt(xc[:, j, d:SEQ], xr[:, j, 0:SEQ - d], w, xc[:, j, d:SEQ], ALU.mult, ALU.add))
                        own(stt(xc[:, j, SEQ:T], buf[:, j, 3 - d, :], w, xc[:, j, SEQ:T], ALU.mult, ALU.add))
                    own.settle()
                nc.vector.memset(small[:, 190:191], 0.0).then_inc(sem("xc_ready"), 1)
                dve.wait_ge(sem("lam_ln"), 1)
                mine(ts(lt[:, 0:4], lt[:, 4:8], 1.0, None, ALU.add))
                mine(ts(lt[:, 0:4], lt[:, 0:4], 1.0, None, ALU.subtract))
                mine(ts(lt[:, 12:16], lt[:, 0:4], 0.0, None, ALU.is_equal))
                mine(tt(lt[:, 12:16], lt[:, 12:16], lt[:, 4:8], ALU.mult))
                mine(ts(lt[:, 0:4], lt[:, 0:4], 1e-30, None, ALU.max))
                mine(nc.vector.reciprocal(lt[:, 0:4], lt[:, 0:4]))
                mine(tt(lt[:, 8:12], lt[:, 8:12], lt[:, 4:8], ALU.mult))
                mine(tt(lt[:, 8:12], lt[:, 8:12], lt[:, 0:4], ALU.mult))
                mine(tt(lt[:, 8:12], lt[:, 8:12], lt[:, 12:16], ALU.add))
                mine(ts(lt[:, 16:20], lt[:, 16:20], 0.0, None, ALU.max))
                mine(tt(lt[:, 8:12], lt[:, 8:12], lt[:, 16:20], ALU.add))
                mine(ts(lru_sp, lt[:, 8:12], 8.0, None, ALU.mult))
                ts(lru_nsp, lt[:, 8:12], -8.0, None, ALU.mult).then_inc(sem("lru_sp_ready"), 1)
                dve.wait_ge(sem("dlam_exp"), 1)
                mine(tt(neglam, lamt[:, 3:4], lamt[:, 2:3], ALU.subtract))
                mine(ts(neglam, neglam, LAM_INIT, None, ALU.subtract))
                dve.wait_ge(sem("gates_copied"), 8)
                own(tt(FA[0][:, :, :], X[2][:, :, :], X[0][:, :, :], ALU.mult))
                dve.wait_ge(sem("lru_decays"), 8)
                mine(tt(FA[1][:, :, :], X[1][:, :, :], X[1][:, :, :], ALU.mult))
                for j in range(GT):
                    own(stt(X[3][:, j, :], FA[1][:, j, :], 1.0, X[3][:, j, :], ALU.add, ALU.mult))
                own.settle()
                nc.vector.memset(small[:, 190:191], 0.0).then_inc(sem("lru_v"), 1)
                dve.wait_ge(sem("lru_root"), 1)
                mine(tt(FA[1][:, :, :], FA[0][:, :, :], X[3][:, :, :], ALU.mult))
                for j in range(GT):
                    own(nc.vector.tensor_tensor_scan(FA[0][:, j, 0:SEQ], X[1][:, j, 0:SEQ], FA[1][:, j, 0:SEQ], 0.0, ALU.mult, ALU.add))
                mine(tt(FA[0][:, :, SEQ:T], X[1][:, :, SEQ:T], lrucol[:, 96:128].rearrange("p (b j) -> p j b", b=NS), ALU.mult))
                mine(tt(FA[0][:, :, SEQ:T], FA[0][:, :, SEQ:T], FA[1][:, :, SEQ:T], ALU.add))
                nc.vector.memset(small[:, 190:191], 0.0).then_inc(sem("lruh_ready"), 1)
                dve.wait_ge(sem("gelu_ready"), 1)
                mine(tt(A[4][:, :, :], A[4][:, :, :], FA[0][:, :, :], ALU.mult))
                dve.wait_ge(sem("lruh_turned"), 1)
                nc.vector.memset(small[:, 190:191], 0.0).then_inc(sem("lru_done"), 1)
                for n in range(16):
                    i = n // 4
                    nk = (i + 1) * P
                    ps = psum[:, 2 * (n % 2):2 * (n % 2) + 2, :]
                    dve.wait_ge(sem("qk2_ready"), n + 1)
                    mine(tt(ps[:, :, i * P:nk], ps[:, :, i * P:nk], C("causal_add").rearrange("p (o b) -> p o b", o=1).to_broadcast([P, 2, P]), ALU.add))
                    mine(nc.vector.tensor_reduce(mx2, ps[:, :, 0:nk], axis=AX.X, op=ALU.max))
                    ts(nb2, mx2, -HD ** -0.5, None, ALU.mult).then_inc(sem("mx_ready"), 1)
                    dve.wait_ge(sem("exp_done"), 2 * (n + 1))
                    mine(nc.vector.reciprocal(rl2, l2))
                    mine(tt(rl2[:, 1:2], rl2[:, 1:2], neglam, ALU.mult))
                    mine(ts(probs[:, n % 2, 0, 0:nk], probs[:, n % 2, 0, 0:nk], rl2[:, 0:1], None, ALU.mult))
                    stt(probs[:, n % 2, 0, 0:nk], probs[:, n % 2, 1, 0:nk], rl2[:, 1:2], probs[:, n % 2, 0, 0:nk], ALU.mult, ALU.add).then_inc(sem("w_ready"), 1)
                dve.wait_ge(sem("lru_stored"), 80)
                tt(prodn[:, :, :].rearrange("p b h -> p h b"), A[0][:, :, SEQ:T], A[1][:, :, SEQ:T], ALU.mult).then_inc(sem("sdec_ready"), 1)
                for b in range(NS):
                    dve.wait_ge(sem(f"kd_loaded{b % 2}"), 64 * (b // 2 + 1))
                    dve.wait_ge(sem("qb_ready"), b + 1)
                    dve.wait_ge(sem("sdec_ready"), b + 1)
                    tt(kprod[:, :, :], kd[b % 2][:, :, :], bank(b % 2).rearrange("p (o n) -> p o n", o=1).to_broadcast([P, PAGES, GW]), ALU.mult).then_inc(sem("qb_used"), 1)
                    dve.wait_ge(sem("qb_used"), b + 1)
                    for x in range(PAGES):
                        ins = nc.vector.tensor_reduce(sdec[:, :, x, b, :].rearrange("p m h -> p h m"), kprod[:, x, :].rearrange("p (h m d) -> p h m d", h=4, m=2), axis=AX.X, op=ALU.add)
                    ins.then_inc(sem("sdec_ready"), 1)
                dve.wait_ge(sem("sd_turned"), 1)
                ps = psum[0:32, 2:4, :]
                mine(nc.vector.tensor_reduce(mxn[0:32], ps, axis=AX.X, op=ALU.max))
                mine(tt(mxn[0:32], mxn[0:32], psum[0:32, 4, 0:2], ALU.max))
                ts(mxn[0:32], mxn[0:32], -HD ** -0.5, None, ALU.mult).then_inc(sem("mxn_ready"), 1)
                dve.wait_ge(sem("expd_done"), 4)
                mine(tt(l2[0:32], l2[0:32], pn2[0:32], ALU.add))
                mine(nc.vector.reciprocal(rl2[0:32], l2[0:32]))
                mine(tt(rl2[0:32, 1:2], rl2[0:32, 1:2], neglam[0:32], ALU.mult))
                mine(ts(pdec[:, 0, :], pdec[:, 0, :], rl2[0:32, 0:1], None, ALU.mult))
                mine(stt(pdec[:, 0, :], pdec[:, 1, :], rl2[0:32, 1:2], pdec[:, 0, :], ALU.mult, ALU.add))
                mine(tt(wn2[0:32], pn2[0:32], rl2[0:32], ALU.mult))
                mine(tt(wn2[0:32, 0:1], wn2[0:32, 0:1], wn2[0:32, 1:2], ALU.add))
                ts(wdiag[:, :], ident[0:32, 0:32], wn2[0:32, 0:1], None, ALU.mult).then_inc(sem("wd_ready"), 1)
                dve.wait_ge(sem("vd_used"), NS)
                tmp = kprod[:, 0, 0:32].rearrange("p (b h) -> p h b", b=NS)
                mine(tt(tmp, A[2][:, :, SEQ:T], psum[:, 6, 0:32].rearrange("p (b h) -> p h b", b=NS), ALU.mult))
                tt(A[0][:, :, SEQ:T], tmp, psum[:, 7, 0:32].rearrange("p (b h) -> p h b", b=NS), ALU.add).then_inc(sem("os2_ready"), 1)
                own(ts(small[:, 188:189], V("subln"), 1.0 - LAM_INIT, None, ALU.mult))
                own.settle()
                stat_rate(3, 20)
                spread_mul(3, A[0], A[0], small[:, 188:189])
                nc.vector.memset(small[:, 190:191], 0.0).then_inc(sem("ob_ready"), 4)
                cat(1, (A[0], A[4]))

            def mix_in(i):
                name = ("mix_in", i)
                u0 = UB[name]
                with dve.Fori(0, NT[name] // 4) as it:
                    for m in range(4):
                        ahead(it * 4 + (u0 + m), m)
                        if m % 2:
                            dve.wait_ge(unit_used, it * 4 + (u0 + m + 1))
                            nc.vector.tensor_copy(one2(u, it * 4 + m), halves(4)).then_inc(psum_free[1], 1)

            def mix_out(i):
                u0 = UB[("mix_out", i)]
                with dve.Fori(0, 2) as it:
                    for m in range(4):
                        ahead(it * 4 + (u0 + m), m)
                        dve.wait_ge(unit_used, it * 4 + (u0 + m + 1))
                        nc.vector.tensor_copy(one2(f, it * 4 + m), halves(4 * (m % 2))).then_inc(psum_free[m % 2], 1)

            nc.vector.memset(eps_col, EPS).then_inc(sem("eps_set"), 1)
            nc.vector.memset(gn_eps_col, GN_EPS).then_inc(sem("eps_set"), 1)
            dve.wait_ge(sem("rows_turned"), 1)
            for n, (dst, rows) in enumerate(row_tables):
                w = rows.shape[0]
                own(nc.vector.tensor_copy(dst[:, 0:w], psum[:, 6, n * P:n * P + w]))
            own.settle()
            for i in range(2):
                for k in (1, 5):
                    x = (i * 8 + k) * 8
                    own(ts(gcol[:, x:x + 8], gcol[:, x:x + 8], 0.5, None, ALU.mult))
            for k in range(KT):
                dve.wait_ge(sem("xt_turned"), k + 1)
                b = 4 * (k % 2)
                nc.vector.tensor_copy(h[:, k, :], flat[:, b * 512:b * 512 + T]).then_inc(h_ready, 1)
            for r in range(3):
                ahead(r, r, 0)
            own.settle()
            for i in range(2):
                pre(NORM[(i, 0)])
                ffn(i, 0)
                post(NORM[(i, 1)])
                pre(NORM[(i, 2)])
                mix_in(i)
                (even_mix if i == 0 else odd_mix)()
                mix_out(i)
                post(NORM[(i, 3)])
                pre(NORM[(i, 4)])
                ffn(i, 1)
                post(NORM[(i, 5)])
                pre(NORM[(i, 6)])
                with dve.Fori(0, 2) as it:
                    for m in range(4):
                        ahead(it * 4 + (UB[("gate", i)] + m), m)
                for k in range(2):
                    dve.wait_ge(sem("phi_ready"), 2 * i + k + 1)
                    b = (2 + 4 * k) * 512
                    tt(plo[:, k, :], flat[:, b:b + T], phi[:, k, :].bitcast(F32), ALU.subtract).then_inc(sem("plo_ready"), 1)
                for e in range(4):
                    ahead(UB[("ple", i)] + e, e)
                    for m in range(2):
                        dve.wait_ge(unit_used, UB[("ple", i)] + e + 1)
                        dst = tok(f[:, 2 * e + m, :])
                        tt(dst, halves(4 * m), dst, ALU.mult).then_inc(psum_free[m], 1)
                post(NORM[(i, 7)])
            for x in range(5):
                w = P if x < 4 else NS
                dve.wait_ge(sem("y_turned"), x + 1)
                b = 4 * (x % 2) * 512
                dst = stage[:, x, :] if x < 4 else stage_s[:, :]
                nc.vector.tensor_copy(dst, flat[0:w, b:b + D]).then_inc(sem("y_copied"), 1)

        @block.gpsimd
        def _(pool):
            dma = pool.dma_start

            def zero(x, signal):
                nc.gpsimd.memset(x, 0.0).then_inc(signal, 1)

            dma(cst[:, :], I["consts"]).then_inc(sem("inputs_loaded"), 16)
            for dst, src in ROWS:
                dma(dst, src).then_inc(sem("inputs_loaded"), 16)
            dma(stage[:, :, :], I["x_prompt"][0].rearrange("(x p) d -> p x d", p=P)).then_inc(sem("inputs_loaded"), 16)
            dma(stage_s[:, :], I["x_sample"][:, 0, :]).then_inc(sem("inputs_loaded"), 16)

            def p_load(i):
                dma(pst[:, :, :], I["p_prompt"][i, 0].rearrange("(x p) d -> p x d", p=P)).then_inc(sem("p_loaded"), 16)
                dma(pss[:, :], I["p_sample"][i, :, 0, :]).then_inc(sem("p_loaded"), 16)

            pool.wait_ge(xn_ready, 16)
            dma(rope[:, :, :], I["rope"].rearrange("p (a t) -> p a t", a=2)).then_inc(sem("tables_loaded"), 16)
            dma(decay[:, :, :, :], I["decay"].rearrange("p (a j t) -> p a j t", a=2, j=GT)).then_inc(sem("tables_loaded"), 16)
            for s in range(2):
                pool.wait_ge(psum_free[s], TB[("mix_in", 0)] // 2 + 16)
            zero(ubd[:, :, :], sem("ubd_ready"))
            for j in range(GT):
                dma(s_ret[:, j, :, :], I["state_ret"][0, :, 2 * j:2 * j + 2].rearrange("b h d v -> (h d) b v")).then_inc(sem("sret_loaded"), 16)
            pool.wait_ge(sem("shift_copied"), 4)
            dma(O["shift_prompt"][0, 0], shst[0:1, :, :].rearrange("p a b -> p (a b)")).then_inc(sem("rows_stored"), 16)
            dma(O["shift_sample"][0, :, 0, :], shst[1:9, :, :].rearrange("p a b -> p (a b)")).then_inc(sem("rows_stored"), 16)
            pool.wait_ge(sem("qk_ready"), 8)
            dma(reset[:, :], I["reset"]).then_inc(sem("tables_loaded"), 16)
            pool.wait_ge(sem("uout_ready"), 2)
            dma(O["ret_prompt"][0, 0].rearrange("(j h) d v -> (h d) j v", h=2), uout[:, :, :]).then_inc(sem("rows_stored"), 16)
            for j in range(GT):
                pool.wait_ge(sem("sret_ready"), j + 1)
                dma(O["ret_sample"][0, :, 2 * j:2 * j + 2].rearrange("b h d v -> (h d) b v"), s_ret[:, j, :, :]).then_inc(sem("sret_stored"), 16)
            pool.wait_ge(sem("oa_ready"), 1)
            dma(lw1[:, :, :], I["rwkv_w1"][0].rearrange("(k p) n -> p k n", p=P)).then_inc(sem("lora_loaded"), 16)
            dma(la1[:, :, :], I["rwkv_a1"][0].rearrange("(k p) n -> p k n", p=P)).then_inc(sem("lora_loaded"), 16)
            dma(lg1[:, :, :], I["rwkv_g1"][0].rearrange("(k p) n -> p k n", p=P)).then_inc(sem("lora_loaded"), 16)
            dma(lw2[:, :], I["rwkv_w2"][0]).then_inc(sem("lora_loaded"), 16)
            dma(la2[:, :], I["rwkv_a2"][0]).then_inc(sem("lora_loaded"), 16)
            dma(lg2[:, :], I["rwkv_g2"][0]).then_inc(sem("lora_loaded"), 16)
            pool.wait_ge(sem("l1_ready"), 3)
            for j in range(GT):
                dma(s_rw[:, j, :, :], I["state_rwkv"][0, :, 2 * j:2 * j + 2].rearrange("b h v k -> (h v) b k")).then_inc(sem("srw_loaded"), 16)
            pool.wait_ge(sem("cs_ready"), 1)
            for x in ("al", "be", "ka", "rh", "vb", "ob"):
                zero(c[x][:, :, :], sem("bd_zeroed"))
            pool.wait_ge(sem("srw_ready"), 1)
            for j in range(GT):
                dma(O["rwkv_sample"][0, :, 2 * j:2 * j + 2].rearrange("b h v k -> (h v) b k"), s_rw[:, j, :, :]).then_inc(sem("srw_stored"), 16)
            pool.wait_ge(sem("rwst_ready"), 1)
            dma(O["rwkv_prompt"][0, 0].rearrange("(j h) v k -> v j h k", h=2), rwst[:, :, :].rearrange("p j (h k) -> p j h k", h=2)).then_inc(sem("rows_stored"), 16)
            pool.wait_ge(sem("ob_ready"), 4)
            pool.wait_ge(cat_ready, 8)
            p_load(0)
            pool.wait_ge(xn_ready, 8 * 6)
            dma(dlam[:, :, :], I["diff_lam"][0].rearrange("a (o d) -> o a d", o=1).to_broadcast([P, 4, HD])).then_inc(sem("lam_pages_loaded"), 16)
            dma(pages[:, :], I["page_table"].rearrange("(o b) g -> o (b g)", o=1)).then_inc(sem("lam_pages_loaded"), 16)
            for s in range(2):
                pool.wait_ge(psum_free[s], TB[("mix_in", 1)] // 2 + 10)
            zero(wabd[:, :, :], sem("lruw_zeroed"))
            zero(wibd[:, :, :], sem("lruw_zeroed"))
            pool.wait_ge(sem("lruw_zeroed"), 2)
            for n in range(8):
                hp = slice((n % 2) * HD, (n % 2 + 1) * HD)
                dma(wabd[hp, n // 2, hp], I["lru_wa"][0, n]).then_inc(sem("lruw_loaded"), 16)
                dma(wibd[hp, n // 2, hp], I["lru_wi"][0, n]).then_inc(sem("lruw_loaded"), 16)
            pool.wait_ge(sem("lconv_copied"), 1)
            dma(O["lru_conv_prompt"][0, 0], lcst[0:3, :]).then_inc(sem("lru_stored"), 16)
            dma(O["lru_conv_sample"][0, :, 2, :], lcst[3:11, :]).then_inc(sem("lru_stored"), 16)
            dma(O["lru_conv_sample"][0, :, 0:2, :], I["state_lru_conv"][0, :, 1:3, :]).then_inc(sem("lru_stored"), 16)
            pool.wait_ge(sem("lruh_copied"), 1)
            dma(O["lru_h_prompt"][0], lhst[0:1, :]).then_inc(sem("lru_stored"), 16)
            dma(O["lru_h_sample"][0], lhst[1:9, :]).then_inc(sem("lru_stored"), 16)
            pool.wait_ge(sem("kv_copied"), 10)
            dma(O["v_prompt"][0, 0].rearrange("(x p) h d -> p x (h d)", p=P), vtm[:, :, :]).then_inc(sem("kv_stored"), 16)
            dma(O["k_prompt"][0, 0].rearrange("(x p) h d -> p x (h d)", p=P), ktm[:, :, :]).then_inc(sem("kv_stored"), 16)
            dma(O["v_sample"][0, :, 0].rearrange("b h d -> b (h d)"), vs8o[:, :]).then_inc(sem("kv_stored"), 16)
            dma(O["k_sample"][0, :, 0].rearrange("b h d -> b (h d)"), ks8[:, :]).then_inc(sem("kv_stored"), 16)
            pool.wait_ge(sem("lam_pages_loaded"), 32)
            pool.wait_ge(sem("lru_done"), 1)

            def page_loads(cache, dst, b, signal):
                for x in range(PAGES):
                    page = pool.value_load(pages[0:1, b * PAGES + x:b * PAGES + x + 1], min_val=0, max_val=cache.shape[1] - 1)
                    dma(dst[:, x, :], cache[0, bass.ds(page, 1), :, :, :].rearrange("o p h d -> p (o h d)")).then_inc(signal, 16)

            for b in range(2):
                page_loads(I["cache_k"], kd[b], b, sem(f"kd_loaded{b}"))
            for b in range(2):
                page_loads(I["cache_v"], vd[b], b, sem(f"vd_loaded{b}"))
            for b in range(2, NS):
                pool.wait_ge(sem("qb_used"), b - 1)
                page_loads(I["cache_k"], kd[b % 2], b, sem(f"kd_loaded{b % 2}"))
            for b in range(2, NS):
                pool.wait_ge(sem("vd_used"), b - 1)
                page_loads(I["cache_v"], vd[b % 2], b, sem(f"vd_loaded{b % 2}"))
            pool.wait_ge(sem("kv_stored"), 64)
            pool.wait_ge(cat_ready, 16)
            p_load(1)
            pool.wait_ge(sem("y_copied"), 5)
            dma(O["y_prompt"][0].rearrange("(x p) d -> p x d", p=P), stage[:, :, :]).then_inc(sem("y_stored"), 16)
            dma(O["y_sample"][:, 0, :], stage_s[:, :]).then_inc(sem("y_stored"), 16)
            pool.wait_ge(sem("rows_stored"), 64)
            pool.wait_ge(sem("sret_stored"), 64)
            pool.wait_ge(sem("srw_stored"), 64)
            pool.wait_ge(sem("lru_stored"), 80)
            pool.wait_ge(sem("kv_stored"), 64)
            pool.wait_ge(sem("y_stored"), 32)


INS = ["x_prompt", "x_sample", "cache_k", "cache_v", "state_ret", "state_rwkv", "state_rwkv_shift", "state_lru_h",
       "state_lru_conv", "page_table", "p_prompt", "p_sample", "norm_g", "ffn_w_in", "ffn_w_out", "ple_w",
       "ple_gate_w", "ab_w_in", "ab_w_out", "rwkv_mu", "rwkv_w0", "rwkv_w1", "rwkv_w2", "rwkv_a0", "rwkv_a1",
       "rwkv_a2", "rwkv_g1", "rwkv_g2", "rwkv_kk", "rwkv_ka", "rwkv_rk", "rwkv_ln", "cd_w_in", "cd_w_out",
       "diff_lam", "diff_subln", "lru_conv_w", "lru_conv_b", "lru_wa", "lru_ba", "lru_wi", "lru_bi", "lru_lambda"]
OUTS = [("y_prompt", (1, SEQ, D)), ("y_sample", (NS, 1, D)), ("k_prompt", (1, 1, SEQ, 4, 128)),
        ("v_prompt", (1, 1, SEQ, 4, 128)), ("ret_prompt", (1, 1, 8, HD, HD)), ("rwkv_prompt", (1, 1, 8, HD, HD)),
        ("shift_prompt", (1, 1, 1, 4 * GW)), ("lru_h_prompt", (1, 1, GW)), ("lru_conv_prompt", (1, 1, 3, GW)),
        ("k_sample", (1, NS, 1, 4, 128)), ("v_sample", (1, NS, 1, 4, 128)), ("ret_sample", (1, NS, 8, HD, HD)),
        ("rwkv_sample", (1, NS, 8, HD, HD)), ("shift_sample", (1, NS, 1, 4 * GW)), ("lru_h_sample", (1, NS, GW)),
        ("lru_conv_sample", (1, NS, 3, GW))]


def kernel(**inputs):
    import concourse.bacc as bacc
    from concourse.bass_utils import run_bass_kernel_spmd

    nc = bacc.Bacc("TRN2", target_bir_lowering=False, num_devices=1)
    arrays = {f"in_{n}": np.ascontiguousarray(inputs[n]) for n in INS}
    for n, a in zip(("consts", "rope", "decay", "reset"), host_constants()):
        arrays[f"in_{n}"] = a
    I = {n[3:]: nc.dram_tensor(n, a.shape, mybir.dt.from_np(a.dtype), kind="ExternalInput").ap() for n, a in arrays.items()}
    O = {n: nc.dram_tensor(f"out_{n}", s, F32, kind="ExternalOutput").ap() for n, s in OUTS}
    build(nc, I, O)
    r = run_bass_kernel_spmd(nc, [arrays], core_ids=[0])
    return tuple(r.results[0][f"out_{n}"] for n, _ in OUTS)
```

```python
import math
from contextlib import ExitStack

import numpy as np

import concourse.bass as bass
from concourse import mybir
from concourse.alu_op_type import AluOpType as ALU

ACT = mybir.ActivationFunctionType
AX = mybir.AxisListType
F32 = mybir.dt.float32
F32R = mybir.dt.float32r
I32 = mybir.dt.int32

P = 128
SEQ = 512
NS = 8
T = SEQ + NS
TH = T // 2
D = 1024
KT = D // P
GW = 512
GT = GW // P
HD = 64
EPS = 1e-6
GN_EPS = 64e-5
CH = 64
NCH = SEQ // CH
TOK_TILES = [0, 128, 256, 384, T - P]
NEG = -1e30
LAM_INIT = 0.8 - 0.6 * math.exp(-0.3 * 1)
PAGES = 4

CONST = {}
_at = 0
for _n, _w in [("ident", 128), ("bones", 128), ("center", 128), ("rot", 128), ("causal_t", 128),
               ("causal_add", 128), ("m_a", 64), ("m_at", 64), ("m_e", 64), ("m_s", 64),
               ("m_i", 64), ("stack", 64), ("hsel", 2), ("ones2", 2), ("g511", 4), ("gam", 4),
               ("bsel", 2)]:
    CONST[_n] = (_at, _w)
    _at += _w
NCONST = _at

VEC = {}
_at = 0
for _n, _w in [("mu", 24), ("w0", 4), ("a0", 4), ("kk", 4), ("ka", 4), ("rk", 4), ("ln", 8),
               ("conv_w", 16), ("conv_b", 4), ("ba", 4), ("bi", 4), ("lam", 4), ("subln", 1)]:
    VEC[_n] = (_at, _w)
    _at += _w
NVEC = _at


def host_constants():
    c = np.zeros((P, NCONST), np.float32)

    def put(name, a):
        s, w = CONST[name]
        c[:, s:s + w] = a

    i = np.arange(P)
    blk = (i[:, None] // HD) == (i[None, :] // HD)
    r, q = i[:, None] % HD, np.arange(HD)[None, :]
    same16 = (r // 16) == (q // 16)
    put("ident", np.eye(P))
    put("bones", blk)
    put("center", np.eye(P) - blk / HD)
    rot = np.zeros((P, P))
    for m in range(P):
        if m % HD < 32:
            rot[m + 32, m] = -1
        else:
            rot[m - 32, m] = 1
    put("rot", rot)
    put("causal_t", i[:, None] <= i[None, :])
    put("causal_add", np.where(i[None, :] > i[:, None], NEG, 0.0))
    put("m_a", -1.0 * ((q < r) & same16))
    put("m_at", -1.0 * ((r < q) & same16))
    put("m_e", 1.0 * ((q < r) & ~same16))
    put("m_s", 1.0 * (r < q))
    put("m_i", 1.0 * (r <= q))
    put("stack", np.vstack([np.eye(HD)] * 2))
    put("hsel", np.stack([i < HD, i >= HD], 1) / HD)
    put("ones2", np.ones((P, 2)))
    put("bsel", np.stack([i < HD, i >= HD], 1))
    head = np.arange(8)
    lg = np.log1p(-np.exp2(-5.0 - head))
    hp = 2 * np.arange(GT)[None, :] + (i[:, None] // HD)
    put("g511", np.exp((SEQ - 1) * lg[hp]))
    put("gam", np.exp(lg[hp]))
    pos = np.concatenate([np.arange(SEQ), np.full(NS, SEQ)]).astype(np.float64)
    freq = 1.0 / (10000.0 ** np.linspace(0.0, 1.0, 32))
    ang = pos[None, :].astype(np.float32) * freq[i % 32].astype(np.float32)[:, None]
    rope = np.stack([np.cos(ang), np.sin(ang)], 1).astype(np.float32)
    t = np.concatenate([np.arange(SEQ), np.zeros(NS)])
    sample = (np.arange(T) >= SEQ)
    dq = np.exp(t[None, None, :] * lg[hp][:, :, None])
    dk = np.exp(-t[None, None, :] * lg[hp][:, :, None]) * HD ** -0.5
    decay = np.stack([dq, dk], 1).astype(np.float32)
    reset = (np.arange(SEQ) % CH != 0).astype(np.float32)[None].repeat(P, 0)
    return c, rope.reshape(P, 2 * T), decay.reshape(P, 2 * GT * T), reset


class Steps:

    def __init__(self, eng, sem):
        self.eng, self.sem, self.n = eng, sem, 0

    def __call__(self, ins):
        self.n += 1
        ins.then_inc(self.sem, 1)
        return ins

    def settle(self):
        self.eng.wait_ge(self.sem, self.n)


def build(nc, I, O):
    ctx = ExitStack()
    with ctx:
        sems = {}

        def sem(name):
            if name not in sems:
                sems[name] = ctx.enter_context(nc.semaphore(name))
            return sems[name]

        base = (nc.sbuf_base + 63) // 64 * 64
        top = [base]

        def at(name, shape, offset, dt=F32):
            return nc.alloc_sbuf_tensor_at(name, shape, dt, offset=offset)

        def new(name, shape, dt=F32):
            n = int(np.prod(shape[1:])) * 4
            o = top[0]
            top[0] += (n + 31) // 32 * 32
            assert top[0] <= nc.sbuf_usable_end, (name, top[0])
            return at(name, shape, o, dt), o

        UNIT = KT * P
        raw = [new(f"raw{s}", [P, UNIT])[0] for s in range(4)]
        whi, whi_at = zip(*[new(f"whi{s}", [P, UNIT], F32R) for s in range(4)])
        wlo, wlo_at = zip(*[new(f"wlo{s}", [P, UNIT], F32R) for s in range(4)])
        h, _ = new("h", [P, KT, T])
        f, F_AT = new("f", [P, KT, T])
        xhi, X_AT = new("xhi", [P, KT, T], F32R)
        xlo, _ = new("xlo", [P, KT, T], F32R)
        ghi, A_AT = new("ghi", [P, 16, T], F32R)
        glo, _ = new("glo", [P, 16, T], F32R)
        sgt, SG_AT = new("sgt", [P, 4, T])
        sq, SQ_AT = new("sq", [P, 2, T])
        cst, _ = new("cst", [P, NCONST])
        gcol, _ = new("gcol", [P, P])
        vcol, _ = new("vcol", [P, 96])
        shcol, _ = new("shcol", [P, P])
        lrucol, _ = new("lrucol", [P, P])
        small, _ = new("small", [P, 192])
        rs5, rs5b, eps_col, gn_eps_col = small[:, 0:5], small[:, 8:13], small[:, 14:15], small[:, 15:16]
        st_in, st_sd, st_rs = small[:, 16:56], small[:, 56:96], small[:, 96:136]
        omka, lru_sp, lru_nsp, lt = small[:, 136:140], small[:, 140:144], small[:, 144:148], small[:, 148:168]
        neglam, mx2, nb2, l2, rl2 = small[:, 168:169], small[:, 170:172], small[:, 172:174], small[:, 174:176], small[:, 176:178]
        mx2s, nb2s, l2s = (mx2, small[:, 16:18]), (nb2, small[:, 18:20]), (l2, small[:, 20:22])
        lamt, mxn, pn2, wn2 = small[:, 178:182], small[:, 182:184], small[:, 184:186], small[:, 186:188]
        EXTRA = top[0]
        assert EXTRA + 6144 <= nc.sbuf_usable_end, EXTRA
        AR = GT * T * 4
        u = at("u", [P, 32, T], A_AT)
        A = [u[:, 4 * n:4 * n + 4, :] for n in range(8)]
        FA = [at(f"FA{n}", [P, GT, T], F_AT + n * AR) for n in range(2)]
        X = [at(f"X{n}", [P, GT, T], X_AT + n * AR) for n in range(4)]
        stage = at("stage", [P, 4, D], A_AT)
        stage_s = at("stage_s", [NS, D], A_AT + 4 * D * 4)
        phi = at("phi", [P, 2, T], A_AT, F32R)
        plo = at("plo", [P, 2, T], A_AT + 2 * T * 4, F32R)
        pst = at("pst", [P, 4, 256], EXTRA)
        pss = at("pss", [NS, 256], EXTRA + 4096)

        rope = at("rope", [P, 2, T], SG_AT)
        decay = at("decay", [P, 2, GT, T], F_AT)
        shst = at("shst", [9, 16, P], X_AT + 3 * AR)
        ktok = at("ktok", [P, GT, P], X_AT)
        vtok = at("vtok", [P, GT, P], X_AT + 2048)
        ubd = at("ubd", [P, GT, P], X_AT + 4096)
        uout = at("uout", [P, GT, HD], X_AT + 6144)
        vs8 = at("vs8", [NS, GW], SQ_AT)
        att = at("att", [P, 2, GT, P], X_AT + AR)
        kvt = at("kvt", [P, NS, HD], SQ_AT + 2048)
        s_ret = at("s_ret", [P, GT, NS, HD], X_AT + 2 * AR)

        lw1 = at("lw1", [P, GT, HD], A_AT + 3 * AR)
        la1 = at("la1", [P, GT, HD], A_AT + 3 * AR + 1024)
        lg1 = at("lg1", [P, GT, P], A_AT + 3 * AR + 2048)
        lw2 = at("lw2", [HD, GW], A_AT + 3 * AR + 4096)
        la2 = at("la2", [HD, GW], A_AT + 3 * AR + 6144)
        lg2 = at("lg2", [P, GW], EXTRA)
        tw = at("tw", [HD, T], SQ_AT)
        ta = at("ta", [HD, T], SQ_AT + T * 4)
        tg = at("tg", [P, T], SG_AT)
        reset = at("reset", [P, SEQ], SG_AT + T * 4)
        rows8 = [at(f"rows8_{n}", [NS, GW], A_AT + 6 * AR + 2048 * n) for n in range(4)] + [at("rows8_4", [NS, GW], SQ_AT)]
        s_rw = at("s_rw", [P, GT, NS, HD], A_AT + AR)
        swt = [at(f"swt{n}", [P, NS, HD], EXTRA + 2048 * (n + 1)) for n in range(2)]
        sa8 = at("sa8", [P, NS], EXTRA)

        SPLIT_AT = [whi_at[n] for n in range(4)] + [wlo_at[n] for n in range(4)]
        bd_at = SPLIT_AT + [A_AT + 3 * AR + 4096 * n for n in range(6)] + [SG_AT, SG_AT + 4096]
        bd = {x: at(f"bd_{x}", [P, 2 * GT, P], bd_at[n]) for n, x in enumerate(
            ["al", "be", "m", "mt", "m2", "m2t", "e", "ka", "alu", "rh", "wt", "bt", "kt", "akt", "rbt", "rkt"])}
        mv = at("mv", [P, 4, 2 * GT, HD], A_AT + AR)
        mx = at("mx", [P, 2, 2 * GT, HD], A_AT + 6 * AR)
        cm = {x: at(f"cm_{x}", [P, 2 * GT, HD], o) for x, o in
              [("m", A_AT + 6 * AR + 4096), ("mt", A_AT + 6 * AR + 6144), ("m2", SQ_AT + 2048), ("vc", EXTRA)]}
        cm.update(e=mv[:, 3], m2t=mx[:, 0], x1=mx[:, 1])
        zc, rc, uc = [at(f"c_{x}", [P, GT, HD], EXTRA + 3072 + 1024 * n) for n, x in enumerate(["zc", "rc", "uc"])]
        ob = at("ob", [P, GT, P], SQ_AT)
        rwst = at("rwst", [HD, GT, P], SQ_AT + 2048)
        dcol = small[:, 16:16 + GT * NCH].rearrange("p (j c) -> p j c", j=GT)

        wabd = at("wabd", [P, GT, P], A_AT + 5 * AR)
        wibd = at("wibd", [P, GT, P], A_AT + 5 * AR + 2048)
        lcst = at("lcst", [11, GW], A_AT + 7 * AR)
        lhst = at("lhst", [9, GW], A_AT + 7 * AR + 2048)
        vtm = at("vtm", [P, GT, GW], A_AT + 5 * AR)
        ktm = at("ktm", [P, GT, GW], A_AT + 6 * AR)
        ks8 = at("ks8", [NS, GW], EXTRA)
        vs8o = at("vs8o", [NS, GW], EXTRA + 2048)
        qs8 = at("qs8", [NS, GW], EXTRA + 4096)
        dlam = at("dlam", [P, 4, HD], SG_AT)
        pages = at("pages", [1, NS * PAGES], SG_AT + 1024, I32)
        probs = at("probs", [P, 2, 2, SEQ], X_AT)
        wtp = at("wtp", [P, 2, SEQ], X_AT + AR)
        sdec = at("sdec", [P, 2, PAGES, NS, 4], X_AT + AR + 4096)
        kd = [at(f"kd{n}", [P, PAGES, GW], X_AT + (2 + n) * AR) for n in range(2)]
        vd = [at(f"vd{n}", [P, PAGES, GW], o) for n, o in enumerate(
            [whi_at[0], whi_at[2], wlo_at[0], wlo_at[2], F_AT, F_AT + AR, A_AT + 6 * AR, A_AT + 5 * AR])]
        kprod = at("kprod", [P, PAGES, GW], A_AT + 7 * AR)
        odec = at("odec", [32, GW], SG_AT + 2048)
        pdec = at("pdec", [32, 2, SEQ], SG_AT + 2048)
        wtz = at("wtz", [P, PAGES, NS * 36], A_AT + 7 * AR)
        prodn = at("prodn", [P, NS, 4], SG_AT + 2048 + 4096 + 512)
        wdiag = at("wdiag", [32, 32], SG_AT + 2048 + 4096 + 512 + 128)
        assert SG_AT + 2048 + 4096 + 512 + 256 <= SG_AT + 4 * T * 4

        row_g = at("row_g", [P, P], A_AT + 5 * AR)
        row_v = at("row_v", [NVEC, P], A_AT + 5 * AR + 512)
        row_s = at("row_s", [P, P], A_AT + 5 * AR + 1024)
        row_l = at("row_l", [P, P], A_AT + 5 * AR + 1536)
        row_tables = [(gcol, row_g), (vcol, row_v), (shcol, row_s), (lrucol, row_l)]

        psum = ctx.enter_context(nc.psum_tensor("psum", [P, 8, 512], F32))
        flat = psum[:, :, :].rearrange("p b n -> p (b n)")

        def bank(b, n=512):
            return psum[:, b, 0:n]

        def halves(b):
            return psum[:, b:b + 2, 0:TH]

        def tok(x):
            return x.rearrange("p (h t) -> p h t", h=2)

        def C(name):
            s, w = CONST[name]
            return cst[:, s:s + w]

        def V(name, j=0):
            s, _ = VEC[name]
            return vcol[:, s + j:s + j + 1]

        ident = C("ident")

        w_in, w_out = I["ffn_w_in"], I["ffn_w_out"]
        PHASES = []

        def ffn_phases(i, a):
            for r in range(2):
                PHASES.append((("in", i, a, r), 32, 16))
                PHASES.append((("out", i, a, r), 16, 8))

        for i in range(2):
            ffn_phases(i, 0)
            PHASES.append((("mix_in", i), 32 if i == 0 else 20, 32 if i == 0 else 20))
            PHASES.append((("mix_out", i), 8, 8))
            ffn_phases(i, 1)
            PHASES.append((("gate", i), 8, 8))
            PHASES.append((("ple", i), 4, 8))
        UB, TB = {}, {}
        ub = tb = 0
        for name, nu, nt in PHASES:
            UB[name], TB[name] = ub, tb
            ub, tb = ub + nu, tb + nt
        NU = ub

        raw_loaded = [sem(f"raw_loaded{s}") for s in range(4)]
        hi_ready, lo_ready, unit_used = sem("hi_ready"), sem("lo_ready"), sem("unit_used")
        psum_free = [sem(f"psum_free{s}") for s in range(2)]
        sg_ready, hid_ready, hhi_ready = sem("sg_ready"), sem("hid_ready"), sem("hhi_ready")
        sq_ready, sq_used, sq_summed = sem("sq_ready"), sem("sq_used"), sem("sq_summed")
        sd_ready, rs_ready, rb_ready = sem("sd_ready"), sem("rs_ready"), sem("rb_ready")
        h_ready, xt_ready, xh_ready, xn_ready = sem("h_ready"), sem("xt_ready"), sem("xh_ready"), sem("xn_ready")

        def free_count(t):
            return t // 2

        NORM = {}
        for i in range(2):
            for k in range(8):
                NORM[(i, k)] = 8 * i + k

        PAIRS = {}
        n = 0
        for name, _, nt in PHASES:
            if name[0] == "in":
                PAIRS[name] = n
                n += nt

        block = ctx.enter_context(nc.Block())

        cen_ready, cen_copied = sem("centred"), sem("centred_copied")
        stat_summed, stat_rooted, stat_ready = sem("stat_summed"), sem("stat_rooted"), sem("stat_ready")
        stat_spread, stat_used = sem("stat_spread"), sem("stat_used")
        cath_ready, cat_ready = sem("cat_hi_ready"), sem("cat_ready")

        def raw_cols(u):
            small_u = isinstance(u, int) and any(UB[("ple", i)] <= u < UB[("ple", i)] + 4 for i in range(2))
            return 512 if small_u else UNIT

        def one(x, m):
            return x[:, m, :] if isinstance(m, int) else x[:, bass.ds(m, 1), :].rearrange("p a t -> p (a t)")

        def one2(x, m):
            if isinstance(m, int):
                return tok(x[:, m, :])
            return x[:, bass.ds(m, 1), :].rearrange("p a (h t) -> p (a h) t", h=2)

        def row128(a):
            return a.rearrange("(k p) -> k p", p=P)

        def vrow(name):
            s, w = VEC[name]
            return row_v[s:s + w, :]

        ROWS = [
            (row_g[:, :], I["norm_g"].rearrange("i n (k p) -> (i n k) p", p=P)),
            (vrow("mu"), I["rwkv_mu"][0].rearrange("m (k p) -> (m k) p", p=P)),
            (vrow("w0"), row128(I["rwkv_w0"][0])), (vrow("a0"), row128(I["rwkv_a0"][0])),
            (vrow("kk"), row128(I["rwkv_kk"][0])), (vrow("ka"), row128(I["rwkv_ka"][0])),
            (vrow("rk"), I["rwkv_rk"][0].rearrange("(k h) d -> k (h d)", h=2)),
            (vrow("ln"), I["rwkv_ln"][0].rearrange("m (k p) -> (m k) p", p=P)),
            (vrow("conv_w"), I["lru_conv_w"][0].rearrange("m (k p) -> (m k) p", p=P)),
            (vrow("conv_b"), row128(I["lru_conv_b"][0])), (vrow("ba"), row128(I["lru_ba"][0])),
            (vrow("bi"), row128(I["lru_bi"][0])), (vrow("lam"), row128(I["lru_lambda"][0])),
            (vrow("subln"), I["diff_subln"]),
            (row_s[:, :], I["state_rwkv_shift"][0, :, 0, :].rearrange("b (k p) -> (b k) p", p=P)),
            (row_l[0:96, :], I["state_lru_conv"][0].rearrange("b t (k p) -> (b t k) p", p=P)),
            (row_l[96:128, :], I["state_lru_h"][0].rearrange("b (k p) -> (b k) p", p=P)),
        ]
        NROWS = len(ROWS)

        lin = I["ab_w_in"][0], I["cd_w_in"][0]
        lout = I["ab_w_out"][0], I["cd_w_out"][0]
        VD_GROUP = [0, 0, 0, 0, 1, 1, 1, 2]
        DC = math.exp(-0.5)

        rec = lambda names: [f"{n}{c}" for c in range(2) for n in names]
        STEPS = {
            "inv.pe": ["at", "a", "m2", "m2t", "m4", "x2", "m8", "x4", "x8", "f", "ft", "f2", "v", "h", "rb", "ak", "w", "kt"],
            "inv.act": ["mt", "vb", "ka", "m2", "e", "m4", "m8", "xt", "f", "x", "f2", "v", "bt", "w", "kt"],
            "inv.dve": ["be", "al", "mt", "m", "mb", "e", "x1", "mv", "m2t", "m4t", "x2", "x4", "xt", "xtb", "ft", "ift",
                        "alu", "rh", "h", "rb", "ak", "rk"],
            "rec.pe": rec(["rhs", "pre", "z", "st", "o", "turn"]),
            "rec.act": rec(["rc", "ob", "out"]),
            "rec.dve": rec(["zc", "u", "ud"]),
        }
        step_sem = {who: sem(who.replace(".", "_")) for who in STEPS}

        def after(eng, who, it, step):
            names = STEPS[who]
            count = it * len(names) + names.index(step) + 1
            if not isinstance(count, int) or count > 0:
                eng.wait_ge(step_sem[who], count)

        def by_chunk(x):
            return x.rearrange("p j (c t) -> p j c t", c=2)

        def diagonal(x, hp):
            return x[hp, :, hp].rearrange("p (c j) t -> p j c t", c=2)

        def pair_cols(it, c, n=CH):
            t0 = it * (2 * CH) + c * CH
            return slice(t0, t0 + n) if isinstance(it, int) else bass.ds(t0, n)

        HP = [slice(0, HD), slice(HD, P)]
        four = lambda x: x.rearrange("p (a b) -> p a b", a=GT)
        eight = lambda x: x.rearrange("p (a b) -> p a b", a=2 * GT)
        two_banks = lambda b, n: flat[:, b * 512:(b + 2) * 512].rearrange("p (a s b) -> p a s b", a=2 * GT, s=2)[:, :, n, :]

        @block.sync
        def _(sp):
            def load(u, r, src, width=P, nk=KT):
                if not isinstance(u, int) or u >= 4:
                    sp.wait_ge(lo_ready, u - 3)
                s = r % 4
                dst = raw[s][:, 0:nk * width].rearrange("p (k c) -> p k c", k=nk)
                sp.dma_start(dst, src.rearrange("(k p) c -> p k c", p=P)).then_inc(raw_loaded[s], 16)

            def ffn(i, a):
                win, wout = w_in[i, a, :, :], w_out[i, a, :, :]
                for r in range(2):
                    u0 = UB[("in", i, a, r)]
                    first = 1 if u0 == 0 else 0
                    c0 = r * 16 * P
                    for p in range(2 * first):
                        load(2 * p, 2 * p, win[:, c0 + p * P:c0 + (p + 1) * P])
                        load(2 * p + 1, 2 * p + 1, win[:, 4096 + c0 + p * P:4096 + c0 + (p + 1) * P])
                    with sp.Fori(first, 8) as it:
                        for p in range(2):
                            col = it * (2 * P) + (c0 + p * P)
                            load(it * 4 + (u0 + 2 * p), 2 * p, win[:, bass.ds(col, P)])
                            load(it * 4 + (u0 + 2 * p + 1), 2 * p + 1, win[:, bass.ds(col + 4096, P)])
                    u0 = UB[("out", i, a, r)]
                    with sp.Fori(0, 4) as it:
                        for m in range(2):
                            for g in range(2):
                                row = (r * 2 + g) * D
                                load(it * 4 + (u0 + 2 * m + g), 2 * m + g,
                                     wout[row:row + D, bass.ds(it * (2 * P) + m * P, P)])

            def proj(name, w):
                u0, nt = UB[name], w.shape[1] // P
                with sp.Fori(0, nt // 4) as it:
                    for m in range(4):
                        load(it * 4 + (u0 + m), m, w[:, bass.ds(it * (4 * P) + m * P, P)])

            def page_stream():
                sp.wait_ge(sem("lam_pages_loaded"), 32)
                for s in range(2):
                    sp.wait_ge(psum_free[s], TB[("mix_in", 1)] // 2 + 10)

                def pages_of(cache, dst, b, signal):
                    for x in range(PAGES):
                        page = sp.value_load(pages[0:1, b * PAGES + x:b * PAGES + x + 1], min_val=0, max_val=cache.shape[1] - 1)
                        sp.dma_start(dst[:, x, :], cache[0, bass.ds(page, 1), :, :, :].rearrange("o p h d -> p (o h d)")).then_inc(signal, 16)

                def values(b):
                    pages_of(I["cache_v"], vd[b], b, sem(f"vd_loaded{VD_GROUP[b]}"))

                def keys(b):
                    pages_of(I["cache_k"], kd[b % 2], b, sem(f"kd_loaded{b % 2}"))

                for b in range(4):
                    values(b)
                sp.wait_ge(sem("lru_done"), 1)
                keys(0)
                keys(1)
                values(4)
                values(5)
                sp.wait_ge(sem("kv_y_stored"), 64)
                values(6)
                sp.wait_ge(sem("oc_copied"), 16)
                values(7)
                for b in range(2, NS):
                    sp.wait_ge(sem("qb_used"), b - 1)
                    keys(b)

            for dst, src in ROWS[:10]:
                sp.dma_start(dst, src).then_inc(sem("x_loaded"), 16)
            for i in range(2):
                ffn(i, 0)
                proj(("mix_in", i), lin[i])
                if i == 1:
                    page_stream()
                proj(("mix_out", i), lout[i])
                ffn(i, 1)
                proj(("gate", i), I["ple_gate_w"][i])
                for e in range(4):
                    load(UB[("ple", i)] + e, e, I["ple_w"][i][:, e * 256:(e + 1) * 256], 256, 2)

        NT = {name: nt for name, _, nt in PHASES}

        @block.tensor
        def _(pe):
            mm = nc.tensor.matmul

            def turn(out, in_):
                return nc.tensor.transpose(out, in_, ident[0:in_.shape[0], 0:in_.shape[0]])

            def unit(u, r, out, xh, xl, nk=KT, start=True, stop=True, width=P, c0=0, k0=0, last=True, paced=None):
                pe.wait_ge(lo_ready, u + 1)
                s = r % 4
                hi = whi[s][:, 0:nk * width].rearrange("p (k c) -> p k c", k=nk)
                lo = wlo[s][:, 0:nk * width].rearrange("p (k c) -> p k c", k=nk)
                for k in range(nk):
                    if paced is not None:
                        pe.wait_ge(xn_ready, paced + k + 1)
                    for e in range(2):
                        for n, (w, x) in enumerate(((hi, xh), (hi, xl), (lo, xh))):
                            ins = mm(out[:, e, :], w[:, k, c0:c0 + P], x[:, k0 + k, e * TH:(e + 1) * TH],
                                     start=start and k == 0 and n == 0, stop=stop and k == nk - 1 and n == 2)
                if last:
                    ins.then_inc(unit_used, 1)

            def free(s, count):
                if not isinstance(count, int) or count > 0:
                    pe.wait_ge(psum_free[s], count)

            def ffn(i, a):
                nx = 8 * (NORM[(i, 0 if a == 0 else 4)] // 2)
                for r in range(2):
                    name = ("in", i, a, r)
                    u0, t0 = UB[name], TB[name] // 2

                    def body(it, lead):
                        for p in range(2):
                            free(p, it + t0)
                            for g in range(2):
                                if lead and p == 0 and g == 1:
                                    pe.wait_ge(xn_ready, nx + 8)
                                unit(it * 4 + (u0 + 2 * p + g), 2 * p + g, halves(4 * p + 2 * g), xhi, xlo,
                                     paced=nx if lead and p == 0 and g == 0 else None)

                    if r == 0:
                        body(0, True)
                    with pe.Fori(1 - r, 8) as it:
                        body(it, False)
                    name = ("out", i, a, r)
                    uo, to = UB[name], TB[name] // 2

                    def obody(it, lead):
                        for m in range(2):
                            if lead and m == 0:
                                pe.wait_ge(psum_free[1], to - 4)
                                pe.wait_ge(psum_free[0], to)
                            else:
                                free(m, it + to)
                            unit(it * 4 + (uo + 2 * m), 2 * m, halves(4 * m), ghi, glo, stop=False)
                            if lead and m == 0:
                                pe.wait_ge(psum_free[1], to)
                            unit(it * 4 + (uo + 2 * m + 1), 2 * m + 1, halves(4 * m), ghi, glo, start=False, k0=KT)

                    obody(0, True)
                    with pe.Fori(1, 4) as it:
                        obody(it, False)

            def proj(name, nx, cat=None):
                u0, t0 = UB[name], TB[name] // 2
                if cat is None:
                    pe.wait_ge(xn_ready, nx)
                else:
                    pe.wait_ge(cat_ready, cat)
                with pe.Fori(0, NT[name] // 4) as it:
                    for m in range(4):
                        free(m % 2, it * 2 + (t0 + m // 2))
                        unit(it * 4 + (u0 + m), m, halves(4 * (m % 2)), xhi, xlo)

            def spread(b, r5, signal):
                heads = r5.shape[2]
                for x in range(5):
                    for g in range(heads):
                        n = P // heads
                        out, r = flat[g * n:(g + 1) * n, b * 512 + x * P:b * 512 + x * P + (P if x < 4 else NS)], r5[:, x, g:g + 1].to_broadcast([P, n])
                        last = mm(out, r, ident if x < 4 else ident[:, P - NS:P], start=True, stop=True)
                last.then_inc(signal, 1)

            def norm(n):
                pe.wait_ge(sq_used, (KT - 1) * (n + 1))
                for x, t0 in enumerate(TOK_TILES):
                    last = mm(psum[:, 7, x:x + 1], sgt[:, 0, t0:t0 + P], C("ones2")[:, 0:1], start=(x == 0), stop=True, skip_group_check=True)
                last.then_inc(sq_summed, 1)
                pe.wait_ge(rs_ready, n + 1)
                spread(2, rs5b.rearrange("p (x o) -> p x o", o=1), rb_ready)

            def centre(g, src):
                for j in range(GT):
                    if 4 * g + j >= 2:
                        pe.wait_ge(cen_copied, 2 * (4 * g + j - 1))
                    for e in range(2):
                        last = mm(halves(4 * (j % 2))[:, e, :], C("center"), src[:, j, e * TH:(e + 1) * TH], start=True, stop=True)
                    last.then_inc(cen_ready, 1)

            def even_mix():
                q, k, v = A[0], A[1], A[2]
                for s in range(2):
                    pe.wait_ge(psum_free[s], TB[("mix_in", 0)] // 2 + 16)
                for n in range(16):
                    last = turn(psum[0:9, n // 4, (n % 4) * P:(n % 4 + 1) * P], u[:, 16 + n, SEQ - 1:T])
                last.then_inc(sem("shift_turned"), 1)
                pe.wait_ge(sem("shift_copied"), 4)
                for n in range(8):
                    if n >= 2:
                        pe.wait_ge(sem("rot_used"), n - 1)
                    for e in range(2):
                        last = mm(halves(4 * (n % 2))[:, e, :], C("rot"), A[n // 4][:, n % 4, e * TH:(e + 1) * TH], start=True, stop=True)
                    last.then_inc(sem("rot_ready"), 1)
                pe.wait_ge(sem("qk_ready"), 8)
                for i in range(4):
                    ts = slice(i * P, (i + 1) * P)
                    if i:
                        pe.wait_ge(sem("tk_copied"), 2 * i)
                    for j in range(GT):
                        turn(bank(0)[:, j * P:(j + 1) * P], k[:, j, ts])
                        last = turn(bank(1)[:, j * P:(j + 1) * P], v[:, j, ts])
                    last.then_inc(sem("tk_turned"), 1)
                    if i:
                        pe.wait_ge(sem("att_ready"), 2 * i)
                    for hh in range(2):
                        hp = slice(hh * HD, (hh + 1) * HD)
                        for j in range(GT):
                            last = mm(bank(2 + hh)[:, j * P:(j + 1) * P], k[hp, j, ts], q[hp, j, ts], start=True, stop=True)
                    last.then_inc(sem("sc_ready"), 1)
                    pe.wait_ge(sem("tk_copied"), 2 * (i + 1))
                    pe.wait_ge(sem("att_ready"), 2 * (i + 1))
                    pe.wait_ge(sem("ubd_ready"), i + 1)
                    if i:
                        pe.wait_ge(sem("o_copied"), i)
                    for j in range(GT):
                        js = slice(j * P, (j + 1) * P)
                        mm(bank(4)[:, js], ubd[:, j, :], q[:, j, ts], start=True, stop=False, skip_group_check=True)
                        for hh in range(2):
                            hp = slice(hh * HD, (hh + 1) * HD)
                            mm(bank(4)[hp, js], vtok[:, j, hp], att[:, hh, j, :], start=False, stop=True, skip_group_check=True)
                    for j in range(GT):
                        last = mm(bank(5)[:, j * P:(j + 1) * P], ktok[:, j, :], vtok[:, j, :], start=True, stop=True)
                    last.then_inc(sem("pv_done"), 1)
                for j in range(GT):
                    last = turn(psum[0:NS, 6, j * P:(j + 1) * P], v[:, j, SEQ:T])
                last.then_inc(sem("vs_turned"), 1)
                pe.wait_ge(sem("vs8_ready"), 1)
                for j in range(GT):
                    if j >= 2:
                        pe.wait_ge(sem("vb_used"), j - 1)
                    for hh in range(2):
                        for b in range(NS):
                            last = mm(psum[hh * HD:(hh + 1) * HD, j % 2, b * HD:(b + 1) * HD], ident[0:NS, b:b + 1].to_broadcast([NS, HD]),
                                      vs8[:, (2 * j + hh) * HD:(2 * j + hh + 1) * HD], start=True, stop=True)
                    last.then_inc(sem("vb_ready"), 1)
                for j in range(GT):
                    pe.wait_ge(sem("sret_ready"), j + 1)
                    for hh in range(2):
                        hp = slice(hh * HD, (hh + 1) * HD)
                        for b in range(NS):
                            last = mm(psum[hp, 2 + hh, j * NS + b:j * NS + b + 1], s_ret[hp, j, b, :], q[hp, j, SEQ + b:SEQ + b + 1], start=True, stop=True)
                last.then_inc(sem("os_ready"), 1)
                pe.wait_ge(sem("o_copied"), 6)
                centre(0, A[0])
                head_stat0(0)
                pe.wait_ge(sem("lora_loaded"), 96)
                pe.wait_ge(sem("z_ready"), 12)
                pe.wait_ge(stat_used, 4)
                for n, (w, x, b, m) in enumerate(((lw1, FA[1], 0, HD), (la1, X[3], 2, HD), (lg1, A[1], 4, P))):
                    for e in range(2):
                        for j in range(GT):
                            last = mm(halves(b)[0:m, e, :], w[:, j, :], x[:, j, e * TH:(e + 1) * TH], start=(j == 0), stop=(j == GT - 1))
                    last.then_inc(sem("l1_ready"), 1)
                for n in range(12):
                    w, x = ((lw2, tw), (la2, ta), (lg2, tg))[n // 4]
                    if n % 4 == 0:
                        pe.wait_ge(sem("l1_copied"), 3)
                    if n >= 2:
                        pe.wait_ge(sem("l2_copied"), n - 1)
                    j = n % 4
                    for e in range(2):
                        last = mm(halves(4 * (n % 2))[:, e, :], w[:, j * P:(j + 1) * P], x[:, e * TH:(e + 1) * TH], start=True, stop=True)
                    last.then_inc(sem("l2_ready"), 1)
                pe.wait_ge(sem("l2_copied"), 12)
                pe.wait_ge(sem("kk_sq"), 4)
                stat_body(1, X[3], C("bsel"))
                pe.wait_ge(sem("rw_ready"), 1)
                for n, x in enumerate((FA[0], A[5], FA[1], X[1], X[0])):
                    for j in range(GT):
                        last = turn(psum[0:NS, n, j * P:(j + 1) * P], x[:, j, SEQ:T])
                last.then_inc(sem("rw_turned"), 1)
                pe.wait_ge(sem("rows8_ready"), 5)
                for n in range(20):
                    j, x = n // 5, n % 5
                    if n >= 6:
                        pe.wait_ge(sem("bc_used"), n - 5)
                    for hh in range(2):
                        for b in range(NS):
                            last = mm(psum[hh * HD:(hh + 1) * HD, n % 6, b * HD:(b + 1) * HD], ident[0:NS, b:b + 1].to_broadcast([NS, HD]),
                                      rows8[x][:, (2 * j + hh) * HD:(2 * j + hh + 1) * HD], start=True, stop=True)
                    last.then_inc(sem("bc_ready"), 1)
                pe.wait_ge(sem("bc_used"), 20)
                stack = C("stack")

                def prod(b, lhs, rhs, who, step, groups=range(2 * GT), more=None, first=True, w=HD):
                    terms = [(lhs, rhs)] + (more or [])
                    for n, g in enumerate(groups):
                        for x, (l, r) in enumerate(terms):
                            last = mm(flat[:, b * 512 + n * w:b * 512 + (n + 1) * w], l[:, g, :], r(g), start=first and (n * w) % 512 == 0 and x == 0,
                                      stop=(x == len(terms) - 1), skip_group_check=True)
                    if step:
                        last.then_inc(step_sem[who], 1)

                def of(x):
                    return (lambda g: x[:, g, :]) if len(x.shape) == 3 else (lambda g: x)

                def chunks(it, q):
                    col = lambda x: (lambda g: x[:, g % GT, pair_cols(it, g // GT)])

                    def inv(b, lhs, rhs, step, w=HD):
                        if it is not None:
                            prod(b, lhs, rhs, "inv.pe", step, w=w)

                    def two(x, n=0):
                        return lambda g: x[:, n:n + 2, g, :]

                    def need(who, step, back=0):
                        if it is not None and not (back and isinstance(it, int) and it == 0):
                            after(pe, who, it - back, step)

                    def head(c):
                        if q is None:
                            return
                        if c == 0:
                            for who, step in (("inv.dve", "rh"), ("inv.dve", "ak"), ("inv.dve", "rk"), ("inv.act", "kt")):
                                after(pe, who, q, step)
                            if isinstance(q, int) and q == 0:
                                pe.wait_ge(sem("state_zeroed"), 1)
                            else:
                                after(pe, "rec.dve", q - 1, "ud1")
                                after(pe, "rec.act", q - 1, "out1")
                        else:
                            after(pe, "rec.dve", q, "ud0")
                            after(pe, "rec.act", q, "out0")
                        gs = range(4 * c, 4 * c + 4)
                        state = lambda g: uc[:, g % GT, :]
                        prod(4, bd["alu"], state, "rec.pe", f"rhs{c}", gs, [(bd["akt"], of(cm["vc"]))])
                        prod(6, bd["rh"], state, "rec.pe", None, gs, [(bd["rkt"], of(cm["vc"]))])
                        prod(7, bd["kt"], of(cm["vc"]), "rec.pe", f"pre{c}", gs)

                    def solve(c):
                        if q is None:
                            return
                        after(pe, "inv.act", q, "w")
                        after(pe, "rec.act", q, f"rc{c}")
                        prod(5, bd["wt"], lambda g: rc[:, g % GT, :], "rec.pe", f"z{c}", range(4 * c, 4 * c + 4))

                    def tail(c):
                        if q is None:
                            return
                        after(pe, "inv.dve", q, "rb")
                        after(pe, "rec.dve", q, f"zc{c}")
                        gs, z = range(4 * c, 4 * c + 4), lambda g: zc[:, g % GT, :]
                        prod(7, bd["bt"], z, "rec.pe", f"st{c}", gs, first=False)
                        prod(6, bd["rbt"], z, "rec.pe", f"o{c}", gs, first=False)

                    def out(c):
                        if q is None:
                            return
                        after(pe, "rec.act", q, f"ob{c}")
                        prod(6, ob, of(stack), "rec.pe", f"turn{c}", range(GT))

                    need("inv.dve", "be")
                    need("inv.dve", "rk", 1)
                    inv(1, bd["be"], it is not None and col(FA[0]), "at")
                    need("inv.dve", "al")
                    inv(0, bd["al"], it is not None and col(FA[1]), "a")
                    head(0)
                    need("inv.act", "mt")
                    need("inv.dve", "m")
                    need("inv.act", "w", 1)
                    inv(2, bd["mt"], of(cm["m"]), "m2")
                    need("inv.dve", "mb")
                    need("inv.act", "kt", 1)
                    inv(3, bd["m"], of(cm["mt"]), "m2t")
                    solve(0)
                    need("inv.act", "m2")
                    need("inv.dve", "m2t")
                    inv(0, bd["m2t"], of(cm["m2"]), "m4")
                    inv(2, bd["m2"], two(mx), "x2", P)
                    tail(0)
                    need("inv.act", "m4")
                    need("inv.dve", "m4t")
                    inv(1, bd["mt"], of(cm["m"]), "m8")
                    need("inv.dve", "x2")
                    inv(0, bd["m"], of(cm["mt"]), "x4")
                    out(0)
                    need("inv.act", "m8")
                    need("inv.dve", "x4")
                    inv(2, bd["m2"], of(cm["x1"]), "x8")
                    head(1)
                    need("inv.act", "xt")
                    need("inv.dve", "xtb")
                    need("inv.act", "e")
                    inv(0, bd["m2t"], two(mv, 2), "f", P)
                    inv(3, bd["e"], of(cm["m2"]), "ft")
                    solve(1)
                    need("inv.act", "f")
                    need("inv.dve", "ft")
                    inv(2, bd["m"], of(cm["m2t"]), "f2")
                    tail(1)
                    need("inv.act", "vb")
                    need("inv.act", "x")
                    inv(0, bd["al"], of(stack), "v")
                    need("inv.act", "f2")
                    need("inv.dve", "ift")
                    inv(1, bd["m2"], of(cm["m"]), "h")
                    out(1)
                    need("inv.dve", "mv")
                    inv(2, bd["be"], two(mv, 1), "rb", P)
                    need("inv.act", "ka")
                    need("inv.act", "v")
                    need("inv.dve", "h")
                    inv(0, bd["ka"], two(mv, 0), "ak", P)
                    need("inv.dve", "rb")
                    need("inv.act", "bt")
                    inv(2, bd["mt"], of(cm["mt"]), "w")
                    inv(3, bd["ka"], of(stack), "kt")

                pe.wait_ge(sem("products_ready"), 6)
                chunks(0, None)
                with pe.Fori(1, NCH // 2) as it:
                    chunks(it, it - 1)
                chunks(None, NCH // 2 - 1)
                after(pe, "rec.dve", NCH // 2 - 1, "ud1")
                after(pe, "rec.act", NCH // 2 - 1, "out1")
                for j in range(GT):
                    last = turn(psum[0:HD, 6, j * P:(j + 1) * P], uc[:, j, :])
                last.then_inc(sem("state_turned"), 1)
                centre(1, X[3])
                head_stat0(2)
                pe.wait_ge(sem("rkk_ready"), 1)
                for j in range(GT):
                    pe.wait_ge(stat_used, 12)
                    if j >= 2:
                        pe.wait_ge(sem("bonus_used"), j - 1)
                    for e in range(2):
                        last = mm(halves(4 * (j % 2))[:, e, :], C("bones"), A[2][:, j, e * TH:(e + 1) * TH], start=True, stop=True)
                    last.then_inc(sem("bonus_ready"), 1)

            def head_stat0(g):
                pe.wait_ge(cen_copied, 8 * (g // 2 + 1))
                stat_body(g, X[1] if g == 0 else FA[1], C("hsel"))

            def stat_body(g, src, sel):
                w = sel.shape[1]
                for j in range(GT):
                    for x, t0 in enumerate(TOK_TILES):
                        last = mm(psum[:, 7, (x * GT + j) * w:(x * GT + j + 1) * w], src[:, j, t0:t0 + P], sel,
                                  start=(j == 0 and x == 0), stop=(j == GT - 1), skip_group_check=True)
                last.then_inc(stat_summed, 1)
                pe.wait_ge(stat_ready, g + 1)
                r = st_rs[:, 0:20 * w].rearrange("p (x j s) -> p x j s", j=GT, s=w)
                for j in range(GT):
                    if 4 * g + j >= 2:
                        pe.wait_ge(stat_used, 4 * g + j - 1)
                    spread(4 * (j % 2), r[:, :, j, :], stat_spread)

            def odd_mix():
                q, k, v = A[0], A[1], A[2]
                for s in range(2):
                    pe.wait_ge(psum_free[s], TB[("mix_in", 1)] // 2 + 10)
                for j in range(GT):
                    last = turn(psum[0:11, 6, j * P:(j + 1) * P], A[3][:, j, SEQ - 3:T])
                last.then_inc(sem("lconv_turned"), 1)
                pe.wait_ge(sem("lruw_loaded"), 16 * 4)
                pe.wait_ge(sem("xc_ready"), 1)
                for n in range(8):
                    if n >= 2:
                        pe.wait_ge(sem("gates_copied"), n - 1)
                    for e in range(2):
                        last = mm(halves(4 * (n % 2))[:, e, :], (wabd, wibd)[n // 4][:, n % 4, :], X[0][:, n % 4, e * TH:(e + 1) * TH], start=True, stop=True)
                    last.then_inc(sem("gates_ready"), 1)
                pe.wait_ge(sem("gates_copied"), 8)
                for x in range(5):
                    w = P if x < 4 else NS
                    if x >= 2:
                        pe.wait_ge(sem("kv_copied"), 2 * (x - 1))
                    for n, a in enumerate((v, k)):
                        for j in range(GT):
                            last = turn(psum[0:w, 2 * (x % 2) + n, j * P:(j + 1) * P], a[:, j, x * P:x * P + w])
                    last.then_inc(sem("kv_turned"), 1)
                for j in range(GT):
                    last = turn(psum[0:NS, 4, j * P:(j + 1) * P], q[:, j, SEQ:T])
                last.then_inc(sem("qs_turned"), 1)
                pe.wait_ge(sem("lruh_ready"), 1)
                for j in range(GT):
                    last = turn(psum[0:9, 5, j * P:(j + 1) * P], FA[0][:, j, SEQ - 1:T])
                last.then_inc(sem("lruh_turned"), 1)
                pe.wait_ge(sem("qs_copied"), 1)
                pe.wait_ge(sem("lruh_copied"), 1)
                pe.wait_ge(sem("kv_copied"), 10)

                def scores(n):
                    i, j = n // 4, n % 4
                    if n >= 2:
                        pe.wait_ge(sem("exp_done"), 2 * (n - 1))
                    for m in range(2):
                        hp = slice(m * HD, (m + 1) * HD)
                        last = mm(psum[:, 2 * (n % 2) + m, 0:(i + 1) * P], q[hp, j, i * P:(i + 1) * P], k[hp, j, 0:(i + 1) * P], start=True, stop=True)
                    last.then_inc(sem("qk2_ready"), 1)

                def values(n):
                    i, j = n // 4, n % 4
                    pe.wait_ge(sem("wt_copied"), n + 1)
                    if n >= 2:
                        pe.wait_ge(sem("oc_copied"), n - 1)
                    for x in range(i + 1):
                        last = mm(psum[:, 6 + n % 2, 0:P], vtm[:, x, j * P:(j + 1) * P], wtp[:, n % 2, x * P:(x + 1) * P], start=(x == 0), stop=(x == i))
                    last.then_inc(sem("pv2_done"), 1)

                scores(0)
                scores(1)
                for n in range(16):
                    if n < 14:
                        scores(n + 2)
                    if n >= 1:
                        values(n - 1)
                    pe.wait_ge(sem("w_ready"), n + 1)
                    if n >= 2:
                        pe.wait_ge(sem("wt_copied"), n - 1)
                    for x in range(n // 4 + 1):
                        last = turn(psum[:, 4 + n % 2, x * P:(x + 1) * P], probs[:, n % 2, 0, x * P:(x + 1) * P])
                    last.then_inc(sem("wt_turned"), 1)
                values(15)
                pe.wait_ge(sem("oc_copied"), 16)
                for b in range(NS):
                    if b >= 2:
                        pe.wait_ge(sem("qb_used"), b - 1)
                    mm(bank(b % 2), ident[0:NS, b:b + 1].to_broadcast([NS, P]), qs8[:, :], start=True, stop=True).then_inc(sem("qb_ready"), 1)
                pe.wait_ge(sem("sdec_ready"), NS + 1)
                for m in range(2):
                    for x in range(PAGES):
                        turn(psum[0:32, 2 + m, x * P:(x + 1) * P], sdec[:, m, x, :, :].rearrange("p b h -> p (b h)"))
                mm(psum[0:32, 4, 0:2], prodn[:, :, :].rearrange("p b h -> p (b h)"), C("bsel"), start=True, stop=True).then_inc(sem("sd_turned"), 1)
                pe.wait_ge(sem("wd_ready"), 1)
                for x in range(PAGES):
                    turn(psum[:, 5, x * 32:(x + 1) * 32], pdec[:, 0, x * P:(x + 1) * P])
                mm(psum[:, 6, 0:32], C("ones2")[0:32, 0:1].to_broadcast([32, P]), wdiag[:, :], start=True, stop=True).then_inc(sem("wd_turned"), 1)
                pe.wait_ge(sem("wtd_copied"), 1)
                for b in range(NS):
                    g = VD_GROUP[b]
                    pe.wait_ge(sem(f"vd_loaded{g}"), 64 * VD_GROUP.count(g))
                    for x in range(PAGES):
                        last = mm(psum[0:32, 4, :], wtz[:, x, b * 32:(b + 1) * 32], vd[b][:, x, :], start=(b == 0 and x == 0), stop=(b == NS - 1 and x == PAGES - 1))
                last.then_inc(sem("vd_used"), 1)
                pe.wait_ge(sem("wtd_copied"), 2)
                for j in range(4):
                    last = turn(psum[:, 7, j * 32:(j + 1) * 32], odec[:, j * P:(j + 1) * P])
                last.then_inc(sem("vd_used"), 1)
                pe.wait_ge(sem("oc_sq"), 1)
                stat_body(3, X[1], C("ones2")[:, 0:1])

            pe.wait_ge(sem("inputs_loaded"), 16 * (NROWS - 10))
            pe.wait_ge(sem("x_loaded"), 16 * 16)
            for n, (dst, rows) in enumerate(row_tables):
                last = turn(psum[:, 6, n * P:n * P + rows.shape[0]], rows[:, :])
            last.then_inc(sem("rows_turned"), 1)
            for k in range(KT):
                b = 4 * (k % 2)
                if k >= 2:
                    pe.wait_ge(h_ready, k - 1)
                for x in range(4):
                    turn(psum[:, b, x * P:(x + 1) * P], stage[:, x, k * P:(k + 1) * P])
                turn(psum[:, b + 1, 0:NS], stage_s[:, k * P:(k + 1) * P]).then_inc(sem("xt_turned"), 1)
            for i in range(2):
                norm(NORM[(i, 0)])
                ffn(i, 0)
                norm(NORM[(i, 1)])
                norm(NORM[(i, 2)])
                proj(("mix_in", i), 8 * (NORM[(i, 2)] // 2 + 1))
                (even_mix if i == 0 else odd_mix)()
                proj(("mix_out", i), None, 8 * (i + 1))
                norm(NORM[(i, 3)])
                norm(NORM[(i, 4)])
                ffn(i, 1)
                norm(NORM[(i, 5)])
                norm(NORM[(i, 6)])
                proj(("gate", i), 8 * (NORM[(i, 6)] // 2 + 1))
                pe.wait_ge(psum_free[1], TB[("ple", i)] // 2)
                pe.wait_ge(psum_free[0], TB[("ple", i)] // 2)
                pe.wait_ge(sem("p_loaded"), 32 * (i + 1))
                for k in range(2):
                    for x in range(4):
                        turn(psum[:, 2 + 4 * k, x * P:(x + 1) * P], pst[:, x, k * P:(k + 1) * P])
                    last = turn(psum[:, 3 + 4 * k, 0:NS], pss[:, k * P:(k + 1) * P])
                last.then_inc(sem("p_turned"), 1)
                pe.wait_ge(sem("plo_ready"), 2 * (i + 1))
                for e in range(4):
                    for m in range(2):
                        free(m, TB[("ple", i)] // 2 + e)
                        unit(UB[("ple", i)] + e, e, halves(4 * m), phi, plo, nk=2, width=256, c0=m * P, last=(m == 1))
                norm(NORM[(i, 7)])
            pe.wait_ge(h_ready, 8 * 9)
            for x in range(5):
                w = P if x < 4 else NS
                if x >= 2:
                    pe.wait_ge(sem("y_copied"), x - 1)
                for k in range(KT):
                    last = turn(psum[0:w, 4 * (x % 2) + k // 4, (k % 4) * P:(k % 4 + 1) * P], h[:, k, x * P:x * P + w])
                last.then_inc(sem("y_turned"), 1)

        @block.scalar
        def _(act):
            own = Steps(act, sem("act_steps"))
            fn = nc.scalar.activation

            def ahead(u, r, lead=3):
                u, r = u + lead, r + lead
                if isinstance(u, int) and u >= NU:
                    return
                s = r % 4
                act.wait_ge(raw_loaded[s], 16 * (u // 4 + 1) if isinstance(u, int) else (u - s) * 4 + 16)
                if not isinstance(u, int) or u >= 4:
                    act.wait_ge(unit_used, u - 3)
                fn(whi[s][:, 0:raw_cols(u)], raw[s][:, 0:raw_cols(u)], ACT.Copy).then_inc(hi_ready, 1)

            def ffn(i, a):
                for r in range(2):
                    name = ("in", i, a, r)
                    u0, p0 = UB[name], PAIRS[name]

                    def body(it):
                        for p in range(2):
                            for g in range(2):
                                ahead(it * 4 + (u0 + 2 * p + g), 2 * p + g)
                            pr = it * 2 + (p0 + p)
                            act.wait_ge(unit_used, it * 4 + (u0 + 2 * p + 2))
                            if not isinstance(pr, int) or pr >= 2:
                                act.wait_ge(hid_ready, pr - 1)
                            fn(tok(sgt[:, p, :]), halves(4 * p), ACT.Silu).then_inc(sg_ready, 1)
                            act.wait_ge(hid_ready, pr + 1)
                            fn(one(ghi, it * 2 + p), sgt[:, 2 + p, :], ACT.Copy).then_inc(hhi_ready, 1)

                    if u0 == 0:
                        body(0)
                    with act.Fori(1 if u0 == 0 else 0, 8) as it:
                        body(it)
                    uo = UB[("out", i, a, r)]
                    with act.Fori(0, 4) as it:
                        for m in range(4):
                            ahead(it * 4 + (uo + m), m)

            def norm(n, src, ready, pre):
                for k in range(KT):
                    ready(k)
                    if k >= 3:
                        act.wait_ge(sq_used, (KT - 1) * n + k - 2)
                    fn(sq[:, k % 2, :] if k else sgt[:, 0, :], src[:, k, :], ACT.Square).then_inc(sq_ready, 1)
                act.wait_ge(sq_summed, n + 1)
                fn(rs5, psum[:, 7, 0:5], ACT.Sqrt, scale=1.0 / D, bias=eps_col).then_inc(sd_ready, 1)
                if pre:
                    for k in range(KT):
                        act.wait_ge(xt_ready, 8 * (n // 2) + k + 1)
                        fn(xhi[:, k, :], sgt[:, 2 + k % 2, :], ACT.Copy).then_inc(xh_ready, 1)

            def pre(n):
                norm(n, h, lambda k: act.wait_ge(h_ready, 8 * (n // 2) + k + 1), True)

            def post(n, name):
                norm(n, f, lambda k: act.wait_ge(psum_free[k % 2], TB[name] // 2 + k // 2 + 1), False)

            def stat_root(g, n, scale, eps):
                act.wait_ge(stat_summed, g + 1)
                fn(st_sd[:, 0:n], psum[:, 7, 0:n], ACT.Sqrt, scale=scale, bias=eps).then_inc(stat_rooted, 1)

            def centred(g, xc, xs):
                for j in range(GT):
                    act.wait_ge(cen_ready, 4 * g + j + 1)
                    fn(tok(xc[:, j, :]), halves(4 * (j % 2)), ACT.Copy).then_inc(cen_copied, 1)
                    fn(tok(xs[:, j, :]), halves(4 * (j % 2)), ACT.Square).then_inc(cen_copied, 1)

            def cat(i, parts):
                for k in range(KT):
                    fn(xhi[:, k, :], parts[k // 4][:, k % 4, :], ACT.Copy).then_inc(cath_ready, 1)

            def even_mix():
                act.wait_ge(sem("shift_turned"), 1)
                for n in range(4):
                    fn(shst[:, 4 * n:4 * n + 4, :].rearrange("p a b -> p (a b)"), psum[0:9, n, :], ACT.Copy).then_inc(sem("shift_copied"), 1)
                for i in range(4):
                    act.wait_ge(sem("tk_turned"), i + 1)
                    if i:
                        act.wait_ge(sem("pv_done"), i)
                    for n, x in enumerate((ktok, vtok)):
                        fn(x[:, :, :].rearrange("p a b -> p (a b)"), bank(n), ACT.Copy).then_inc(sem("tk_copied"), 1)
                    act.wait_ge(sem("pv_done"), i + 1)
                    fn(A[0][:, :, i * P:(i + 1) * P], psum[:, 4, :].rearrange("p (a b) -> p a b", a=GT), ACT.Copy).then_inc(sem("o_copied"), 1)
                act.wait_ge(sem("vs_turned"), 1)
                fn(vs8[:, :], psum[0:NS, 6, :], ACT.Copy).then_inc(sem("vs8_ready"), 1)
                act.wait_ge(sem("os_ready"), 1)
                for hh in range(2):
                    hp = slice(hh * HD, (hh + 1) * HD)
                    fn(A[0][hp, :, SEQ:T], psum[hp, 2 + hh, 0:GT * NS].rearrange("p (a b) -> p a b", a=GT), ACT.Copy).then_inc(sem("o_copied"), 1)
                act.wait_ge(sem("rows_stored"), 48)
                centred(0, X[0], X[1])
                stat_root(0, 40, 1.0, eps_col)
                fn(A[3][:, :, :], A[3][:, :, :], ACT.Silu).then_inc(sem("silu_ready"), 1)
                act.wait_ge(sem("l1_ready"), 1)
                fn(tok(tw[:, :]), halves(0)[0:HD], ACT.Tanh).then_inc(sem("l1_copied"), 1)
                act.wait_ge(sem("l1_ready"), 2)
                fn(tok(ta[:, :]), halves(2)[0:HD], ACT.Copy).then_inc(sem("l1_copied"), 1)
                act.wait_ge(sem("l1_ready"), 3)
                fn(tok(tg[:, :]), halves(4), ACT.Sigmoid).then_inc(sem("l1_copied"), 1)
                act.wait_ge(sem("rkv_ready"), 3)
                for n in range(12):
                    j, kind = n % 4, n // 4
                    act.wait_ge(sem("l2_ready"), n + 1)
                    src = halves(4 * (n % 2))
                    if kind == 0:
                        ins = fn(tok(A[2][:, j, :]), src, ACT.Sigmoid, bias=V("w0", j))
                    elif kind == 1:
                        ins = fn(tok(FA[1][:, j, :]), src, ACT.Sigmoid, bias=V("a0", j))
                    else:
                        ins = fn(tok(A[7][:, j, :]), src, ACT.Copy)
                    ins.then_inc(sem("l2_copied"), 1)
                for j in range(GT):
                    act.wait_ge(sem("kk_raw"), j + 1)
                    fn(X[3][:, j, :], FA[0][:, j, :], ACT.Square).then_inc(sem("kk_sq"), 1)
                act.wait_ge(sem("kk_clamped"), 1)
                fn(st_sd[:, 0:40], st_in[:, 0:40], ACT.Sqrt).then_inc(stat_rooted, 1)
                act.wait_ge(sem("cs_ready"), 1)
                fn(A[3][:, :, :], A[5][:, :, :], ACT.Exp, scale=DC).then_inc(sem("dec_ready"), 1)
                fn(A[2][:, :, :], A[2][:, :, :], ACT.Exp, scale=-DC).then_inc(sem("dec_ready"), 1)
                act.wait_ge(sem("dec_ready"), 2)
                fn(A[5][:, :, :], A[5][:, :, :], ACT.Exp, scale=-DC).then_inc(sem("dec_ready"), 1)
                act.wait_ge(sem("rw_turned"), 1)
                for n in range(5):
                    fn(rows8[n][:, :], psum[0:NS, n, :], ACT.Copy).then_inc(sem("rows8_ready"), 1)

                def chunks(it, q):
                    def need(step):
                        if it is not None:
                            after(act, "inv.pe", it, step)

                    def copy(step, src, side=None, diag=None, scale=1.0):
                        if it is None:
                            return
                        if step:
                            need(step)
                        src = eight(bank(src)) if isinstance(src, int) else src
                        if side is not None:
                            ins = fn(side, src, ACT.Copy, scale=scale)
                        for hp in HP if diag is not None else ():
                            ins = fn(diag[hp, :, hp], src[hp], ACT.Copy, scale=scale)
                        ins.then_inc(step_sem["inv.act"], 1)

                    def right(c):
                        if q is not None:
                            after(act, "rec.pe", q, f"rhs{c}")
                            fn(rc[:, :, :], four(bank(4, 256)), ACT.Copy).then_inc(step_sem["rec.act"], 1)

                    def outputs(c):
                        if q is not None:
                            after(act, "rec.pe", q, f"o{c}")
                            for hp in HP:
                                ins = fn(ob[hp, :, hp], four(bank(6, 256))[hp], ACT.Copy)
                            ins.then_inc(step_sem["rec.act"], 1)

                    def channels(c):
                        if q is not None:
                            after(act, "rec.pe", q, f"turn{c}")
                            fn(X[3][:, :, pair_cols(q, c)], four(bank(6, 256)), ACT.Copy).then_inc(step_sem["rec.act"], 1)

                    if it is not None:
                        after(act, "inv.dve", it, "mt")
                        for hp in HP:
                            ins = fn(bd["mt"][hp, :, hp], cm["mt"][hp, :, :], ACT.Copy)
                        ins.then_inc(step_sem["inv.act"], 1)
                    right(0)
                    if it is not None:
                        after(act, "inv.pe", it, "a")
                        for x, src in (("al", X[2]), ("ka", X[1])):
                            for hp in HP:
                                ins = fn(diagonal(bd[x], hp), by_chunk(src[hp, :, pair_cols(it, 0, 2 * CH)]), ACT.Copy)
                            ins.then_inc(step_sem["inv.act"], 1)
                    copy("m2", 2, cm["m2"][:, :, :], bd["m2"])
                    if it is not None:
                        after(act, "inv.dve", it, "e")
                        for hp in HP:
                            ins = fn(bd["e"][hp, :, hp], cm["e"][hp], ACT.Copy)
                        ins.then_inc(step_sem["inv.act"], 1)
                        after(act, "inv.pe", it, "m2t")
                    copy("m4", 0, cm["m"][:, :, :], bd["m"])
                    outputs(0)
                    if it is not None:
                        after(act, "inv.pe", it, "x2")
                    copy("m8", 1, None, bd["m2"])
                    channels(0)
                    right(1)
                    if it is not None:
                        after(act, "inv.dve", it, "xt")
                        fn(bd["m2t"][HP[0], :, HP[0]], cm["m2"][HP[0], :, :], ACT.Copy).then_inc(step_sem["inv.act"], 1)
                    copy("f", two_banks(0, 1), cm["m2t"])
                    copy(None, two_banks(0, 0), None, bd["mt"])
                    copy("f2", 2, None, bd["m2"])
                    outputs(1)
                    copy("v", 0, cm["vc"][:, :, :])
                    channels(1)
                    if it is not None:
                        after(act, "inv.dve", it, "rb")
                    copy(None, two_banks(2, 1), None, bd["bt"])
                    copy("w", 2, None, bd["wt"], -1.0)
                    copy("kt", 3, None, bd["kt"])

                chunks(0, None)
                with act.Fori(1, NCH // 2) as it:
                    chunks(it, it - 1)
                chunks(None, NCH // 2 - 1)
                for r in range(3):
                    ahead(UB[("mix_out", 0)] + r, r, 0)
                act.wait_ge(sem("state_turned"), 1)
                fn(rwst[:, :, :].rearrange("p a b -> p (a b)"), psum[0:HD, 6, :], ACT.Copy).then_inc(sem("rwst_ready"), 1)
                centred(1, FA[0], FA[1])
                stat_root(2, 40, 1.0, gn_eps_col)
                act.wait_ge(sem("ob_ready"), 4)
                cat(0, (A[0], A[7]))

            def odd_mix():
                act.wait_ge(sem("lconv_turned"), 1)
                fn(lcst[:, :], psum[0:11, 6, :], ACT.Copy).then_inc(sem("lconv_copied"), 1)
                act.wait_ge(sem("lam_abs"), 1)
                fn(lt[:, 4:8], lt[:, 0:4], ACT.Exp, scale=-1.0).then_inc(sem("lam_exp"), 1)
                act.wait_ge(sem("lam_exp"), 1)
                fn(lt[:, 8:12], lt[:, 4:8], ACT.Ln, bias=1.0).then_inc(sem("lam_ln"), 1)
                act.wait_ge(sem("dlam_sums"), 2)
                fn(lamt[:, 2:4], lamt[:, 0:2], ACT.Exp).then_inc(sem("dlam_exp"), 1)
                for n in range(8):
                    j = n % 4
                    act.wait_ge(sem("gates_ready"), n + 1)
                    fn(tok(X[1 + n // 4][:, j, :]), halves(4 * (n % 2)), ACT.Sigmoid, bias=V("ba" if n < 4 else "bi", j)).then_inc(sem("gates_copied"), 1)
                act.wait_ge(sem("lru_sp_ready"), 1)
                act.wait_ge(sem("gates_copied"), 8)
                for j in range(GT):
                    fn(X[3][:, j, :], X[1][:, j, :], ACT.Tanh, scale=lru_sp[:, j:j + 1]).then_inc(sem("lru_decays"), 1)
                for j in range(GT):
                    fn(X[1][:, j, :], X[1][:, j, :], ACT.Exp, scale=lru_nsp[:, j:j + 1]).then_inc(sem("lru_decays"), 1)
                act.wait_ge(sem("lru_v"), 1)
                fn(X[3][:, :, :], X[3][:, :, :], ACT.Sqrt).then_inc(sem("lru_root"), 1)
                fn(A[4][:, :, :], A[4][:, :, :], ACT.Gelu_apprx_tanh).then_inc(sem("gelu_ready"), 1)
                for x in range(5):
                    w = P if x < 4 else NS
                    act.wait_ge(sem("kv_turned"), x + 1)
                    for n in range(2):
                        dst = (vtm, ktm)[n][:, x, :] if x < 4 else (vs8o, ks8)[n][:, :]
                        fn(dst, psum[0:w, 2 * (x % 2) + n, :], ACT.Copy).then_inc(sem("kv_copied"), 1)
                act.wait_ge(sem("qs_turned"), 1)
                fn(qs8[:, :], psum[0:NS, 4, :], ACT.Copy).then_inc(sem("qs_copied"), 1)
                act.wait_ge(sem("lruh_turned"), 1)
                fn(lhst[:, :], psum[0:9, 5, :], ACT.Copy).then_inc(sem("lruh_copied"), 1)
                act.wait_ge(sem("lru_done"), 1)
                def exps(n):
                    nk = (n // 4 + 1) * P
                    act.wait_ge(sem("mx_ready"), n + 1)
                    if n >= 2:
                        act.wait_ge(sem("wt_turned"), n - 1)
                    for m in range(2):
                        fn(probs[:, n % 2, m, 0:nk], psum[:, 2 * (n % 2) + m, 0:nk], ACT.Exp, bias=nb2s[n % 2][:, m:m + 1], scale=HD ** -0.5,
                           accum_out=l2s[n % 2][:, m:m + 1]).then_inc(sem("exp_done"), 1)

                def out(n):
                    i, j = n // 4, n % 4
                    act.wait_ge(sem("pv2_done"), n + 1)
                    fn(A[0][:, j, i * P:(i + 1) * P], psum[:, 6 + n % 2, 0:P], ACT.Copy).then_inc(sem("oc_copied"), 1)

                exps(0)
                exps(1)
                for n in range(16):
                    nk = (n // 4 + 1) * P
                    act.wait_ge(sem("wt_turned"), n + 1)
                    fn(wtp[:, n % 2, 0:nk], psum[:, 4 + n % 2, 0:nk], ACT.Copy).then_inc(sem("wt_copied"), 1)
                    if n >= 1:
                        out(n - 1)
                    if n < 14:
                        exps(n + 2)
                out(15)
                act.wait_ge(sem("mxn_ready"), 1)
                for m in range(2):
                    fn(pdec[:, m, :], psum[0:32, 2 + m, :], ACT.Exp, bias=mxn[0:32, m:m + 1], scale=HD ** -0.5,
                       accum_out=l2[0:32, m:m + 1]).then_inc(sem("expd_done"), 1)
                    fn(pn2[0:32, m:m + 1], psum[0:32, 4, m:m + 1], ACT.Exp, bias=mxn[0:32, m:m + 1], scale=HD ** -0.5).then_inc(sem("expd_done"), 1)
                act.wait_ge(sem("wd_turned"), 1)
                fn(wtz[:, :, :].rearrange("p x (b c) -> p x b c", c=36)[:, :, :, 0:4], psum[:, 5, 0:128].rearrange("p (x b c) -> p x b c", x=PAGES, b=NS), ACT.Copy).then_inc(sem("wtd_copied"), 1)
                act.wait_ge(sem("vd_used"), 1)
                fn(odec[:, :], psum[0:32, 4, :], ACT.Copy).then_inc(sem("wtd_copied"), 1)
                act.wait_ge(sem("os2_ready"), 1)
                fn(X[1][:, :, :], A[0][:, :, :], ACT.Square).then_inc(sem("oc_sq"), 1)
                for r in range(3):
                    ahead(UB[("mix_out", 1)] + r, r, 0)
                stat_root(3, 20, 1.0 / P, eps_col)
                act.wait_ge(sem("ob_ready"), 8)
                cat(1, (A[0], A[4]))

            def mix_in(i):
                name = ("mix_in", i)
                u0, t0 = UB[name], TB[name]

                def body(it, stop):
                    for m in range(4):
                        if not (stop and m):
                            ahead(it * 4 + (u0 + m), m)
                        if m % 2 == 0:
                            continue
                        act.wait_ge(unit_used, it * 4 + (u0 + m))
                        fn(one2(u, it * 4 + (m - 1)), halves(0), ACT.Copy).then_inc(psum_free[0], 1)

                n = NT[name] // 4
                with act.Fori(0, n - 1) as it:
                    body(it, False)
                body(n - 1, True)

            def just_ahead(name, n):
                with act.Fori(0, n) as it:
                    for m in range(4):
                        ahead(it * 4 + (UB[name] + m), m)

            def gate(i):
                name = ("gate", i)
                u0 = UB[name]
                with act.Fori(0, 2) as it:
                    for m in range(4):
                        ahead(it * 4 + (u0 + m), m)
                        act.wait_ge(unit_used, it * 4 + (u0 + m + 1))
                        fn(one2(f, it * 4 + m), halves(4 * (m % 2)), ACT.Sigmoid).then_inc(psum_free[m % 2], 1)

            act.dma_start(cst[:, :], I["consts"]).then_inc(sem("x_loaded"), 16)
            for x in range(4):
                act.dma_start(stage[:, x, :], I["x_prompt"][0, x * P:(x + 1) * P]).then_inc(sem("x_loaded"), 16)
            act.dma_start(stage_s[:, :], I["x_sample"][:, 0, :]).then_inc(sem("x_loaded"), 16)
            for r in range(3):
                ahead(r, r, 0)
            act.wait_ge(sem("eps_set"), 2)
            for i in range(2):
                pre(NORM[(i, 0)])
                ffn(i, 0)
                post(NORM[(i, 1)], ("out", i, 0, 1))
                pre(NORM[(i, 2)])
                mix_in(i)
                (even_mix if i == 0 else odd_mix)()
                just_ahead(("mix_out", i), 2)
                post(NORM[(i, 3)], ("mix_out", i))
                pre(NORM[(i, 4)])
                ffn(i, 1)
                post(NORM[(i, 5)], ("out", i, 1, 1))
                pre(NORM[(i, 6)])
                gate(i)
                act.wait_ge(sem("p_turned"), i + 1)
                for k in range(2):
                    b = (2 + 4 * k) * 512
                    fn(phi[:, k, :], flat[:, b:b + T], ACT.Copy).then_inc(sem("phi_ready"), 1)
                for e in range(4):
                    ahead(UB[("ple", i)] + e, e)
                post(NORM[(i, 7)], ("ple", i))

        @block.vector
        def _(dve):
            own = Steps(dve, sem("dve_steps"))
            tt, ts, stt = nc.vector.tensor_tensor, nc.vector.tensor_scalar, nc.vector.scalar_tensor_tensor

            def ahead(u, r, lead=3):
                u, r = u + lead, r + lead
                if isinstance(u, int) and u >= NU:
                    return
                s, w = r % 4, raw_cols(u)
                dve.wait_ge(hi_ready, u + 1)
                tt(wlo[s][:, 0:w], raw[s][:, 0:w], whi[s][:, 0:w].bitcast(F32), ALU.subtract).then_inc(lo_ready, 1)

            def ffn(i, a):
                for r in range(2):
                    name = ("in", i, a, r)
                    u0, p0 = UB[name], PAIRS[name]
                    with dve.Fori(0, 8) as it:
                        for p in range(2):
                            for g in range(2):
                                ahead(it * 4 + (u0 + 2 * p + g), 2 * p + g)
                            pr = it * 2 + (p0 + p)
                            dve.wait_ge(sg_ready, pr + 1)
                            tt(tok(sgt[:, 2 + p, :]), tok(sgt[:, p, :]), halves(4 * p + 2), ALU.mult).then_inc(hid_ready, 1)
                            dve.wait_ge(hhi_ready, pr + 1)
                            tt(one(glo, it * 2 + p), sgt[:, 2 + p, :], one(ghi, it * 2 + p).bitcast(F32), ALU.subtract).then_inc(psum_free[p], 1)
                    name = ("out", i, a, r)
                    uo = UB[name]
                    with dve.Fori(0, 4) as it:
                        for m in range(2):
                            for g in range(2):
                                ahead(it * 4 + (uo + 2 * m + g), 2 * m + g)
                            dve.wait_ge(unit_used, it * 4 + (uo + 2 * m + 2))
                            dst = one2(f, it * 2 + m)
                            if r == 0:
                                ins = nc.vector.tensor_copy(dst, halves(4 * m))
                            else:
                                ins = tt(dst, halves(4 * m), dst, ALU.add)
                            ins.then_inc(psum_free[m], 1)

            RB = flat[:, 1024:1024 + T]

            def rstd(n):
                dve.wait_ge(sd_ready, n + 1)
                nc.vector.reciprocal(rs5b, rs5).then_inc(rs_ready, 1)
                dve.wait_ge(rb_ready, n + 1)

            def pre(n):
                rstd(n)
                for k in range(KT + 1):
                    if k < KT:
                        if k >= 2:
                            dve.wait_ge(xn_ready, 8 * (n // 2) + k - 1)
                        stt(sgt[:, 2 + k % 2, :], h[:, k, :], gcol[:, n * 8 + k:n * 8 + k + 1], RB, ALU.mult, ALU.mult).then_inc(xt_ready, 1)
                    if k >= 1:
                        j = k - 1
                        dve.wait_ge(xh_ready, 8 * (n // 2) + j + 1)
                        tt(xlo[:, j, :], sgt[:, 2 + j % 2, :], xhi[:, j, :].bitcast(F32), ALU.subtract).then_inc(xn_ready, 1)

            def post(n):
                rstd(n)
                for k in range(KT + 1):
                    if k < KT:
                        own(stt(f[:, k, :], f[:, k, :], gcol[:, n * 8 + k:n * 8 + k + 1], RB, ALU.mult, ALU.mult))
                    if k >= 1:
                        j = k - 1
                        dve.wait_ge(own.sem, own.n - (1 if k < KT else 0))
                        tt(h[:, j, :], h[:, j, :], f[:, j, :], ALU.add).then_inc(h_ready, 1)

            def stat_rate(g, n):
                dve.wait_ge(stat_rooted, g + 1)
                nc.vector.reciprocal(st_rs[:, 0:n], st_sd[:, 0:n]).then_inc(stat_ready, 1)

            def spread_mul(g, dst, src, gain=None):
                for j in range(GT):
                    dve.wait_ge(stat_spread, 4 * g + j + 1)
                    rb = flat[:, 4 * (j % 2) * 512:4 * (j % 2) * 512 + T]
                    if gain is None:
                        tt(dst[:, j, :], src[:, j, :], rb, ALU.mult).then_inc(stat_used, 1)
                    else:
                        stt(dst[:, j, :], src[:, j, :], gain, rb, ALU.mult, ALU.mult).then_inc(stat_used, 1)
                dve.wait_ge(stat_used, 4 * (g + 1))

            def cat(i, parts):
                for k in range(KT):
                    dve.wait_ge(cath_ready, 8 * i + k + 1)
                    tt(xlo[:, k, :], parts[k // 4][:, k % 4, :], xhi[:, k, :].bitcast(F32), ALU.subtract).then_inc(cat_ready, 1)

            def even_mix():
                q, k, v = A[0], A[1], A[2]
                dve.wait_ge(sem("tables_loaded"), 32)
                for n in range(8):
                    j, x = n % 4, A[n // 4]
                    dve.wait_ge(sem("rot_ready"), n + 1)
                    tt(tok(X[1][:, j, :]), halves(4 * (n % 2)), tok(rope[:, 1, :]), ALU.mult).then_inc(sem("rot_used"), 1)
                    own(tt(x[:, j, :], x[:, j, :], rope[:, 0, :], ALU.mult))
                    own.settle()
                    dve.wait_ge(sem("rot_used"), n + 1)
                    own(tt(x[:, j, :], x[:, j, :], X[1][:, j, :], ALU.add))
                    own.settle()
                    tt(x[:, j, :], x[:, j, :], decay[:, n // 4, j, :], ALU.mult).then_inc(sem("qk_ready"), 1)
                for i in range(4):
                    dve.wait_ge(sem("sc_ready"), i + 1)
                    if i:
                        dve.wait_ge(sem("pv_done"), i)
                    else:
                        dve.wait_ge(sem("qk_ready"), 8)
                    for hh in range(2):
                        tt(att[:, hh, :, :], psum[:, 2 + hh, :].rearrange("p (a b) -> p a b", a=GT),
                           C("causal_t").rearrange("p (o b) -> p o b", o=1).to_broadcast([P, GT, P]), ALU.mult).then_inc(sem("att_ready"), 1)
                    dve.wait_ge(sem("pv_done"), i + 1)
                    dve.wait_ge(sem("ubd_ready"), i + 1)
                    for hh in range(2):
                        hp = slice(hh * HD, (hh + 1) * HD)
                        ins = tt(ubd[hp, :, hp], ubd[hp, :, hp], psum[hp, 5, :].rearrange("p (a b) -> p a b", a=GT)[:, :, hp], ALU.add)
                        own(ins) if hh == 0 else ins.then_inc(sem("ubd_ready"), 1)
                    own.settle()
                dve.wait_ge(sem("ubd_ready"), 5)
                for hh in range(2):
                    hp = slice(hh * HD, (hh + 1) * HD)
                    tt(uout[hp, :, :], ubd[hp, :, hp], C("g511")[hp].rearrange("p (a o) -> p a o", o=1).to_broadcast([HD, GT, HD]), ALU.mult).then_inc(sem("uout_ready"), 1)
                dve.wait_ge(sem("sret_loaded"), 16 * GT)
                for j in range(GT):
                    dve.wait_ge(sem("vb_ready"), j + 1)
                    if j:
                        dve.wait_ge(sem("sret_ready"), j)
                    tt(kvt[:, :, :], psum[:, j % 2, :].rearrange("p (b v) -> p b v", b=NS),
                       k[:, j, SEQ:T].rearrange("p (b o) -> p b o", o=1).to_broadcast([P, NS, HD]), ALU.mult).then_inc(sem("vb_used"), 1)
                    dve.wait_ge(sem("vb_used"), j + 1)
                    stt(s_ret[:, j, :, :], s_ret[:, j, :, :], C("gam")[:, j:j + 1], kvt[:, :, :], ALU.mult, ALU.add).then_inc(sem("sret_ready"), 1)
                r_, k_, v_, z_ = A[4], A[5], A[6], A[7]

                def shift(x, n, d):
                    own(ts(d[:, :, 0:1], x[:, :, 0:1], -1.0, None, ALU.mult))
                    own(tt(d[:, :, 1:SEQ], x[:, :, 0:SEQ - 1], x[:, :, 1:SEQ], ALU.subtract))
                    own(tt(d[:, :, SEQ:T], shcol[:, :].rearrange("p (b j) -> p j b", b=NS)[:, 4 * n:4 * n + 4, :], x[:, :, SEQ:T], ALU.subtract))
                    own.settle()

                def lerp(dst, x, d, mu, signal):
                    for j in range(GT):
                        stt(dst[:, j, :], d[:, j, :], V("mu", 4 * mu + j), x[:, j, :], ALU.mult, ALU.add).then_inc(signal, 1)

                stat_rate(0, 40)
                spread_mul(0, X[0], X[0])
                dve.wait_ge(sem("silu_ready"), 1)
                tt(A[0][:, :, :], X[0][:, :, :], A[3][:, :, :], ALU.mult).then_inc(sem("oa_ready"), 1)
                dve.wait_ge(sem("oa_ready"), 1)
                dve.wait_ge(sem("sret_stored"), 64)
                dve.wait_ge(sem("rows_stored"), 48)
                shift(z_, 3, FA[0])
                lerp(FA[1], z_, FA[0], 3, sem("z_ready"))
                lerp(X[3], z_, FA[0], 4, sem("z_ready"))
                lerp(A[1], z_, FA[0], 5, sem("z_ready"))
                for n, (x, dst) in enumerate(((r_, X[0]), (k_, X[1]), (v_, X[2]))):
                    shift(x, n, A[2])
                    for j in range(GT):
                        own(stt(dst[:, j, :], A[2][:, j, :], V("mu", 4 * n + j), x[:, j, :], ALU.mult, ALU.add))
                    own.settle()
                nc.vector.memset(small[:, 190:191], 0.0).then_inc(sem("rkv_ready"), 3)
                for j in range(GT):
                    dve.wait_ge(sem("z_ready"), 12)
                    ts(FA[0][:, j, :], X[1][:, j, :], V("kk", j), None, ALU.mult).then_inc(sem("kk_raw"), 1)
                dve.wait_ge(stat_summed, 2)
                own(ts(st_in[:, 0:40], psum[:, 7, 0:40], 1e-24, None, ALU.max))
                own.settle()
                nc.vector.memset(small[:, 190:191], 0.0).then_inc(sem("kk_clamped"), 1)
                own(ts(omka, vcol[:, VEC["ka"][0]:VEC["ka"][0] + 4], -1.0, 1.0, ALU.mult, ALU.add))
                own.settle()
                dve.wait_ge(sem("l2_copied"), 8)
                for j in range(GT):
                    own(ts(A[4][:, j, :], FA[1][:, j, :], V("ka", j), omka[:, j:j + 1], ALU.mult, ALU.add))
                own.settle()
                own(tt(X[1][:, :, :], X[1][:, :, :], A[4][:, :, :], ALU.mult))
                stat_rate(1, 40)
                spread_mul(1, FA[0], FA[0])
                own(tt(FA[1][:, :, :], FA[1][:, :, :], FA[0][:, :, :], ALU.mult))
                dve.wait_ge(sem("tables_loaded"), 48)
                for j in range(GT):
                    own(nc.vector.tensor_tensor_scan(A[5][:, j, 0:SEQ], reset[:, :], A[2][:, j, 0:SEQ], 0.0, ALU.mult, ALU.add))
                own(nc.vector.tensor_copy(A[5][:, :, SEQ:T], A[2][:, :, SEQ:T]))
                own.settle()
                own(tt(A[2][:, :, :], A[5][:, :, :], A[2][:, :, :], ALU.subtract))
                own.settle()
                dve.wait_ge(sem("l2_copied"), 12)
                nc.vector.memset(small[:, 190:191], 0.0).then_inc(sem("cs_ready"), 1)
                dve.wait_ge(sem("dec_ready"), 3)
                nc.vector.memset(small[:, 190:191], 0.0).then_inc(sem("rw_ready"), 1)
                tt(FA[0][:, :, 0:SEQ], FA[0][:, :, 0:SEQ], A[2][:, :, 0:SEQ], ALU.mult).then_inc(sem("products_ready"), 1)
                tt(FA[1][:, :, 0:SEQ], FA[1][:, :, 0:SEQ], A[3][:, :, 0:SEQ], ALU.mult).then_inc(sem("products_ready"), 1)
                nc.vector.tensor_copy(dcol, A[5][:, :, CH - 1:SEQ:CH]).then_inc(sem("products_ready"), 1)
                dve.wait_ge(sem("srw_loaded"), 16 * GT)
                bcn = [0]

                def bc():
                    bcn[0] += 1
                    dve.wait_ge(sem("bc_ready"), bcn[0])
                    return psum[:, (bcn[0] - 1) % 6, :].rearrange("p (b k) -> p b k", b=NS)

                def col(x):
                    return x.rearrange("p (b o) -> p b o", o=1).to_broadcast([P, NS, HD])

                for j in range(GT):
                    S = s_rw[:, j, :, :]
                    t0, t1 = swt[0][:, :, :], swt[1][:, :, :]

                    def step(ins):
                        ins.then_inc(sem("bc_used"), 1)
                        dve.wait_ge(sem("bc_used"), bcn[0])

                    def mine(ins):
                        own(ins)
                        own.settle()

                    step(tt(t0, S, bc(), ALU.mult))
                    mine(nc.vector.tensor_reduce(sa8[:, :], t0, axis=AX.X, op=ALU.add))
                    step(tt(S, S, bc(), ALU.mult))
                    step(tt(t1, bc(), col(sa8[:, :]), ALU.mult))
                    mine(tt(S, S, t1, ALU.subtract))
                    step(tt(t0, bc(), col(X[2][:, j, SEQ:T]), ALU.mult))
                    mine(tt(S, S, t0, ALU.add))
                    step(tt(t1, S, bc(), ALU.mult))
                    mine(nc.vector.tensor_reduce(X[3][:, j, SEQ:T], t1, axis=AX.X, op=ALU.add))
                nc.vector.memset(small[:, 190:191], 0.0).then_inc(sem("srw_ready"), 1)
                nc.vector.memset(uc[:, :, :], 0.0).then_inc(sem("state_zeroed"), 1)
                dve.wait_ge(sem("srw_stored"), 16 * GT)

                def chunks(it, q):
                    wide = lambda name: C(name).rearrange("p (o b) -> p o b", o=1).to_broadcast([P, 2 * GT, HD])

                    def need(who, step):
                        after(dve, who, it, step)

                    def done(ins):
                        ins.then_inc(step_sem["inv.dve"], 1)

                    def masked(src, diag, mask, op=ALU.mult):
                        for hp in HP:
                            ins = tt(diag[hp, :, hp], src[hp], wide(mask)[hp], op)
                        done(ins)

                    def blocks(src, diag):
                        for hp in HP:
                            ins = nc.vector.tensor_copy(diag[hp, :, hp], src[hp])
                        return ins

                    def solution(c):
                        if q is not None:
                            after(dve, "rec.pe", q, f"z{c}")
                            nc.vector.tensor_copy(zc[:, :, :], four(bank(5, 256))).then_inc(step_sem["rec.dve"], 1)

                    def state(c):
                        if q is not None:
                            after(dve, "rec.pe", q, f"st{c}")
                            tt(uc[:, :, :], uc[:, :, :], four(bank(7, 256)), ALU.add).then_inc(step_sem["rec.dve"], 1)
                            after(dve, "rec.dve", q, f"u{c}")
                            k = q * 2 + c
                            d = dcol[:, :, k:k + 1] if isinstance(k, int) else dcol[:, :, bass.ds(k, 1)]
                            tt(uc[:, :, :], uc[:, :, :], d.to_broadcast([P, GT, HD]), ALU.mult).then_inc(step_sem["rec.dve"], 1)

                    def stage(x, src):
                        for hp in HP:
                            ins = ts(diagonal(bd[x], hp), by_chunk(src[hp, :, pair_cols(it, 0, 2 * CH)]), 1.0, None, ALU.mult)
                        done(ins)

                    if it is not None:
                        if not isinstance(it, int):
                            after(dve, "inv.pe", it - 1, "rb")
                        stage("be", FA[1])
                        stage("al", FA[0])
                        need("inv.pe", "at")
                        done(tt(cm["mt"][:, :, :], eight(bank(1)), wide("m_at"), ALU.mult))
                        need("inv.pe", "a")
                        done(tt(cm["m"][:, :, :], eight(bank(0)), wide("m_a"), ALU.mult))
                        need("inv.dve", "m")
                        for hp in HP:
                            ins = nc.vector.tensor_copy(bd["m"][hp, :, hp], cm["m"][hp, :, :])
                        done(ins)
                        done(tt(cm["e"], eight(bank(0)), wide("m_e"), ALU.mult))
                        done(tt(cm["x1"], cm["mt"][:, :, :], wide("stack"), ALU.add))
                        for n, src in enumerate((FA[0], X[0])):
                            ins = nc.vector.tensor_copy(mv[:, n].rearrange("p (c j) t -> p j c t", c=2), by_chunk(src[:, :, pair_cols(it, 0, 2 * CH)]))
                        done(ins)
                    if it is not None:
                        need("inv.pe", "m2t")
                        blocks(eight(bank(3)), bd["m2t"])
                        done(nc.vector.tensor_copy(cm["m2t"], eight(bank(3))))
                    solution(0)
                    if it is not None:
                        need("inv.pe", "x2")
                        done(blocks(two_banks(2, 0), bd["mt"]))
                        done(tt(cm["mt"][:, :, :], two_banks(2, 1), cm["x1"], ALU.add))
                    state(0)
                    if it is not None:
                        need("inv.pe", "x4")
                        need("inv.dve", "x2")
                        done(tt(cm["x1"], eight(bank(0)), cm["mt"][:, :, :], ALU.add))
                        need("inv.pe", "x8")
                        need("inv.dve", "x4")
                        done(tt(cm["m2"][:, :, :], eight(bank(2)), cm["x1"], ALU.add))
                        need("inv.dve", "xt")
                        done(nc.vector.tensor_copy(bd["m2t"][HP[1], :, HP[1]], cm["m2"][HP[1], :, :]))
                    if it is not None:
                        need("inv.pe", "ft")
                        done(blocks(eight(bank(3)), bd["m"]))
                    solution(1)
                    if it is not None:
                        done(tt(cm["m"][:, :, :], wide("stack"), eight(bank(3)), ALU.subtract))
                    state(1)
                    if it is not None:
                        if q is not None:
                            after(dve, "rec.pe", q, "pre1")
                        stage("alu", FA[0])
                        stage("rh", X[0])
                        need("inv.pe", "h")
                        need("inv.dve", "ift")
                        done(tt(cm["mt"][:, :, :], eight(bank(1)), cm["m"][:, :, :], ALU.add))
                        need("inv.pe", "rb")
                        if q is not None:
                            after(dve, "rec.pe", q, "o1")
                        masked(two_banks(2, 0), bd["rbt"], "m_i")
                        need("inv.pe", "ak")
                        masked(two_banks(0, 0), bd["akt"], "m_s")
                        masked(two_banks(0, 1), bd["rkt"], "m_i")

                dve.wait_ge(sem("bd_zeroed"), 18)
                chunks(0, None)
                with dve.Fori(1, NCH // 2) as it:
                    chunks(it, it - 1)
                chunks(None, NCH // 2 - 1)
                for r in range(3):
                    ahead(UB[("mix_out", 0)] + r, r, 0)
                dve.wait_ge(sem("products_ready"), 6)
                for j in range(GT):
                    own(ts(A[2][:, j, :], A[2][:, j, :], V("rk", j), None, ALU.mult))
                own.settle()
                nc.vector.memset(small[:, 190:191], 0.0).then_inc(sem("rkk_ready"), 1)
                stat_rate(2, 40)
                spread_mul(2, X[3], FA[0])
                for j in range(GT):
                    own(ts(X[3][:, j, :], X[3][:, j, :], V("ln", j), V("ln", 4 + j), ALU.mult, ALU.add))
                for j in range(GT):
                    dve.wait_ge(sem("bonus_ready"), j + 1)
                    tt(tok(X[2][:, j, :]), tok(X[2][:, j, :]), halves(4 * (j % 2)), ALU.mult).then_inc(sem("bonus_used"), 1)
                dve.wait_ge(sem("bonus_used"), 4)
                own.settle()
                own(tt(X[3][:, :, :], X[3][:, :, :], X[2][:, :, :], ALU.add))
                own.settle()
                tt(A[7][:, :, :], A[7][:, :, :], X[3][:, :, :], ALU.mult).then_inc(sem("ob_ready"), 4)
                cat(0, (A[0], A[7]))
                dve.wait_ge(sem("rows_stored"), 64)

            def odd_mix():
                xr, xc = A[3], X[0]
                lam = vcol[:, VEC["lam"][0]:VEC["lam"][0] + 4]

                def mine(ins):
                    own(ins)
                    own.settle()

                mine(ts(lt[:, 16:20], lam, -1.0, None, ALU.mult))
                tt(lt[:, 0:4], lt[:, 16:20], lam, ALU.max).then_inc(sem("lam_abs"), 1)
                dve.wait_ge(sem("lam_pages_loaded"), 32)
                mine(tt(dlam[:, 0, :], dlam[:, 0, :], dlam[:, 1, :], ALU.mult))
                nc.vector.tensor_reduce(lamt[:, 0:1], dlam[:, 0, :], axis=AX.X, op=ALU.add).then_inc(sem("dlam_sums"), 1)
                mine(tt(dlam[:, 2, :], dlam[:, 2, :], dlam[:, 3, :], ALU.mult))
                nc.vector.tensor_reduce(lamt[:, 1:2], dlam[:, 2, :], axis=AX.X, op=ALU.add).then_inc(sem("dlam_sums"), 1)
                dve.wait_ge(psum_free[0], TB[("mix_in", 1)] // 2 + 10)
                own.settle()
                for j in range(GT):
                    own(ts(xc[:, j, :], xr[:, j, :], V("conv_w", 12 + j), V("conv_b", j), ALU.mult, ALU.add))
                own.settle()
                buf = lrucol[:, 0:96].rearrange("p (b t j) -> p j t b", b=NS, t=3)
                for d in range(1, 4):
                    for j in range(GT):
                        w = V("conv_w", 4 * (3 - d) + j)
                        own(stt(xc[:, j, d:SEQ], xr[:, j, 0:SEQ - d], w, xc[:, j, d:SEQ], ALU.mult, ALU.add))
                        own(stt(xc[:, j, SEQ:T], buf[:, j, 3 - d, :], w, xc[:, j, SEQ:T], ALU.mult, ALU.add))
                    own.settle()
                nc.vector.memset(small[:, 190:191], 0.0).then_inc(sem("xc_ready"), 1)
                dve.wait_ge(sem("lam_ln"), 1)
                mine(ts(lt[:, 0:4], lt[:, 4:8], 1.0, None, ALU.add))
                mine(ts(lt[:, 0:4], lt[:, 0:4], 1.0, None, ALU.subtract))
                mine(ts(lt[:, 12:16], lt[:, 0:4], 0.0, None, ALU.is_equal))
                mine(tt(lt[:, 12:16], lt[:, 12:16], lt[:, 4:8], ALU.mult))
                mine(ts(lt[:, 0:4], lt[:, 0:4], 1e-30, None, ALU.max))
                mine(nc.vector.reciprocal(lt[:, 0:4], lt[:, 0:4]))
                mine(tt(lt[:, 8:12], lt[:, 8:12], lt[:, 4:8], ALU.mult))
                mine(tt(lt[:, 8:12], lt[:, 8:12], lt[:, 0:4], ALU.mult))
                mine(tt(lt[:, 8:12], lt[:, 8:12], lt[:, 12:16], ALU.add))
                mine(ts(lt[:, 16:20], lt[:, 16:20], 0.0, None, ALU.max))
                mine(tt(lt[:, 8:12], lt[:, 8:12], lt[:, 16:20], ALU.add))
                mine(ts(lru_sp, lt[:, 8:12], 8.0, None, ALU.mult))
                ts(lru_nsp, lt[:, 8:12], -8.0, None, ALU.mult).then_inc(sem("lru_sp_ready"), 1)
                dve.wait_ge(sem("dlam_exp"), 1)
                mine(tt(neglam, lamt[:, 3:4], lamt[:, 2:3], ALU.subtract))
                mine(ts(neglam, neglam, LAM_INIT, None, ALU.subtract))
                dve.wait_ge(sem("gates_copied"), 8)
                own(tt(FA[0][:, :, :], X[2][:, :, :], X[0][:, :, :], ALU.mult))
                dve.wait_ge(sem("lru_decays"), 8)
                mine(tt(FA[1][:, :, :], X[1][:, :, :], X[1][:, :, :], ALU.mult))
                for j in range(GT):
                    own(stt(X[3][:, j, :], FA[1][:, j, :], 1.0, X[3][:, j, :], ALU.add, ALU.mult))
                own.settle()
                nc.vector.memset(small[:, 190:191], 0.0).then_inc(sem("lru_v"), 1)
                dve.wait_ge(sem("lru_root"), 1)
                mine(tt(FA[1][:, :, :], FA[0][:, :, :], X[3][:, :, :], ALU.mult))
                for j in range(GT):
                    own(nc.vector.tensor_tensor_scan(FA[0][:, j, 0:SEQ], X[1][:, j, 0:SEQ], FA[1][:, j, 0:SEQ], 0.0, ALU.mult, ALU.add))
                mine(tt(FA[0][:, :, SEQ:T], X[1][:, :, SEQ:T], lrucol[:, 96:128].rearrange("p (b j) -> p j b", b=NS), ALU.mult))
                mine(tt(FA[0][:, :, SEQ:T], FA[0][:, :, SEQ:T], FA[1][:, :, SEQ:T], ALU.add))
                nc.vector.memset(small[:, 190:191], 0.0).then_inc(sem("lruh_ready"), 1)
                dve.wait_ge(sem("gelu_ready"), 1)
                mine(tt(A[4][:, :, :], A[4][:, :, :], FA[0][:, :, :], ALU.mult))
                dve.wait_ge(sem("lruh_turned"), 1)
                nc.vector.memset(small[:, 190:191], 0.0).then_inc(sem("lru_done"), 1)
                def maxima(n):
                    i = n // 4
                    nk = (i + 1) * P
                    ps = psum[:, 2 * (n % 2):2 * (n % 2) + 2, :]
                    dve.wait_ge(sem("qk2_ready"), n + 1)
                    mine(tt(ps[:, :, i * P:nk], ps[:, :, i * P:nk], C("causal_add").rearrange("p (o b) -> p o b", o=1).to_broadcast([P, 2, P]), ALU.add))
                    mine(nc.vector.tensor_reduce(mx2s[n % 2], ps[:, :, 0:nk], axis=AX.X, op=ALU.max))
                    ts(nb2s[n % 2], mx2s[n % 2], -HD ** -0.5, None, ALU.mult).then_inc(sem("mx_ready"), 1)

                maxima(0)
                maxima(1)
                for n in range(16):
                    nk = (n // 4 + 1) * P
                    dve.wait_ge(sem("exp_done"), 2 * (n + 1))
                    if n:
                        dve.wait_ge(sem("w_ready"), n)
                    mine(nc.vector.reciprocal(rl2, l2s[n % 2]))
                    mine(tt(rl2[:, 1:2], rl2[:, 1:2], neglam, ALU.mult))
                    mine(ts(probs[:, n % 2, 0, 0:nk], probs[:, n % 2, 0, 0:nk], rl2[:, 0:1], None, ALU.mult))
                    stt(probs[:, n % 2, 0, 0:nk], probs[:, n % 2, 1, 0:nk], rl2[:, 1:2], probs[:, n % 2, 0, 0:nk], ALU.mult, ALU.add).then_inc(sem("w_ready"), 1)
                    if n < 14:
                        maxima(n + 2)
                dve.wait_ge(sem("lru_stored"), 80)
                tt(prodn[:, :, :].rearrange("p b h -> p h b"), A[0][:, :, SEQ:T], A[1][:, :, SEQ:T], ALU.mult).then_inc(sem("sdec_ready"), 1)
                for b in range(NS):
                    dve.wait_ge(sem(f"kd_loaded{b % 2}"), 64 * (b // 2 + 1))
                    dve.wait_ge(sem("qb_ready"), b + 1)
                    dve.wait_ge(sem("sdec_ready"), b + 1)
                    tt(kprod[:, :, :], kd[b % 2][:, :, :], bank(b % 2).rearrange("p (o n) -> p o n", o=1).to_broadcast([P, PAGES, GW]), ALU.mult).then_inc(sem("qb_used"), 1)
                    dve.wait_ge(sem("qb_used"), b + 1)
                    for x in range(PAGES):
                        ins = nc.vector.tensor_reduce(sdec[:, :, x, b, :].rearrange("p m h -> p h m"), kprod[:, x, :].rearrange("p (h m d) -> p h m d", h=4, m=2), axis=AX.X, op=ALU.add)
                    ins.then_inc(sem("sdec_ready"), 1)
                dve.wait_ge(sem("sdec_ready"), NS + 1)
                nc.vector.memset(wtz[:, :, :], 0.0)
                dve.wait_ge(sem("sd_turned"), 1)
                ps = psum[0:32, 2:4, :]
                mine(nc.vector.tensor_reduce(mxn[0:32], ps, axis=AX.X, op=ALU.max))
                mine(tt(mxn[0:32], mxn[0:32], psum[0:32, 4, 0:2], ALU.max))
                ts(mxn[0:32], mxn[0:32], -HD ** -0.5, None, ALU.mult).then_inc(sem("mxn_ready"), 1)
                dve.wait_ge(sem("expd_done"), 4)
                mine(tt(l2[0:32], l2[0:32], pn2[0:32], ALU.add))
                mine(nc.vector.reciprocal(rl2[0:32], l2[0:32]))
                mine(tt(rl2[0:32, 1:2], rl2[0:32, 1:2], neglam[0:32], ALU.mult))
                mine(ts(pdec[:, 0, :], pdec[:, 0, :], rl2[0:32, 0:1], None, ALU.mult))
                mine(stt(pdec[:, 0, :], pdec[:, 1, :], rl2[0:32, 1:2], pdec[:, 0, :], ALU.mult, ALU.add))
                mine(tt(wn2[0:32], pn2[0:32], rl2[0:32], ALU.mult))
                mine(tt(wn2[0:32, 0:1], wn2[0:32, 0:1], wn2[0:32, 1:2], ALU.add))
                ts(wdiag[:, :], ident[0:32, 0:32], wn2[0:32, 0:1], None, ALU.mult).then_inc(sem("wd_ready"), 1)
                dve.wait_ge(sem("vd_used"), 2)
                tmp = dlam[:, 0, 0:32].rearrange("p (b h) -> p h b", b=NS)
                mine(tt(tmp, A[2][:, :, SEQ:T], psum[:, 6, 0:32].rearrange("p (b h) -> p h b", b=NS), ALU.mult))
                for j in range(4):
                    ins = tt(A[0][:, j, SEQ:T], tmp[:, j], psum[:, 7, j * 33:j * 33 + 29:4], ALU.add)
                ins.then_inc(sem("os2_ready"), 1)
                own(ts(small[:, 188:189], V("subln"), 1.0 - LAM_INIT, None, ALU.mult))
                own.settle()
                for r in range(3):
                    ahead(UB[("mix_out", 1)] + r, r, 0)
                stat_rate(3, 20)
                spread_mul(3, A[0], A[0], small[:, 188:189])
                nc.vector.memset(small[:, 190:191], 0.0).then_inc(sem("ob_ready"), 4)
                cat(1, (A[0], A[4]))

            def mix_in(i):
                name = ("mix_in", i)
                u0 = UB[name]

                def body(it, stop):
                    for m in range(4):
                        if not (stop and m):
                            ahead(it * 4 + (u0 + m), m)
                        if m % 2:
                            dve.wait_ge(unit_used, it * 4 + (u0 + m + 1))
                            nc.vector.tensor_copy(one2(u, it * 4 + m), halves(4)).then_inc(psum_free[1], 1)

                n = NT[name] // 4
                with dve.Fori(0, n - 1) as it:
                    body(it, False)
                body(n - 1, True)

            def mix_out(i):
                u0 = UB[("mix_out", i)]
                with dve.Fori(0, 2) as it:
                    for m in range(4):
                        ahead(it * 4 + (u0 + m), m)
                        dve.wait_ge(unit_used, it * 4 + (u0 + m + 1))
                        nc.vector.tensor_copy(one2(f, it * 4 + m), halves(4 * (m % 2))).then_inc(psum_free[m % 2], 1)

            nc.vector.memset(eps_col, EPS).then_inc(sem("eps_set"), 1)
            nc.vector.memset(gn_eps_col, GN_EPS).then_inc(sem("eps_set"), 1)
            dve.wait_ge(sem("rows_turned"), 1)
            for n, (dst, rows) in enumerate(row_tables):
                w = rows.shape[0]
                own(nc.vector.tensor_copy(dst[:, 0:w], psum[:, 6, n * P:n * P + w]))
            own.settle()
            for i in range(2):
                for k in (1, 5):
                    x = (i * 8 + k) * 8
                    own(ts(gcol[:, x:x + 8], gcol[:, x:x + 8], 0.5, None, ALU.mult))
            for k in range(KT):
                dve.wait_ge(sem("xt_turned"), k + 1)
                b = 4 * (k % 2)
                nc.vector.tensor_copy(h[:, k, :], flat[:, b * 512:b * 512 + T]).then_inc(h_ready, 1)
            for r in range(3):
                ahead(r, r, 0)
            own.settle()
            for i in range(2):
                pre(NORM[(i, 0)])
                ffn(i, 0)
                post(NORM[(i, 1)])
                pre(NORM[(i, 2)])
                mix_in(i)
                (even_mix if i == 0 else odd_mix)()
                mix_out(i)
                post(NORM[(i, 3)])
                pre(NORM[(i, 4)])
                ffn(i, 1)
                post(NORM[(i, 5)])
                pre(NORM[(i, 6)])
                with dve.Fori(0, 2) as it:
                    for m in range(4):
                        ahead(it * 4 + (UB[("gate", i)] + m), m)
                for k in range(2):
                    dve.wait_ge(sem("phi_ready"), 2 * i + k + 1)
                    b = (2 + 4 * k) * 512
                    tt(plo[:, k, :], flat[:, b:b + T], phi[:, k, :].bitcast(F32), ALU.subtract).then_inc(sem("plo_ready"), 1)
                for e in range(4):
                    ahead(UB[("ple", i)] + e, e)
                    for m in range(2):
                        dve.wait_ge(unit_used, UB[("ple", i)] + e + 1)
                        dst = tok(f[:, 2 * e + m, :])
                        tt(dst, halves(4 * m), dst, ALU.mult).then_inc(psum_free[m], 1)
                post(NORM[(i, 7)])
            for x in range(5):
                w = P if x < 4 else NS
                dve.wait_ge(sem("y_turned"), x + 1)
                b = 4 * (x % 2) * 512
                dst = stage[:, x, :] if x < 4 else stage_s[:, :]
                nc.vector.tensor_copy(dst, flat[0:w, b:b + D]).then_inc(sem("y_copied"), 1)

        @block.gpsimd
        def _(pool):
            dma = pool.dma_start

            def zero(x, signal):
                nc.gpsimd.memset(x, 0.0).then_inc(signal, 1)

            for dst, src in ROWS[10:]:
                dma(dst, src).then_inc(sem("inputs_loaded"), 16)

            def p_load(i):
                dma(pst[:, :, :], I["p_prompt"][i, 0].rearrange("(x p) d -> p x d", p=P)).then_inc(sem("p_loaded"), 16)
                dma(pss[:, :], I["p_sample"][i, :, 0, :]).then_inc(sem("p_loaded"), 16)

            def squares(*norms):
                for n in norms:
                    for k in range(1, KT):
                        pool.wait_ge(sq_ready, KT * n + k + 1)
                        if k > 1:
                            pool.wait_ge(sq_used, (KT - 1) * n + k - 1)
                        nc.gpsimd.tensor_tensor(sgt[:, 0, :], sgt[:, 0, :], sq[:, k % 2, :], ALU.add).then_inc(sq_used, 1)

            squares(0, 1, 2)
            pool.wait_ge(xn_ready, 16)
            dma(rope[:, :, :], I["rope"].rearrange("p (a t) -> p a t", a=2)).then_inc(sem("tables_loaded"), 16)
            dma(decay[:, :, :, :], I["decay"].rearrange("p (a j t) -> p a j t", a=2, j=GT)).then_inc(sem("tables_loaded"), 16)
            for s in range(2):
                pool.wait_ge(psum_free[s], TB[("mix_in", 0)] // 2 + 16)
            zero(ubd[:, :, :], sem("ubd_ready"))
            for j in range(GT):
                dma(s_ret[:, j, :, :], I["state_ret"][0, :, 2 * j:2 * j + 2].rearrange("b h d v -> (h d) b v")).then_inc(sem("sret_loaded"), 16)
            pool.wait_ge(sem("shift_copied"), 4)
            dma(O["shift_prompt"][0, 0], shst[0:1, :, :].rearrange("p a b -> p (a b)")).then_inc(sem("rows_stored"), 16)
            dma(O["shift_sample"][0, :, 0, :], shst[1:9, :, :].rearrange("p a b -> p (a b)")).then_inc(sem("rows_stored"), 16)
            pool.wait_ge(sem("qk_ready"), 8)
            dma(reset[:, :], I["reset"]).then_inc(sem("tables_loaded"), 16)
            pool.wait_ge(sem("uout_ready"), 2)
            dma(O["ret_prompt"][0, 0].rearrange("(j h) d v -> (h d) j v", h=2), uout[:, :, :]).then_inc(sem("rows_stored"), 16)
            for j in range(GT):
                pool.wait_ge(sem("sret_ready"), j + 1)
                dma(O["ret_sample"][0, :, 2 * j:2 * j + 2].rearrange("b h d v -> (h d) b v"), s_ret[:, j, :, :]).then_inc(sem("sret_stored"), 16)
            pool.wait_ge(sem("oa_ready"), 1)
            dma(lw1[:, :, :], I["rwkv_w1"][0].rearrange("(k p) n -> p k n", p=P)).then_inc(sem("lora_loaded"), 16)
            dma(la1[:, :, :], I["rwkv_a1"][0].rearrange("(k p) n -> p k n", p=P)).then_inc(sem("lora_loaded"), 16)
            dma(lg1[:, :, :], I["rwkv_g1"][0].rearrange("(k p) n -> p k n", p=P)).then_inc(sem("lora_loaded"), 16)
            dma(lw2[:, :], I["rwkv_w2"][0]).then_inc(sem("lora_loaded"), 16)
            dma(la2[:, :], I["rwkv_a2"][0]).then_inc(sem("lora_loaded"), 16)
            dma(lg2[:, :], I["rwkv_g2"][0]).then_inc(sem("lora_loaded"), 16)
            pool.wait_ge(sem("l1_ready"), 3)
            for j in range(GT):
                dma(s_rw[:, j, :, :], I["state_rwkv"][0, :, 2 * j:2 * j + 2].rearrange("b h v k -> (h v) b k")).then_inc(sem("srw_loaded"), 16)
            for x in ("al", "be", "m", "mt", "m2", "m2t", "e", "ka"):
                zero(bd[x][:, :, :], sem("bd_zeroed"))
            ptt = nc.gpsimd.tensor_tensor
            pool.wait_ge(sem("products_ready"), 1)
            ptt(A[2][:, :, :], X[0][:, :, :], X[1][:, :, :], ALU.mult).then_inc(sem("products_ready"), 1)
            pool.wait_ge(sem("products_ready"), 4)
            ptt(X[1][:, :, 0:SEQ], X[1][:, :, 0:SEQ], A[3][:, :, 0:SEQ], ALU.mult).then_inc(sem("products_ready"), 1)
            ptt(X[0][:, :, 0:SEQ], X[0][:, :, 0:SEQ], A[5][:, :, 0:SEQ], ALU.mult).then_inc(sem("products_ready"), 1)
            pool.wait_ge(sem("products_ready"), 6)
            pool.wait_ge(sem("rw_turned"), 1)
            for x in ("alu", "rh", "wt", "bt", "kt", "akt", "rbt", "rkt"):
                zero(bd[x][:, :, :], sem("bd_zeroed"))
            pool.wait_ge(sem("srw_ready"), 1)
            zero(ob[:, :, :], sem("bd_zeroed"))
            for j in range(GT):
                dma(O["rwkv_sample"][0, :, 2 * j:2 * j + 2].rearrange("b h v k -> (h v) b k"), s_rw[:, j, :, :]).then_inc(sem("srw_stored"), 16)
            pool.wait_ge(sem("srw_stored"), 16 * GT)
            nc.gpsimd.tensor_copy(mv[:, 2, :, :], C("stack").rearrange("p (o b) -> p o b", o=1).to_broadcast([P, 2 * GT, HD])).then_inc(sem("bd_zeroed"), 1)
            pool.wait_ge(sem("rwst_ready"), 1)
            dma(O["rwkv_prompt"][0, 0].rearrange("(j h) v k -> v j h k", h=2), rwst[:, :, :].rearrange("p j (h k) -> p j h k", h=2)).then_inc(sem("rows_stored"), 16)
            pool.wait_ge(sem("ob_ready"), 4)
            pool.wait_ge(cat_ready, 8)
            p_load(0)
            squares(3, 4, 5, 6, 7, 8, 9, 10)
            pool.wait_ge(xn_ready, 8 * 6)
            dma(dlam[:, :, :], I["diff_lam"][0].rearrange("a (o d) -> o a d", o=1).to_broadcast([P, 4, HD])).then_inc(sem("lam_pages_loaded"), 16)
            dma(pages[:, :], I["page_table"].rearrange("(o b) g -> o (b g)", o=1)).then_inc(sem("lam_pages_loaded"), 16)
            for s in range(2):
                pool.wait_ge(psum_free[s], TB[("mix_in", 1)] // 2 + 10)
            zero(wabd[:, :, :], sem("lruw_zeroed"))
            zero(wibd[:, :, :], sem("lruw_zeroed"))
            pool.wait_ge(sem("lruw_zeroed"), 2)
            for hh, hp in enumerate(HP):
                dma(wabd[hp, :, hp], I["lru_wa"][0, hh::2].rearrange("j d e -> d j e")).then_inc(sem("lruw_loaded"), 16)
                dma(wibd[hp, :, hp], I["lru_wi"][0, hh::2].rearrange("j d e -> d j e")).then_inc(sem("lruw_loaded"), 16)
            pool.wait_ge(sem("lconv_copied"), 1)
            dma(O["lru_conv_prompt"][0, 0], lcst[0:3, :]).then_inc(sem("lru_stored"), 16)
            dma(O["lru_conv_sample"][0, :, 2, :], lcst[3:11, :]).then_inc(sem("lru_stored"), 16)
            dma(O["lru_conv_sample"][0, :, 0:2, :], I["state_lru_conv"][0, :, 1:3, :]).then_inc(sem("lru_stored"), 16)
            pool.wait_ge(sem("lruh_copied"), 1)
            dma(O["lru_h_prompt"][0], lhst[0:1, :]).then_inc(sem("lru_stored"), 16)
            dma(O["lru_h_sample"][0], lhst[1:9, :]).then_inc(sem("lru_stored"), 16)
            pool.wait_ge(sem("kv_copied"), 10)
            dma(O["v_prompt"][0, 0].rearrange("(x p) h d -> p x (h d)", p=P), vtm[:, :, :]).then_inc(sem("kv_y_stored"), 16)
            dma(O["k_prompt"][0, 0].rearrange("(x p) h d -> p x (h d)", p=P), ktm[:, :, :]).then_inc(sem("kv_y_stored"), 16)
            dma(O["v_sample"][0, :, 0].rearrange("b h d -> b (h d)"), vs8o[:, :]).then_inc(sem("kv_y_stored"), 16)
            dma(O["k_sample"][0, :, 0].rearrange("b h d -> b (h d)"), ks8[:, :]).then_inc(sem("kv_y_stored"), 16)
            pool.wait_ge(sem("kv_y_stored"), 64)
            pool.wait_ge(cat_ready, 16)
            p_load(1)
            squares(11, 12, 13, 14, 15)
            pool.wait_ge(sem("y_copied"), 5)
            dma(O["y_prompt"][0].rearrange("(x p) d -> p x d", p=P), stage[:, :, :]).then_inc(sem("kv_y_stored"), 16)
            dma(O["y_sample"][:, 0, :], stage_s[:, :]).then_inc(sem("kv_y_stored"), 16)
            pool.wait_ge(sem("rows_stored"), 64)
            pool.wait_ge(sem("sret_stored"), 64)
            pool.wait_ge(sem("srw_stored"), 64)
            pool.wait_ge(sem("lru_stored"), 80)
            pool.wait_ge(sem("kv_y_stored"), 64)
            pool.wait_ge(sem("kv_y_stored"), 96)


INS = ["x_prompt", "x_sample", "cache_k", "cache_v", "state_ret", "state_rwkv", "state_rwkv_shift", "state_lru_h",
       "state_lru_conv", "page_table", "p_prompt", "p_sample", "norm_g", "ffn_w_in", "ffn_w_out", "ple_w",
       "ple_gate_w", "ab_w_in", "ab_w_out", "rwkv_mu", "rwkv_w0", "rwkv_w1", "rwkv_w2", "rwkv_a0", "rwkv_a1",
       "rwkv_a2", "rwkv_g1", "rwkv_g2", "rwkv_kk", "rwkv_ka", "rwkv_rk", "rwkv_ln", "cd_w_in", "cd_w_out",
       "diff_lam", "diff_subln", "lru_conv_w", "lru_conv_b", "lru_wa", "lru_ba", "lru_wi", "lru_bi", "lru_lambda"]
OUTS = [("y_prompt", (1, SEQ, D)), ("y_sample", (NS, 1, D)), ("k_prompt", (1, 1, SEQ, 4, 128)),
        ("v_prompt", (1, 1, SEQ, 4, 128)), ("ret_prompt", (1, 1, 8, HD, HD)), ("rwkv_prompt", (1, 1, 8, HD, HD)),
        ("shift_prompt", (1, 1, 1, 4 * GW)), ("lru_h_prompt", (1, 1, GW)), ("lru_conv_prompt", (1, 1, 3, GW)),
        ("k_sample", (1, NS, 1, 4, 128)), ("v_sample", (1, NS, 1, 4, 128)), ("ret_sample", (1, NS, 8, HD, HD)),
        ("rwkv_sample", (1, NS, 8, HD, HD)), ("shift_sample", (1, NS, 1, 4 * GW)), ("lru_h_sample", (1, NS, GW)),
        ("lru_conv_sample", (1, NS, 3, GW))]


def kernel(**inputs):
    import concourse.bacc as bacc
    from concourse.bass_utils import run_bass_kernel_spmd

    nc = bacc.Bacc("TRN2", target_bir_lowering=False, num_devices=1)
    arrays = {f"in_{n}": np.ascontiguousarray(inputs[n]) for n in INS}
    for n, a in zip(("consts", "rope", "decay", "reset"), host_constants()):
        arrays[f"in_{n}"] = a
    I = {n[3:]: nc.dram_tensor(n, a.shape, mybir.dt.from_np(a.dtype), kind="ExternalInput").ap() for n, a in arrays.items()}
    O = {n: nc.dram_tensor(f"out_{n}", s, F32, kind="ExternalOutput").ap() for n, s in OUTS}
    build(nc, I, O)
    r = run_bass_kernel_spmd(nc, [arrays], core_ids=[0])
    return tuple(r.results[0][f"out_{n}"] for n, _ in OUTS)
```

```python
import math
from contextlib import ExitStack

import numpy as np

import concourse.bass as bass
from concourse import mybir
from concourse.alu_op_type import AluOpType as ALU

ACT = mybir.ActivationFunctionType
AX = mybir.AxisListType
F32 = mybir.dt.float32
F32R = mybir.dt.float32r
I32 = mybir.dt.int32

P = 128
SEQ = 512
NS = 8
T = SEQ + NS
TH = T // 2
D = 1024
KT = D // P
GW = 512
GT = GW // P
HD = 64
EPS = 1e-6
GN_EPS = 64e-5
CH = 64
NCH = SEQ // CH
TOK_TILES = [0, 128, 256, 384, T - P]
NEG = -1e30
LAM_INIT = 0.8 - 0.6 * math.exp(-0.3 * 1)
PAGES = 4
POOLED = 4

CONST = {}
_at = 0
for _n, _w in [("ident", 128), ("bones", 128), ("center", 128), ("rot", 128), ("causal_t", 128),
               ("causal_add", 128), ("m_a", 64), ("m_at", 64), ("m_e", 64), ("m_s", 64),
               ("m_i", 64), ("stack", 64), ("hsel", 2), ("ones2", 2), ("g511", 4), ("gam", 4),
               ("bsel", 2)]:
    CONST[_n] = (_at, _w)
    _at += _w
NCONST = _at

VEC = {}
_at = 0
for _n, _w in [("mu", 24), ("w0", 4), ("a0", 4), ("kk", 4), ("ka", 4), ("rk", 4), ("ln", 8),
               ("conv_w", 16), ("conv_b", 4), ("ba", 4), ("bi", 4), ("lam", 4), ("subln", 1)]:
    VEC[_n] = (_at, _w)
    _at += _w
NVEC = _at


def host_constants():
    c = np.zeros((P, NCONST), np.float32)

    def put(name, a):
        s, w = CONST[name]
        c[:, s:s + w] = a

    i = np.arange(P)
    blk = (i[:, None] // HD) == (i[None, :] // HD)
    r, q = i[:, None] % HD, np.arange(HD)[None, :]
    same16 = (r // 16) == (q // 16)
    put("ident", np.eye(P))
    put("bones", blk)
    put("center", np.eye(P) - blk / HD)
    rot = np.zeros((P, P))
    for m in range(P):
        if m % HD < 32:
            rot[m + 32, m] = -1
        else:
            rot[m - 32, m] = 1
    put("rot", rot)
    put("causal_t", i[:, None] <= i[None, :])
    put("causal_add", np.where(i[None, :] > i[:, None], NEG, 0.0))
    put("m_a", -1.0 * ((q < r) & same16))
    put("m_at", -1.0 * ((r < q) & same16))
    put("m_e", 1.0 * ((q < r) & ~same16))
    put("m_s", 1.0 * (r < q))
    put("m_i", 1.0 * (r <= q))
    put("stack", np.vstack([np.eye(HD)] * 2))
    put("hsel", np.stack([i < HD, i >= HD], 1) / HD)
    put("ones2", np.ones((P, 2)))
    put("bsel", np.stack([i < HD, i >= HD], 1))
    head = np.arange(8)
    lg = np.log1p(-np.exp2(-5.0 - head))
    hp = 2 * np.arange(GT)[None, :] + (i[:, None] // HD)
    put("g511", np.exp((SEQ - 1) * lg[hp]))
    put("gam", np.exp(lg[hp]))
    pos = np.concatenate([np.arange(SEQ), np.full(NS, SEQ)]).astype(np.float64)
    freq = 1.0 / (10000.0 ** np.linspace(0.0, 1.0, 32))
    ang = pos[None, :].astype(np.float32) * freq[i % 32].astype(np.float32)[:, None]
    rope = np.stack([np.cos(ang), np.sin(ang)], 1).astype(np.float32)
    t = np.concatenate([np.arange(SEQ), np.zeros(NS)])
    sample = (np.arange(T) >= SEQ)
    dq = np.exp(t[None, None, :] * lg[hp][:, :, None])
    dk = np.exp(-t[None, None, :] * lg[hp][:, :, None]) * HD ** -0.5
    decay = np.stack([dq, dk], 1).astype(np.float32)
    reset = (np.arange(SEQ) % CH != 0).astype(np.float32)[None].repeat(P, 0)
    return c, rope.reshape(P, 2 * T), decay.reshape(P, 2 * GT * T), reset


class Steps:

    def __init__(self, eng, sem):
        self.eng, self.sem, self.n = eng, sem, 0

    def __call__(self, ins):
        self.n += 1
        ins.then_inc(self.sem, 1)
        return ins

    def settle(self):
        self.eng.wait_ge(self.sem, self.n)


def build(nc, I, O):
    ctx = ExitStack()
    with ctx:
        sems = {}

        def sem(name):
            if name not in sems:
                sems[name] = ctx.enter_context(nc.semaphore(name))
            return sems[name]

        base = (nc.sbuf_base + 63) // 64 * 64
        top = [base]

        def at(name, shape, offset, dt=F32):
            return nc.alloc_sbuf_tensor_at(name, shape, dt, offset=offset)

        def new(name, shape, dt=F32):
            n = int(np.prod(shape[1:])) * 4
            o = top[0]
            top[0] += (n + 31) // 32 * 32
            assert top[0] <= nc.sbuf_usable_end, (name, top[0])
            return at(name, shape, o, dt), o

        UNIT = KT * P
        raw = [new(f"raw{s}", [P, UNIT])[0] for s in range(4)]
        whi, whi_at = zip(*[new(f"whi{s}", [P, UNIT], F32R) for s in range(4)])
        wlo, wlo_at = zip(*[new(f"wlo{s}", [P, UNIT], F32R) for s in range(4)])
        h, _ = new("h", [P, KT, T])
        f, F_AT = new("f", [P, KT, T])
        xhi, X_AT = new("xhi", [P, KT, T], F32R)
        xlo, _ = new("xlo", [P, KT, T], F32R)
        ghi, A_AT = new("ghi", [P, 16, T], F32R)
        glo, _ = new("glo", [P, 16, T], F32R)
        sgt, SG_AT = new("sgt", [P, 4, T])
        sq, SQ_AT = new("sq", [P, 2, T])
        rbk = sq[:, 0, :]
        cst, _ = new("cst", [P, NCONST])
        gcol, _ = new("gcol", [P, P])
        vcol, _ = new("vcol", [P, 96])
        shcol, _ = new("shcol", [P, P])
        lrucol, _ = new("lrucol", [P, P])
        small, _ = new("small", [P, 192])
        rs5, rs5b, eps_col, gn_eps_col = small[:, 0:5], small[:, 8:13], small[:, 14:15], small[:, 15:16]
        st_in, st_sd, st_rs = small[:, 16:56], small[:, 56:96], small[:, 96:136]
        omka, lru_sp, lru_nsp, lt = small[:, 136:140], small[:, 140:144], small[:, 144:148], small[:, 148:168]
        neglam, mx2, nb2, l2, rl2 = small[:, 168:169], small[:, 170:172], small[:, 172:174], small[:, 174:176], small[:, 176:178]
        mx2s, nb2s, l2s = (mx2, small[:, 16:18]), (nb2, small[:, 18:20]), (l2, small[:, 20:22])
        lamt, mxn, pn2, wn2 = small[:, 178:182], small[:, 182:184], small[:, 184:186], small[:, 186:188]
        EXTRA = top[0]
        assert EXTRA + 6144 <= nc.sbuf_usable_end, EXTRA
        AR = GT * T * 4
        u = at("u", [P, 32, T], A_AT)
        A = [u[:, 4 * n:4 * n + 4, :] for n in range(8)]
        FA = [at(f"FA{n}", [P, GT, T], F_AT + n * AR) for n in range(2)]
        X = [at(f"X{n}", [P, GT, T], X_AT + n * AR) for n in range(4)]
        stage = at("stage", [P, 4, D], A_AT)
        stage_s = at("stage_s", [NS, D], A_AT + 4 * D * 4)
        phi = at("phi", [P, 2, T], A_AT, F32R)
        plo = at("plo", [P, 2, T], A_AT + 2 * T * 4, F32R)
        pst = at("pst", [P, 4, 256], EXTRA)
        pss = at("pss", [NS, 256], EXTRA + 4096)

        rope = at("rope", [P, 2, T], SG_AT)
        decay = at("decay", [P, 2, GT, T], F_AT)
        shst = at("shst", [9, 16, P], wlo_at[0])
        ktok = at("ktok", [P, GT, P], whi_at[0])
        vtok = at("vtok", [P, GT, P], whi_at[0] + 2048)
        ubd = at("ubd", [P, GT, P], whi_at[1])
        uout = at("uout", [P, GT, HD], whi_at[1] + 2048)
        vs8 = at("vs8", [NS, GW], SQ_AT)
        att = at("att", [P, 2, GT, P], whi_at[2])
        kvt = at("kvt", [P, NS, HD], SQ_AT + 2048)
        s_ret = at("s_ret", [P, GT, NS, HD], wlo_at[2])

        lw1 = at("lw1", [P, GT, HD], whi_at[3])
        la1 = at("la1", [P, GT, HD], whi_at[3] + 1024)
        lg1 = at("lg1", [P, GT, P], whi_at[3] + 2048)
        lw2 = at("lw2", [HD, GW], SG_AT + 2 * T * 4)
        la2 = at("la2", [HD, GW], SG_AT + 2 * T * 4 + 2048)
        lg2 = at("lg2", [P, GW], EXTRA)
        tw = at("tw", [HD, T], SQ_AT)
        ta = at("ta", [HD, T], SQ_AT + T * 4)
        tg = at("tg", [P, T], SG_AT)
        reset = at("reset", [P, SEQ], SG_AT + T * 4)
        rows8 = [at(f"rows8_{n}", [NS, GW], A_AT + 6 * AR + 2048 * n) for n in range(4)] + [at("rows8_4", [NS, GW], SQ_AT)]
        s_rw = at("s_rw", [P, GT, NS, HD], A_AT + 4 * AR)
        swt = [at(f"swt{n}", [P, NS, HD], EXTRA + 2048 * (n + 1)) for n in range(2)]
        sa8 = at("sa8", [P, NS], EXTRA)

        SPLIT_AT = [whi_at[n] for n in range(4)] + [wlo_at[n] for n in range(4)]
        bd_at = SPLIT_AT + [A_AT + 3 * AR + 4096 * n for n in range(6)] + [SG_AT, SG_AT + 4096]
        bd = {x: at(f"bd_{x}", [P, 2 * GT, P], bd_at[n]) for n, x in enumerate(
            ["al", "be", "m", "mt", "m2", "m2t", "e", "ka", "alu", "rh", "wt", "bt", "kt", "akt", "rbt", "rkt"])}
        mv = at("mv", [P, 4, 2 * GT, HD], A_AT + AR)
        mx = at("mx", [P, 2, 2 * GT, HD], A_AT + 6 * AR)
        cm = {x: at(f"cm_{x}", [P, 2 * GT, HD], o) for x, o in
              [("m", A_AT + 6 * AR + 4096), ("mt", A_AT + 6 * AR + 6144), ("m2", SQ_AT + 2048), ("vc", EXTRA)]}
        cm.update(e=mv[:, 3], m2t=mx[:, 0], x1=mx[:, 1])
        zc, rc, uc = [at(f"c_{x}", [P, GT, HD], EXTRA + 3072 + 1024 * n) for n, x in enumerate(["zc", "rc", "uc"])]
        ob = at("ob", [P, GT, P], SQ_AT)
        rwst = at("rwst", [HD, GT, P], SQ_AT + 2048)
        dcol = small[:, 16:16 + GT * NCH].rearrange("p (j c) -> p j c", j=GT)

        wabd = at("wabd", [P, GT, P], A_AT + 5 * AR)
        wibd = at("wibd", [P, GT, P], A_AT + 5 * AR + 2048)
        lcst = at("lcst", [11, GW], A_AT + 7 * AR)
        lhst = at("lhst", [9, GW], A_AT + 7 * AR + 2048)
        vtm = at("vtm", [P, GT, GW], A_AT + 5 * AR)
        ktm = at("ktm", [P, GT, GW], A_AT + 6 * AR)
        ks8 = at("ks8", [NS, GW], EXTRA)
        vs8o = at("vs8o", [NS, GW], EXTRA + 2048)
        qs8 = at("qs8", [NS, GW], EXTRA + 4096)
        dlam = at("dlam", [P, 4, HD], SG_AT)
        pages = at("pages", [1, NS * PAGES], SG_AT + 1024, I32)
        probs = at("probs", [P, 2, 2, SEQ], X_AT)
        wtp = at("wtp", [P, 2, SEQ], X_AT + AR)
        sdec = at("sdec", [P, 2, PAGES, NS, 4], X_AT + AR + 4096)
        kd = [at(f"kd{n}", [P, PAGES, GW], X_AT + (2 + n) * AR) for n in range(2)]
        vd = [at(f"vd{n}", [P, PAGES, GW], o) for n, o in enumerate(
            [whi_at[0], whi_at[2], wlo_at[0], wlo_at[2], F_AT, F_AT + AR, A_AT + 6 * AR, A_AT + 5 * AR])]
        qb = at("qb", [P, POOLED, GW], F_AT + AR)
        kprod = at("kprod", [P, PAGES, GW], A_AT + 7 * AR)
        odec = at("odec", [32, GW], SG_AT + 2048)
        pdec = at("pdec", [32, 2, SEQ], SG_AT + 2048)
        wtz = at("wtz", [P, PAGES, NS * 36], A_AT + 7 * AR)
        prodn = at("prodn", [P, NS, 4], SG_AT + 2048 + 4096 + 512)
        wdiag = at("wdiag", [32, 32], SG_AT + 2048 + 4096 + 512 + 128)
        assert SG_AT + 2048 + 4096 + 512 + 256 <= SG_AT + 4 * T * 4

        row_g = at("row_g", [P, P], A_AT + 5 * AR)
        row_v = at("row_v", [NVEC, P], A_AT + 5 * AR + 512)
        row_s = at("row_s", [P, P], A_AT + 5 * AR + 1024)
        row_l = at("row_l", [P, P], A_AT + 5 * AR + 1536)
        row_tables = [(gcol, row_g), (vcol, row_v), (shcol, row_s), (lrucol, row_l)]

        psum = ctx.enter_context(nc.psum_tensor("psum", [P, 8, 512], F32))
        flat = psum[:, :, :].rearrange("p b n -> p (b n)")

        def bank(b, n=512):
            return psum[:, b, 0:n]

        def halves(b):
            return psum[:, b:b + 2, 0:TH]

        def tok(x):
            return x.rearrange("p (h t) -> p h t", h=2)

        def C(name):
            s, w = CONST[name]
            return cst[:, s:s + w]

        def V(name, j=0):
            s, _ = VEC[name]
            return vcol[:, s + j:s + j + 1]

        ident = C("ident")

        w_in, w_out = I["ffn_w_in"], I["ffn_w_out"]
        PHASES = []

        def ffn_phases(i, a):
            for r in range(2):
                PHASES.append((("in", i, a, r), 32, 16))
                PHASES.append((("out", i, a, r), 16, 8))

        for i in range(2):
            ffn_phases(i, 0)
            PHASES.append((("mix_in", i), 32 if i == 0 else 20, 32 if i == 0 else 20))
            PHASES.append((("mix_out", i), 8, 8))
            ffn_phases(i, 1)
            PHASES.append((("gate", i), 8, 8))
            PHASES.append((("ple", i), 4, 8))
        UB, TB = {}, {}
        ub = tb = 0
        for name, nu, nt in PHASES:
            UB[name], TB[name] = ub, tb
            ub, tb = ub + nu, tb + nt
        NU = ub

        raw_loaded = [sem(f"raw_loaded{s}") for s in range(4)]
        hi_ready, lo_ready, unit_used = sem("hi_ready"), sem("lo_ready"), sem("unit_used")
        psum_free = [sem(f"psum_free{s}") for s in range(2)]
        sg_ready, hid_ready, hhi_ready = sem("sg_ready"), sem("hid_ready"), sem("hhi_ready")
        sq_ready, sq_used, sq_summed = sem("sq_ready"), sem("sq_used"), sem("sq_summed")
        sd_ready, rs_ready, rb_ready = sem("sd_ready"), sem("rs_ready"), sem("rb_ready")
        h_ready, xh_ready, xn_ready, rb_kept = sem("h_ready"), sem("xh_ready"), sem("xn_ready"), sem("rb_kept")
        gate_scaled = sem("gate_scaled")

        def free_count(t):
            return t // 2

        NORM = {}
        for i in range(2):
            for k in range(8):
                NORM[(i, k)] = 8 * i + k

        PAIRS, SG = {}, {}
        n = g = 0
        for name, _, nt in PHASES:
            PAIRS[name], SG[name] = n, g
            if name[0] == "in":
                n += nt
            if name[0] in ("in", "gate"):
                g += nt

        block = ctx.enter_context(nc.Block())

        cen_ready, cen_copied = sem("centred"), sem("centred_copied")
        stat_summed, stat_rooted, stat_ready = sem("stat_summed"), sem("stat_rooted"), sem("stat_ready")
        stat_spread, stat_used = sem("stat_spread"), sem("stat_used")
        cath_ready, cat_ready = sem("cat_hi_ready"), sem("cat_ready")

        def raw_cols(u):
            small_u = isinstance(u, int) and any(UB[("ple", i)] <= u < UB[("ple", i)] + 4 for i in range(2))
            return 512 if small_u else UNIT

        def one(x, m):
            return x[:, m, :] if isinstance(m, int) else x[:, bass.ds(m, 1), :].rearrange("p a t -> p (a t)")

        def one2(x, m):
            if isinstance(m, int):
                return tok(x[:, m, :])
            return x[:, bass.ds(m, 1), :].rearrange("p a (h t) -> p (a h) t", h=2)

        def row128(a):
            return a.rearrange("(k p) -> k p", p=P)

        def vrow(name):
            s, w = VEC[name]
            return row_v[s:s + w, :]

        ROWS = [
            (row_g[:, :], I["norm_g"].rearrange("i n (k p) -> (i n k) p", p=P)),
            (vrow("mu"), I["rwkv_mu"][0].rearrange("m (k p) -> (m k) p", p=P)),
            (vrow("w0"), row128(I["rwkv_w0"][0])), (vrow("a0"), row128(I["rwkv_a0"][0])),
            (vrow("kk"), row128(I["rwkv_kk"][0])), (vrow("ka"), row128(I["rwkv_ka"][0])),
            (vrow("rk"), I["rwkv_rk"][0].rearrange("(k h) d -> k (h d)", h=2)),
            (vrow("ln"), I["rwkv_ln"][0].rearrange("m (k p) -> (m k) p", p=P)),
            (vrow("conv_w"), I["lru_conv_w"][0].rearrange("m (k p) -> (m k) p", p=P)),
            (vrow("conv_b"), row128(I["lru_conv_b"][0])), (vrow("ba"), row128(I["lru_ba"][0])),
            (vrow("bi"), row128(I["lru_bi"][0])), (vrow("lam"), row128(I["lru_lambda"][0])),
            (vrow("subln"), I["diff_subln"]),
            (row_s[:, :], I["state_rwkv_shift"][0, :, 0, :].rearrange("b (k p) -> (b k) p", p=P)),
            (row_l[0:96, :], I["state_lru_conv"][0].rearrange("b t (k p) -> (b t k) p", p=P)),
            (row_l[96:128, :], I["state_lru_h"][0].rearrange("b (k p) -> (b k) p", p=P)),
        ]
        NROWS = len(ROWS)

        lin = I["ab_w_in"][0], I["cd_w_in"][0]
        lout = I["ab_w_out"][0], I["cd_w_out"][0]
        VD_GROUP = [0, 0, 0, 0, 1, 2, 1, 2]
        CAT_ORDER = [0, 1, 2, 3, 4, 5, 6, 7], [4, 5, 6, 7, 0, 1, 2, 3]
        DC = math.exp(-0.5)

        rec = lambda names: [f"{n}{c}" for c in range(2) for n in names]
        STEPS = {
            "inv.pe": ["at", "a", "m2", "m2t", "m4", "x2", "m8", "x4", "x8", "f", "ft", "f2", "v", "h", "rb", "ak", "w", "kt"],
            "inv.act": ["mt", "vb", "ka", "m2", "e", "m4", "m8", "xt", "f", "x", "f2", "v", "bt", "w", "kt"],
            "inv.dve": ["be", "al", "mt", "m", "mb", "e", "x1", "mv", "m2t", "m4t", "x2", "x4", "xt", "xtb", "ft", "ift",
                        "alu", "rh", "h", "rb", "ak", "rk"],
            "rec.pe": rec(["rhs", "pre", "z", "st", "o", "turn"]),
            "rec.act": rec(["rc", "ob", "out"]),
            "rec.dve": rec(["zc", "u", "ud"]),
        }
        step_sem = {who: sem(who.replace(".", "_")) for who in STEPS}

        def after(eng, who, it, step):
            names = STEPS[who]
            count = it * len(names) + names.index(step) + 1
            if not isinstance(count, int) or count > 0:
                eng.wait_ge(step_sem[who], count)

        def by_chunk(x):
            return x.rearrange("p j (c t) -> p j c t", c=2)

        def diagonal(x, hp):
            return x[hp, :, hp].rearrange("p (c j) t -> p j c t", c=2)

        def pair_cols(it, c, n=CH):
            t0 = it * (2 * CH) + c * CH
            return slice(t0, t0 + n) if isinstance(it, int) else bass.ds(t0, n)

        HP = [slice(0, HD), slice(HD, P)]
        four = lambda x: x.rearrange("p (a b) -> p a b", a=GT)
        eight = lambda x: x.rearrange("p (a b) -> p a b", a=2 * GT)
        two_banks = lambda b, n: flat[:, b * 512:(b + 2) * 512].rearrange("p (a s b) -> p a s b", a=2 * GT, s=2)[:, :, n, :]

        @block.sync
        def _(sp):
            def load(u, r, src, width=P, nk=KT):
                if not isinstance(u, int) or u >= 4:
                    sp.wait_ge(lo_ready, u - 3)
                s = r % 4
                dst = raw[s][:, 0:nk * width].rearrange("p (k c) -> p k c", k=nk)
                sp.dma_start(dst, src.rearrange("(k p) c -> p k c", p=P)).then_inc(raw_loaded[s], 16)

            def ffn(i, a):
                win, wout = w_in[i, a, :, :], w_out[i, a, :, :]
                for r in range(2):
                    u0 = UB[("in", i, a, r)]
                    first = 1 if u0 == 0 else 0
                    c0 = r * 16 * P
                    for p in range(2 * first):
                        load(2 * p, 2 * p, win[:, c0 + p * P:c0 + (p + 1) * P])
                        load(2 * p + 1, 2 * p + 1, win[:, 4096 + c0 + p * P:4096 + c0 + (p + 1) * P])
                    with sp.Fori(first, 8) as it:
                        for p in range(2):
                            col = it * (2 * P) + (c0 + p * P)
                            load(it * 4 + (u0 + 2 * p), 2 * p, win[:, bass.ds(col, P)])
                            load(it * 4 + (u0 + 2 * p + 1), 2 * p + 1, win[:, bass.ds(col + 4096, P)])
                    u0 = UB[("out", i, a, r)]
                    with sp.Fori(0, 4) as it:
                        for m in range(2):
                            for g in range(2):
                                row = (r * 2 + g) * D
                                load(it * 4 + (u0 + 2 * m + g), 2 * m + g,
                                     wout[row:row + D, bass.ds(it * (2 * P) + m * P, P)])

            def proj(name, w):
                u0, nt = UB[name], w.shape[1] // P
                with sp.Fori(0, nt // 4) as it:
                    for m in range(4):
                        load(it * 4 + (u0 + m), m, w[:, bass.ds(it * (4 * P) + m * P, P)])

            def page_stream():
                sp.wait_ge(sem("lam_pages_loaded"), 32)
                for s in range(2):
                    sp.wait_ge(psum_free[s], TB[("mix_in", 1)] // 2 + 10)

                def pages_of(cache, dst, b, signal):
                    for x in range(PAGES):
                        page = sp.value_load(pages[0:1, b * PAGES + x:b * PAGES + x + 1], min_val=0, max_val=cache.shape[1] - 1)
                        sp.dma_start(dst[:, x, :], cache[0, bass.ds(page, 1), :, :, :].rearrange("o p h d -> p (o h d)")).then_inc(signal, 16)

                def values(b):
                    pages_of(I["cache_v"], vd[b], b, sem(f"vd_loaded{VD_GROUP[b]}"))

                def keys(b):
                    pages_of(I["cache_k"], kd[b % 2], b, sem(f"kd_loaded{b % 2}"))

                for b in range(4):
                    values(b)
                sp.wait_ge(sem("lru_done"), 1)
                keys(0)
                keys(1)
                values(4)
                sp.wait_ge(sem("kv_y_stored"), 64)
                values(6)
                for b in range(2, POOLED + 2):
                    sp.wait_ge(sem("pool_keys"), 7 * (b - 2) + 1)
                    keys(b)
                sp.wait_ge(sem("pool_keys"), 7 * POOLED)
                values(5)
                sp.wait_ge(sem("oc_copied"), 16)
                values(7)
                for b in range(POOLED + 2, NS):
                    sp.wait_ge(sem("qb_used"), b - POOLED - 1)
                    keys(b)

            for dst, src in ROWS[:10]:
                sp.dma_start(dst, src).then_inc(sem("x_loaded"), 16)
            for i in range(2):
                ffn(i, 0)
                proj(("mix_in", i), lin[i])
                if i == 1:
                    page_stream()
                proj(("mix_out", i), lout[i])
                ffn(i, 1)
                proj(("gate", i), I["ple_gate_w"][i])
                for e in range(4):
                    load(UB[("ple", i)] + e, e, I["ple_w"][i][:, e * 256:(e + 1) * 256], 256, 2)

        NT = {name: nt for name, _, nt in PHASES}

        @block.tensor
        def _(pe):
            mm = nc.tensor.matmul

            def turn(out, in_):
                return nc.tensor.transpose(out, in_, ident[0:in_.shape[0], 0:in_.shape[0]])

            def unit(u, r, out, xh, xl, nk=KT, start=True, stop=True, width=P, c0=0, k0=0, last=True):
                pe.wait_ge(lo_ready, u + 1)
                s = r % 4
                hi = whi[s][:, 0:nk * width].rearrange("p (k c) -> p k c", k=nk)
                lo = wlo[s][:, 0:nk * width].rearrange("p (k c) -> p k c", k=nk)
                for k in range(nk):
                    for e in range(2):
                        for n, (w, x) in enumerate(((hi, xh), (hi, xl), (lo, xh))):
                            ins = mm(out[:, e, :], w[:, k, c0:c0 + P], x[:, k0 + k, e * TH:(e + 1) * TH],
                                     start=start and k == 0 and n == 0, stop=stop and k == nk - 1 and n == 2)
                if last:
                    ins.then_inc(unit_used, 1)

            def free(s, count):
                if not isinstance(count, int) or count > 0:
                    pe.wait_ge(psum_free[s], count)

            def lead_pair(u, outs, ready, count, order=range(KT)):
                pe.wait_ge(lo_ready, u + 2)
                first, last = order[0], order[-1]
                for n, k in enumerate(order):
                    pe.wait_ge(ready, count + n + 1)
                    for r in range(2):
                        hi, lo = [w[(u + r) % 4][:, :].rearrange("p (k c) -> p k c", k=KT) for w in (whi, wlo)]
                        for e in range(2):
                            for x, (w, act) in enumerate(((hi, xhi), (hi, xlo), (lo, xhi))):
                                ins = mm(outs[r][:, e, :], w[:, k, :], act[:, k, e * TH:(e + 1) * TH],
                                         start=(k == first and x == 0), stop=(k == last and x == 2))
                        if k == last:
                            ins.then_inc(unit_used, 1)

            def ffn(i, a):
                nx = NORM[(i, 0 if a == 0 else 4)]
                for r in range(2):
                    name = ("in", i, a, r)
                    u0, t0 = UB[name], TB[name] // 2

                    def body(it):
                        for p in range(2):
                            free(p, it + t0)
                            for g in range(2):
                                unit(it * 4 + (u0 + 2 * p + g), 2 * p + g, halves(4 * p + 2 * g), xhi, xlo)

                    if r == 0:
                        free(0, t0)
                        lead_pair(u0, (halves(0), halves(2)), xn_ready, 8 * (nx // 2))
                        sums(nx)
                        free(1, t0)
                        unit(u0 + 2, 2, halves(4), xhi, xlo)
                        rates(nx)
                        pe.wait_ge(rb_kept, nx // 2 + 1)
                        unit(u0 + 3, 3, halves(6), xhi, xlo)
                    with pe.Fori(1 - r, 8) as it:
                        body(it)
                    name = ("out", i, a, r)
                    uo, to = UB[name], TB[name] // 2

                    def obody(it, lead):
                        for m in range(2):
                            if lead and m == 0:
                                pe.wait_ge(psum_free[1], to - 4)
                                pe.wait_ge(psum_free[0], to)
                            else:
                                free(m, it + to)
                            unit(it * 4 + (uo + 2 * m), 2 * m, halves(4 * m), ghi, glo, stop=False)
                            if lead and m == 0:
                                pe.wait_ge(psum_free[1], to)
                            unit(it * 4 + (uo + 2 * m + 1), 2 * m + 1, halves(4 * m), ghi, glo, start=False, k0=KT)

                    obody(0, True)
                    with pe.Fori(1, 4) as it:
                        obody(it, False)

            def proj(name, nx=None, cat=None):
                u0, t0 = UB[name], TB[name] // 2

                def body(it, ms):
                    for m in ms:
                        free(m % 2, it * 2 + (t0 + m // 2))
                        unit(it * 4 + (u0 + m), m, halves(4 * (m % 2)), xhi, xlo)

                free(0, t0)
                free(1, t0)
                if cat is None:
                    lead_pair(u0, (halves(0), halves(4)), xn_ready, 8 * (nx // 2))
                    sums(nx)
                    rates(nx)
                else:
                    pe.wait_ge(stat_used, 12 + 4 * cat)
                    lead_pair(u0, (halves(0), halves(4)), cat_ready, 8 * cat, CAT_ORDER[cat])
                body(0, (2, 3))
                with pe.Fori(1, NT[name] // 4) as it:
                    body(it, range(4))

            def spread(b, r5, signal):
                heads = r5.shape[2]
                for x in range(5):
                    for g in range(heads):
                        n = P // heads
                        out, r = flat[g * n:(g + 1) * n, b * 512 + x * P:b * 512 + x * P + (P if x < 4 else NS)], r5[:, x, g:g + 1].to_broadcast([P, n])
                        last = mm(out, r, ident if x < 4 else ident[:, P - NS:P], start=True, stop=True)
                last.then_inc(signal, 1)

            def sums(n):
                pe.wait_ge(sq_used, (KT - 2) * (n + 1))
                for a, src in enumerate((sgt[:, 0, :], sq[:, 1, :])):
                    if a:
                        pe.wait_ge(sq_ready, KT * (n + 1))
                    for x, t0 in enumerate(TOK_TILES):
                        last = mm(psum[:, 7, 16 + x:17 + x], src[:, t0:t0 + P], C("ones2")[:, 0:1], start=(a == 0 and x == 0), stop=(a == 1),
                                  skip_group_check=True)
                last.then_inc(sq_summed, 1)

            def rates(n):
                pe.wait_ge(rs_ready, n + 1)
                spread(6, rs5b.rearrange("p (x o) -> p x o", o=1), rb_ready)

            def norm(n):
                sums(n)
                rates(n)

            def centre(g, src):
                for j in range(GT):
                    if 4 * g + j >= 2:
                        pe.wait_ge(cen_copied, 2 * (4 * g + j - 1))
                    for e in range(2):
                        last = mm(halves(4 * (j % 2))[:, e, :], C("center"), src[:, j, e * TH:(e + 1) * TH], start=True, stop=True)
                    last.then_inc(cen_ready, 1)

            def even_mix():
                q, k, v = A[0], A[1], A[2]
                for s in range(2):
                    pe.wait_ge(psum_free[s], TB[("mix_in", 0)] // 2 + 16)
                for n in range(16):
                    last = turn(psum[0:9, n // 4, (n % 4) * P:(n % 4 + 1) * P], u[:, 16 + n, SEQ - 1:T])
                last.then_inc(sem("shift_turned"), 1)
                pe.wait_ge(sem("shift_copied"), 4)
                for n in range(8):
                    if n >= 2:
                        pe.wait_ge(sem("rot_used"), n - 1)
                    for e in range(2):
                        last = mm(halves(4 * (n % 2))[:, e, :], C("rot"), A[n // 4][:, n % 4, e * TH:(e + 1) * TH], start=True, stop=True)
                    last.then_inc(sem("rot_ready"), 1)
                pe.wait_ge(sem("qk_ready"), 8)
                for i in range(4):
                    ts = slice(i * P, (i + 1) * P)
                    if i:
                        pe.wait_ge(sem("tk_copied"), 2 * i)
                    for j in range(GT):
                        turn(bank(0)[:, j * P:(j + 1) * P], k[:, j, ts])
                        last = turn(bank(1)[:, j * P:(j + 1) * P], v[:, j, ts])
                    last.then_inc(sem("tk_turned"), 1)
                    if i:
                        pe.wait_ge(sem("att_ready"), 2 * i)
                    for hh in range(2):
                        hp = slice(hh * HD, (hh + 1) * HD)
                        for j in range(GT):
                            last = mm(bank(2 + hh)[:, j * P:(j + 1) * P], k[hp, j, ts], q[hp, j, ts], start=True, stop=True)
                    last.then_inc(sem("sc_ready"), 1)
                    pe.wait_ge(sem("tk_copied"), 2 * (i + 1))
                    pe.wait_ge(sem("att_ready"), 2 * (i + 1))
                    pe.wait_ge(sem("ubd_ready"), i + 1)
                    if i:
                        pe.wait_ge(sem("o_copied"), i)
                    for j in range(GT):
                        js = slice(j * P, (j + 1) * P)
                        mm(bank(4)[:, js], ubd[:, j, :], q[:, j, ts], start=True, stop=False, skip_group_check=True)
                        for hh in range(2):
                            hp = slice(hh * HD, (hh + 1) * HD)
                            mm(bank(4)[hp, js], vtok[:, j, hp], att[:, hh, j, :], start=False, stop=True, skip_group_check=True)
                    for j in range(GT):
                        last = mm(bank(5)[:, j * P:(j + 1) * P], ktok[:, j, :], vtok[:, j, :], start=True, stop=True)
                    last.then_inc(sem("pv_done"), 1)
                for j in range(GT):
                    last = turn(psum[0:NS, 6, j * P:(j + 1) * P], v[:, j, SEQ:T])
                last.then_inc(sem("vs_turned"), 1)
                pe.wait_ge(sem("vs8_ready"), 1)
                for j in range(GT):
                    if j >= 2:
                        pe.wait_ge(sem("vb_used"), j - 1)
                    for hh in range(2):
                        for b in range(NS):
                            last = mm(psum[hh * HD:(hh + 1) * HD, j % 2, b * HD:(b + 1) * HD], ident[0:NS, b:b + 1].to_broadcast([NS, HD]),
                                      vs8[:, (2 * j + hh) * HD:(2 * j + hh + 1) * HD], start=True, stop=True)
                    last.then_inc(sem("vb_ready"), 1)
                for j in range(GT):
                    pe.wait_ge(sem("sret_ready"), j + 1)
                    for hh in range(2):
                        hp = slice(hh * HD, (hh + 1) * HD)
                        for b in range(NS):
                            last = mm(psum[hp, 2 + hh, j * NS + b:j * NS + b + 1], s_ret[hp, j, b, :], q[hp, j, SEQ + b:SEQ + b + 1], start=True, stop=True)
                last.then_inc(sem("os_ready"), 1)
                pe.wait_ge(sem("o_copied"), 6)
                centre(0, A[0])
                head_stat0(0)
                pe.wait_ge(sem("lora_loaded"), 96)
                pe.wait_ge(sem("z_ready"), 12)
                pe.wait_ge(stat_used, 4)
                for n, (w, x, b, m) in enumerate(((lw1, FA[1], 0, HD), (la1, X[3], 2, HD), (lg1, A[1], 4, P))):
                    for e in range(2):
                        for j in range(GT):
                            last = mm(halves(b)[0:m, e, :], w[:, j, :], x[:, j, e * TH:(e + 1) * TH], start=(j == 0), stop=(j == GT - 1))
                    last.then_inc(sem("l1_ready"), 1)
                for n in range(12):
                    w, x = ((lw2, tw), (la2, ta), (lg2, tg))[n // 4]
                    if n % 4 == 0:
                        pe.wait_ge(sem("l1_copied"), 3)
                    if n >= 2:
                        pe.wait_ge(sem("l2_copied"), n - 1)
                    j = n % 4
                    for e in range(2):
                        last = mm(halves(4 * (n % 2))[:, e, :], w[:, j * P:(j + 1) * P], x[:, e * TH:(e + 1) * TH], start=True, stop=True)
                    last.then_inc(sem("l2_ready"), 1)
                pe.wait_ge(sem("l2_copied"), 12)
                pe.wait_ge(sem("kk_sq"), 4)
                stat_body(1, X[3], C("bsel"))
                pe.wait_ge(sem("rw_ready"), 1)
                for n, x in enumerate((FA[0], A[5], FA[1], X[1], X[0])):
                    for j in range(GT):
                        last = turn(psum[0:NS, n, j * P:(j + 1) * P], x[:, j, SEQ:T])
                last.then_inc(sem("rw_turned"), 1)
                pe.wait_ge(sem("rows8_ready"), 5)
                for n in range(20):
                    j, x = n // 5, n % 5
                    if n >= 6:
                        pe.wait_ge(sem("bc_used"), n - 5)
                    for hh in range(2):
                        for b in range(NS):
                            last = mm(psum[hh * HD:(hh + 1) * HD, n % 6, b * HD:(b + 1) * HD], ident[0:NS, b:b + 1].to_broadcast([NS, HD]),
                                      rows8[x][:, (2 * j + hh) * HD:(2 * j + hh + 1) * HD], start=True, stop=True)
                    last.then_inc(sem("bc_ready"), 1)
                pe.wait_ge(sem("bc_used"), 20)
                stack = C("stack")

                def prod(b, lhs, rhs, who, step, groups=range(2 * GT), more=None, first=True, w=HD):
                    terms = [(lhs, rhs)] + (more or [])
                    for n, g in enumerate(groups):
                        for x, (l, r) in enumerate(terms):
                            last = mm(flat[:, b * 512 + n * w:b * 512 + (n + 1) * w], l[:, g, :], r(g), start=first and (n * w) % 512 == 0 and x == 0,
                                      stop=(x == len(terms) - 1), skip_group_check=True)
                    if step:
                        last.then_inc(step_sem[who], 1)

                def of(x):
                    return (lambda g: x[:, g, :]) if len(x.shape) == 3 else (lambda g: x)

                def chunks(it, q):
                    col = lambda x: (lambda g: x[:, g % GT, pair_cols(it, g // GT)])

                    def inv(b, lhs, rhs, step, w=HD):
                        if it is not None:
                            prod(b, lhs, rhs, "inv.pe", step, w=w)

                    def two(x, n=0):
                        return lambda g: x[:, n:n + 2, g, :]

                    def need(who, step, back=0):
                        if it is not None and not (back and isinstance(it, int) and it == 0):
                            after(pe, who, it - back, step)

                    def head(c):
                        if q is None:
                            return
                        if c == 0:
                            for who, step in (("inv.dve", "rh"), ("inv.dve", "ak"), ("inv.dve", "rk"), ("inv.act", "kt")):
                                after(pe, who, q, step)
                            if not isinstance(q, int) or q > 0:
                                after(pe, "rec.dve", q - 1, "ud1")
                                after(pe, "rec.act", q - 1, "out1")
                        else:
                            after(pe, "rec.dve", q, "ud0")
                            after(pe, "rec.act", q, "out0")
                        gs = range(4 * c, 4 * c + 4)
                        state = lambda g: uc[:, g % GT, :]
                        prod(4, bd["alu"], state, "rec.pe", f"rhs{c}", gs, [(bd["akt"], of(cm["vc"]))])
                        prod(6, bd["rh"], state, "rec.pe", None, gs, [(bd["rkt"], of(cm["vc"]))])
                        prod(7, bd["kt"], of(cm["vc"]), "rec.pe", f"pre{c}", gs)

                    def solve(c):
                        if q is None:
                            return
                        after(pe, "inv.act", q, "w")
                        after(pe, "rec.act", q, f"rc{c}")
                        prod(5, bd["wt"], lambda g: rc[:, g % GT, :], "rec.pe", f"z{c}", range(4 * c, 4 * c + 4))

                    def tail(c):
                        if q is None:
                            return
                        after(pe, "inv.dve", q, "rb")
                        after(pe, "rec.dve", q, f"zc{c}")
                        gs, z = range(4 * c, 4 * c + 4), lambda g: zc[:, g % GT, :]
                        prod(7, bd["bt"], z, "rec.pe", f"st{c}", gs, first=False)
                        prod(6, bd["rbt"], z, "rec.pe", f"o{c}", gs, first=False)

                    def out(c):
                        if q is None:
                            return
                        after(pe, "rec.act", q, f"ob{c}")
                        prod(6, ob, of(stack), "rec.pe", f"turn{c}", range(GT))

                    need("inv.dve", "be")
                    need("inv.dve", "rk", 1)
                    inv(1, bd["be"], it is not None and col(FA[0]), "at")
                    need("inv.dve", "al")
                    inv(0, bd["al"], it is not None and col(FA[1]), "a")
                    head(0)
                    need("inv.act", "mt")
                    need("inv.dve", "m")
                    need("inv.act", "w", 1)
                    inv(2, bd["mt"], of(cm["m"]), "m2")
                    need("inv.dve", "mb")
                    need("inv.act", "kt", 1)
                    inv(3, bd["m"], of(cm["mt"]), "m2t")
                    solve(0)
                    need("inv.act", "m2")
                    need("inv.dve", "m2t")
                    inv(0, bd["m2t"], of(cm["m2"]), "m4")
                    inv(2, bd["m2"], two(mx), "x2", P)
                    tail(0)
                    need("inv.act", "m4")
                    need("inv.dve", "m4t")
                    inv(1, bd["mt"], of(cm["m"]), "m8")
                    need("inv.dve", "x2")
                    inv(0, bd["m"], of(cm["mt"]), "x4")
                    out(0)
                    need("inv.act", "m8")
                    need("inv.dve", "x4")
                    inv(2, bd["m2"], of(cm["x1"]), "x8")
                    head(1)
                    need("inv.act", "xt")
                    need("inv.dve", "xtb")
                    need("inv.act", "e")
                    inv(0, bd["m2t"], two(mv, 2), "f", P)
                    inv(3, bd["e"], of(cm["m2"]), "ft")
                    solve(1)
                    need("inv.act", "f")
                    need("inv.dve", "ft")
                    inv(2, bd["m"], of(cm["m2t"]), "f2")
                    tail(1)
                    need("inv.act", "vb")
                    need("inv.act", "x")
                    inv(0, bd["al"], of(stack), "v")
                    need("inv.act", "f2")
                    need("inv.dve", "ift")
                    inv(1, bd["m2"], of(cm["m"]), "h")
                    out(1)
                    need("inv.dve", "mv")
                    inv(2, bd["be"], two(mv, 1), "rb", P)
                    need("inv.act", "ka")
                    need("inv.act", "v")
                    need("inv.dve", "h")
                    inv(0, bd["ka"], two(mv, 0), "ak", P)
                    need("inv.dve", "rb")
                    need("inv.act", "bt")
                    inv(2, bd["mt"], of(cm["mt"]), "w")
                    inv(3, bd["ka"], of(stack), "kt")

                pe.wait_ge(sem("products_ready"), 6)
                chunks(0, None)
                with pe.Fori(1, NCH // 2) as it:
                    chunks(it, it - 1)
                chunks(None, NCH // 2 - 1)
                after(pe, "rec.dve", NCH // 2 - 1, "ud1")
                after(pe, "rec.act", NCH // 2 - 1, "out1")
                for j in range(GT):
                    last = turn(psum[0:HD, 6, j * P:(j + 1) * P], uc[:, j, :])
                last.then_inc(sem("state_turned"), 1)
                centre(1, X[3])
                head_stat0(2)
                pe.wait_ge(sem("rkk_ready"), 1)
                for j in range(GT):
                    pe.wait_ge(stat_used, 12)
                    if j >= 2:
                        pe.wait_ge(sem("bonus_used"), j - 1)
                    for e in range(2):
                        last = mm(halves(4 * (j % 2))[:, e, :], C("bones"), A[2][:, j, e * TH:(e + 1) * TH], start=True, stop=True)
                    last.then_inc(sem("bonus_ready"), 1)

            def head_stat0(g):
                pe.wait_ge(cen_copied, 8 * (g // 2 + 1))
                stat_body(g, A[1] if g == 0 else FA[1], C("hsel"))

            def stat_body(g, src, sel):
                w = sel.shape[1]
                for j in range(GT):
                    for x, t0 in enumerate(TOK_TILES):
                        last = mm(psum[:, 7, (x * GT + j) * w:(x * GT + j + 1) * w], src[:, j, t0:t0 + P], sel,
                                  start=(j == 0 and x == 0), stop=(j == GT - 1), skip_group_check=True)
                last.then_inc(stat_summed, 1)
                pe.wait_ge(stat_ready, g + 1)
                r = st_rs[:, 0:20 * w].rearrange("p (x j s) -> p x j s", j=GT, s=w)
                for j in range(GT):
                    if 4 * g + j >= 2:
                        pe.wait_ge(stat_used, 4 * g + j - 1)
                    spread(4 * (j % 2), r[:, :, j, :], stat_spread)

            def odd_mix():
                q, k, v = A[0], A[1], A[2]
                for s in range(2):
                    pe.wait_ge(psum_free[s], TB[("mix_in", 1)] // 2 + 10)
                for j in range(GT):
                    last = turn(psum[0:11, 6, j * P:(j + 1) * P], A[3][:, j, SEQ - 3:T])
                last.then_inc(sem("lconv_turned"), 1)
                pe.wait_ge(sem("lruw_loaded"), 16 * 4)
                pe.wait_ge(sem("xc_ready"), 1)
                for n in range(8):
                    if n >= 2:
                        pe.wait_ge(sem("gates_copied"), n - 1)
                    for e in range(2):
                        last = mm(halves(4 * (n % 2))[:, e, :], (wabd, wibd)[n // 4][:, n % 4, :], X[0][:, n % 4, e * TH:(e + 1) * TH], start=True, stop=True)
                    last.then_inc(sem("gates_ready"), 1)
                pe.wait_ge(sem("gates_copied"), 8)
                for x in range(5):
                    w = P if x < 4 else NS
                    if x >= 2:
                        pe.wait_ge(sem("kv_copied"), 2 * (x - 1))
                    for n, a in enumerate((v, k)):
                        for j in range(GT):
                            last = turn(psum[0:w, 2 * (x % 2) + n, j * P:(j + 1) * P], a[:, j, x * P:x * P + w])
                    last.then_inc(sem("kv_turned"), 1)
                for j in range(GT):
                    last = turn(psum[0:NS, 4, j * P:(j + 1) * P], q[:, j, SEQ:T])
                last.then_inc(sem("qs_turned"), 1)
                pe.wait_ge(sem("lruh_ready"), 1)
                for j in range(GT):
                    last = turn(psum[0:9, 5, j * P:(j + 1) * P], FA[0][:, j, SEQ - 1:T])
                last.then_inc(sem("lruh_turned"), 1)
                pe.wait_ge(sem("qs_copied"), 1)
                pe.wait_ge(sem("lruh_copied"), 1)
                pe.wait_ge(sem("kv_copied"), 10)

                def query(b, bk):
                    mm(bank(bk), ident[0:NS, b:b + 1].to_broadcast([NS, P]), qs8[:, :], start=True, stop=True).then_inc(sem("qb_ready"), 1)

                for b in range(POOLED):
                    query(b, 4 + b)

                def scores(n):
                    i, j = n // 4, n % 4
                    if n >= 2:
                        pe.wait_ge(sem("exp_done"), 2 * (n - 1))
                    for m in range(2):
                        hp = slice(m * HD, (m + 1) * HD)
                        last = mm(psum[:, 2 * (n % 2) + m, 0:(i + 1) * P], q[hp, j, i * P:(i + 1) * P], k[hp, j, 0:(i + 1) * P], start=True, stop=True)
                    last.then_inc(sem("qk2_ready"), 1)

                def values(n):
                    i, j = n // 4, n % 4
                    pe.wait_ge(sem("wt_copied"), n + 1)
                    if n >= 2:
                        pe.wait_ge(sem("oc_copied"), n - 1)
                    for x in range(i + 1):
                        last = mm(psum[:, 6 + n % 2, 0:P], vtm[:, x, j * P:(j + 1) * P], wtp[:, n % 2, x * P:(x + 1) * P], start=(x == 0), stop=(x == i))
                    last.then_inc(sem("pv2_done"), 1)

                scores(0)
                scores(1)
                for n in range(16):
                    if n < 14:
                        scores(n + 2)
                    if n >= 1:
                        values(n - 1)
                    pe.wait_ge(sem("w_ready"), n + 1)
                    if n == 0:
                        pe.wait_ge(sem("qb_copied"), POOLED)
                    if n >= 2:
                        pe.wait_ge(sem("wt_copied"), n - 1)
                    for x in range(n // 4 + 1):
                        last = turn(psum[:, 4 + n % 2, x * P:(x + 1) * P], probs[:, n % 2, 0, x * P:(x + 1) * P])
                    last.then_inc(sem("wt_turned"), 1)
                values(15)
                pe.wait_ge(sem("oc_copied"), 16)
                for b in range(POOLED, NS):
                    if b >= POOLED + 2:
                        pe.wait_ge(sem("qb_used"), b - POOLED - 1)
                    query(b, b % 2)
                pe.wait_ge(sem("sdec_ready"), NS - POOLED + 1)
                pe.wait_ge(sem("pool_keys"), 7 * POOLED)
                for m in range(2):
                    for x in range(PAGES):
                        turn(psum[0:32, 2 + m, x * P:(x + 1) * P], sdec[:, m, x, :, :].rearrange("p b h -> p (b h)"))
                mm(psum[0:32, 4, 0:2], prodn[:, :, :].rearrange("p b h -> p (b h)"), C("bsel"), start=True, stop=True).then_inc(sem("sd_turned"), 1)
                pe.wait_ge(sem("wd_ready"), 1)
                for x in range(PAGES):
                    turn(psum[:, 5, x * 32:(x + 1) * 32], pdec[:, 0, x * P:(x + 1) * P])
                mm(psum[:, 6, 0:32], C("ones2")[0:32, 0:1].to_broadcast([32, P]), wdiag[:, :], start=True, stop=True).then_inc(sem("wd_turned"), 1)
                pe.wait_ge(sem("wtd_copied"), 1)
                for b in range(NS):
                    g = VD_GROUP[b]
                    pe.wait_ge(sem(f"vd_loaded{g}"), 64 * VD_GROUP.count(g))
                    for x in range(PAGES):
                        last = mm(psum[0:32, 4, :], wtz[:, x, b * 32:(b + 1) * 32], vd[b][:, x, :], start=(b == 0 and x == 0), stop=(b == NS - 1 and x == PAGES - 1))
                last.then_inc(sem("vd_used"), 1)
                pe.wait_ge(sem("wtd_copied"), 2)
                for j in range(4):
                    last = turn(psum[:, 7, j * 32:(j + 1) * 32], odec[:, j * P:(j + 1) * P])
                last.then_inc(sem("vd_used"), 1)
                pe.wait_ge(sem("oc_sq"), 1)
                stat_body(3, X[1], C("ones2")[:, 0:1])

            pe.wait_ge(sem("inputs_loaded"), 16 * (NROWS - 10))
            pe.wait_ge(sem("x_loaded"), 16 * 16)
            for n, (dst, rows) in enumerate(row_tables):
                last = turn(psum[:, 6, n * P:n * P + rows.shape[0]], rows[:, :])
            last.then_inc(sem("rows_turned"), 1)
            for k in range(KT):
                b = 4 * (k % 2)
                if k >= 2:
                    pe.wait_ge(h_ready, k - 1)
                for x in range(4):
                    turn(psum[:, b, x * P:(x + 1) * P], stage[:, x, k * P:(k + 1) * P])
                turn(psum[:, b + 1, 0:NS], stage_s[:, k * P:(k + 1) * P]).then_inc(sem("xt_turned"), 1)
            for i in range(2):
                ffn(i, 0)
                norm(NORM[(i, 1)])
                proj(("mix_in", i), NORM[(i, 2)])
                (even_mix if i == 0 else odd_mix)()
                proj(("mix_out", i), None, i)
                norm(NORM[(i, 3)])
                ffn(i, 1)
                norm(NORM[(i, 5)])
                proj(("gate", i), NORM[(i, 6)])
                pe.wait_ge(psum_free[1], TB[("ple", i)] // 2)
                pe.wait_ge(psum_free[0], TB[("ple", i)] // 2)
                pe.wait_ge(sem("p_loaded"), 32 * (i + 1))
                for k in range(2):
                    for x in range(4):
                        turn(psum[:, 2 + 4 * k, x * P:(x + 1) * P], pst[:, x, k * P:(k + 1) * P])
                    last = turn(psum[:, 3 + 4 * k, 0:NS], pss[:, k * P:(k + 1) * P])
                last.then_inc(sem("p_turned"), 1)
                pe.wait_ge(sem("plo_ready"), 2 * (i + 1))
                for e in range(4):
                    for m in range(2):
                        free(m, TB[("ple", i)] // 2 + e)
                        unit(UB[("ple", i)] + e, e, halves(4 * m), phi, plo, nk=2, width=256, c0=m * P, last=(m == 1))
                norm(NORM[(i, 7)])
            pe.wait_ge(h_ready, 8 * 9)
            for x in range(5):
                w = P if x < 4 else NS
                if x >= 2:
                    pe.wait_ge(sem("y_copied"), x - 1)
                for k in range(KT):
                    last = turn(psum[0:w, 4 * (x % 2) + k // 4, (k % 4) * P:(k % 4 + 1) * P], h[:, k, x * P:x * P + w])
                last.then_inc(sem("y_turned"), 1)

        @block.scalar
        def _(act):
            own = Steps(act, sem("act_steps"))
            fn = nc.scalar.activation

            def ahead(u, r, lead=3):
                u, r = u + lead, r + lead
                if isinstance(u, int) and u >= NU:
                    return
                s = r % 4
                act.wait_ge(raw_loaded[s], 16 * (u // 4 + 1) if isinstance(u, int) else (u - s) * 4 + 16)
                if not isinstance(u, int) or u >= 4:
                    act.wait_ge(unit_used, u - 3)
                fn(whi[s][:, 0:raw_cols(u)], raw[s][:, 0:raw_cols(u)], ACT.Copy).then_inc(hi_ready, 1)

            def square(n, k, src):
                static = isinstance(k, int)
                if not static or k >= 3:
                    act.wait_ge(sq_used, k + ((KT - 2) * n - 2))
                odd = k % 2 if static else src[1]
                src = one(src, k) if static else one(src[0], k)
                fn(sgt[:, 0, :] if static and k == 0 else sq[:, odd, :], src, ACT.Square).then_inc(sq_ready, 1)

            def root(n):
                act.wait_ge(sq_summed, n + 1)
                fn(rs5, psum[:, 7, 16:21], ACT.Sqrt, scale=1.0 / D, bias=eps_col).then_inc(sd_ready, 1)

            def ffn(i, a):
                for r in range(2):
                    name = ("in", i, a, r)
                    u0, p0, g0 = UB[name], PAIRS[name], SG[name]

                    def body(it):
                        for p in range(2):
                            for g in range(2):
                                ahead(it * 4 + (u0 + 2 * p + g), 2 * p + g)
                            pr = it * 2 + (p0 + p)
                            act.wait_ge(gate_scaled, pr + 1)
                            fn(sgt[:, p, :], sgt[:, p, :], ACT.Silu).then_inc(sg_ready, 1)
                            act.wait_ge(hid_ready, pr * 2 + 2)
                            fn(one(ghi, it * 2 + p), sgt[:, 2 + p, :], ACT.Copy).then_inc(hhi_ready, 1)

                    if u0 == 0:
                        body(0)
                    with act.Fori(1 if u0 == 0 else 0, 8) as it:
                        body(it)
                    name = ("out", i, a, r)
                    uo = UB[name]
                    if r == 0:
                        with act.Fori(0, 4) as it:
                            for m in range(4):
                                ahead(it * 4 + (uo + m), m)
                    else:
                        n = NORM[(i, 1 if a == 0 else 5)]

                        def obody(it):
                            for m in range(4):
                                ahead(it * 4 + (uo + m), m)
                                if m >= 2:
                                    p = m - 2
                                    act.wait_ge(psum_free[p], it + (TB[name] // 2 + 1))
                                    square(n, it * 2 + p, f if isinstance(it, int) else (f, p))

                        obody(0)
                        with act.Fori(1, 4) as it:
                            obody(it)

            def pre(n):
                for k in range(KT):
                    act.wait_ge(h_ready, 8 * (n // 2) + k + 1)
                    fn(xhi[:, k, :], h[:, k, :], ACT.Copy, scale=gcol[:, n * 8 + k:n * 8 + k + 1]).then_inc(xh_ready, 1)
                    square(n, k, h)
                root(n)

            def stat_root(g, n, scale, eps):
                act.wait_ge(stat_summed, g + 1)
                fn(st_sd[:, 0:n], psum[:, 7, 0:n], ACT.Sqrt, scale=scale, bias=eps).then_inc(stat_rooted, 1)

            def centred(g, xc, xs):
                for j in range(GT):
                    act.wait_ge(cen_ready, 4 * g + j + 1)
                    fn(tok(xc[:, j, :]), halves(4 * (j % 2)), ACT.Copy).then_inc(cen_copied, 1)
                    fn(tok(xs[:, j, :]), halves(4 * (j % 2)), ACT.Square).then_inc(cen_copied, 1)

            def cat_hi(k, src):
                fn(xhi[:, k, :], src[:, k % 4, :], ACT.Copy).then_inc(cath_ready, 1)

            def even_mix():
                act.wait_ge(sem("shift_turned"), 1)
                for n in range(4):
                    fn(shst[:, 4 * n:4 * n + 4, :].rearrange("p a b -> p (a b)"), psum[0:9, n, :], ACT.Copy).then_inc(sem("shift_copied"), 1)
                for i in range(4):
                    act.wait_ge(sem("tk_turned"), i + 1)
                    if i:
                        act.wait_ge(sem("pv_done"), i)
                    for n, x in enumerate((ktok, vtok)):
                        fn(x[:, :, :].rearrange("p a b -> p (a b)"), bank(n), ACT.Copy).then_inc(sem("tk_copied"), 1)
                    act.wait_ge(sem("pv_done"), i + 1)
                    fn(A[0][:, :, i * P:(i + 1) * P], psum[:, 4, :].rearrange("p (a b) -> p a b", a=GT), ACT.Copy).then_inc(sem("o_copied"), 1)
                act.wait_ge(sem("vs_turned"), 1)
                fn(vs8[:, :], psum[0:NS, 6, :], ACT.Copy).then_inc(sem("vs8_ready"), 1)
                act.wait_ge(sem("os_ready"), 1)
                for hh in range(2):
                    hp = slice(hh * HD, (hh + 1) * HD)
                    fn(A[0][hp, :, SEQ:T], psum[hp, 2 + hh, 0:GT * NS].rearrange("p (a b) -> p a b", a=GT), ACT.Copy).then_inc(sem("o_copied"), 1)
                centred(0, A[2], A[1])
                stat_root(0, 40, 1.0, eps_col)
                fn(A[3][:, :, :], A[3][:, :, :], ACT.Silu).then_inc(sem("silu_ready"), 1)
                act.wait_ge(sem("l1_ready"), 1)
                fn(tok(tw[:, :]), halves(0)[0:HD], ACT.Tanh).then_inc(sem("l1_copied"), 1)
                act.wait_ge(sem("l1_ready"), 2)
                fn(tok(ta[:, :]), halves(2)[0:HD], ACT.Copy).then_inc(sem("l1_copied"), 1)
                act.wait_ge(sem("l1_ready"), 3)
                fn(tok(tg[:, :]), halves(4), ACT.Sigmoid).then_inc(sem("l1_copied"), 1)
                act.wait_ge(sem("rkv_ready"), 3)
                for n in range(12):
                    j, kind = n % 4, n // 4
                    act.wait_ge(sem("l2_ready"), n + 1)
                    src = halves(4 * (n % 2))
                    if kind == 0:
                        ins = fn(tok(A[2][:, j, :]), src, ACT.Sigmoid, bias=V("w0", j))
                    elif kind == 1:
                        ins = fn(tok(FA[1][:, j, :]), src, ACT.Sigmoid, bias=V("a0", j))
                    else:
                        ins = fn(tok(A[7][:, j, :]), src, ACT.Copy)
                    ins.then_inc(sem("l2_copied"), 1)
                for j in range(GT):
                    act.wait_ge(sem("kk_raw"), j + 1)
                    fn(X[3][:, j, :], FA[0][:, j, :], ACT.Square).then_inc(sem("kk_sq"), 1)
                act.wait_ge(sem("kk_clamped"), 1)
                fn(st_sd[:, 0:40], st_in[:, 0:40], ACT.Sqrt).then_inc(stat_rooted, 1)
                act.wait_ge(sem("cs_ready"), 1)
                fn(A[3][:, :, :], A[5][:, :, :], ACT.Exp, scale=DC).then_inc(sem("dec_ready"), 1)
                fn(A[2][:, :, :], A[2][:, :, :], ACT.Exp, scale=-DC).then_inc(sem("dec_ready"), 1)
                act.wait_ge(sem("dec_ready"), 2)
                fn(A[5][:, :, :], A[5][:, :, :], ACT.Exp, scale=-DC).then_inc(sem("dec_ready"), 1)
                act.wait_ge(sem("rw_turned"), 1)
                for n in range(5):
                    fn(rows8[n][:, :], psum[0:NS, n, :], ACT.Copy).then_inc(sem("rows8_ready"), 1)

                def chunks(it, q):
                    def need(step):
                        if it is not None:
                            after(act, "inv.pe", it, step)

                    def copy(step, src, side=None, diag=None, scale=1.0):
                        if it is None:
                            return
                        if step:
                            need(step)
                        src = eight(bank(src)) if isinstance(src, int) else src
                        if side is not None:
                            ins = fn(side, src, ACT.Copy, scale=scale)
                        for hp in HP if diag is not None else ():
                            ins = fn(diag[hp, :, hp], src[hp], ACT.Copy, scale=scale)
                        ins.then_inc(step_sem["inv.act"], 1)

                    def right(c):
                        if q is not None:
                            after(act, "rec.pe", q, f"rhs{c}")
                            fn(rc[:, :, :], four(bank(4, 256)), ACT.Copy).then_inc(step_sem["rec.act"], 1)

                    def outputs(c):
                        if q is not None:
                            after(act, "rec.pe", q, f"o{c}")
                            for hp in HP:
                                ins = fn(ob[hp, :, hp], four(bank(6, 256))[hp], ACT.Copy)
                            ins.then_inc(step_sem["rec.act"], 1)

                    def channels(c):
                        if q is not None:
                            after(act, "rec.pe", q, f"turn{c}")
                            fn(X[3][:, :, pair_cols(q, c)], four(bank(6, 256)), ACT.Copy).then_inc(step_sem["rec.act"], 1)

                    if it is not None:
                        after(act, "inv.dve", it, "mt")
                        for hp in HP:
                            ins = fn(bd["mt"][hp, :, hp], cm["mt"][hp, :, :], ACT.Copy)
                        ins.then_inc(step_sem["inv.act"], 1)
                    right(0)
                    if it is not None:
                        after(act, "inv.pe", it, "a")
                        for x, src in (("al", X[2]), ("ka", X[1])):
                            for hp in HP:
                                ins = fn(diagonal(bd[x], hp), by_chunk(src[hp, :, pair_cols(it, 0, 2 * CH)]), ACT.Copy)
                            ins.then_inc(step_sem["inv.act"], 1)
                    copy("m2", 2, cm["m2"][:, :, :], bd["m2"])
                    if it is not None:
                        after(act, "inv.dve", it, "e")
                        for hp in HP:
                            ins = fn(bd["e"][hp, :, hp], cm["e"][hp], ACT.Copy)
                        ins.then_inc(step_sem["inv.act"], 1)
                        after(act, "inv.pe", it, "m2t")
                    copy("m4", 0, cm["m"][:, :, :], bd["m"])
                    outputs(0)
                    if it is not None:
                        after(act, "inv.pe", it, "x2")
                    copy("m8", 1, None, bd["m2"])
                    channels(0)
                    right(1)
                    if it is not None:
                        after(act, "inv.dve", it, "xt")
                        fn(bd["m2t"][HP[0], :, HP[0]], cm["m2"][HP[0], :, :], ACT.Copy).then_inc(step_sem["inv.act"], 1)
                    copy("f", two_banks(0, 1), cm["m2t"])
                    copy(None, two_banks(0, 0), None, bd["mt"])
                    copy("f2", 2, None, bd["m2"])
                    outputs(1)
                    copy("v", 0, cm["vc"][:, :, :])
                    channels(1)
                    if it is not None:
                        after(act, "inv.dve", it, "rb")
                    if q is None:
                        act.wait_ge(sem("bd_zeroed"), 18)
                    copy(None, two_banks(2, 1), None, bd["bt"])
                    copy("w", 2, None, bd["wt"], -1.0)
                    copy("kt", 3, None, bd["kt"])

                chunks(0, None)
                with act.Fori(1, NCH // 2) as it:
                    chunks(it, it - 1)
                chunks(None, NCH // 2 - 1)
                for r in range(3):
                    ahead(UB[("mix_out", 0)] + r, r, 0)
                act.wait_ge(sem("state_turned"), 1)
                fn(rwst[:, :, :].rearrange("p a b -> p (a b)"), psum[0:HD, 6, :], ACT.Copy).then_inc(sem("rwst_ready"), 1)
                centred(1, FA[0], FA[1])
                for k in range(4):
                    cat_hi(k, A[0])
                stat_root(2, 40, 1.0, gn_eps_col)
                for k in range(4, 8):
                    act.wait_ge(sem("ob_ready"), k - 3)
                    cat_hi(k, A[7])

            def odd_mix():
                act.wait_ge(sem("lconv_turned"), 1)
                fn(lcst[:, :], psum[0:11, 6, :], ACT.Copy).then_inc(sem("lconv_copied"), 1)
                act.wait_ge(sem("lam_abs"), 1)
                fn(lt[:, 4:8], lt[:, 0:4], ACT.Exp, scale=-1.0).then_inc(sem("lam_ln1p"), 1)
                act.wait_ge(sem("lam_ln1p"), 1)
                fn(lt[:, 8:12], lt[:, 4:8], ACT.Ln, bias=1.0).then_inc(sem("lam_ln1p"), 1)
                act.wait_ge(sem("dlam_sums"), 2)
                fn(lamt[:, 2:4], lamt[:, 0:2], ACT.Exp).then_inc(sem("dlam_exp"), 1)
                for n in range(8):
                    j = n % 4
                    act.wait_ge(sem("gates_ready"), n + 1)
                    fn(tok(X[1 + n // 4][:, j, :]), halves(4 * (n % 2)), ACT.Sigmoid, bias=V("ba" if n < 4 else "bi", j)).then_inc(sem("gates_copied"), 1)
                act.wait_ge(sem("lru_sp_ready"), 1)
                act.wait_ge(sem("gates_copied"), 8)
                for j in range(GT):
                    fn(X[3][:, j, :], X[1][:, j, :], ACT.Tanh, scale=lru_sp[:, j:j + 1]).then_inc(sem("lru_decays"), 1)
                for j in range(GT):
                    fn(X[1][:, j, :], X[1][:, j, :], ACT.Exp, scale=lru_nsp[:, j:j + 1]).then_inc(sem("lru_decays"), 1)
                act.wait_ge(sem("lru_v"), 1)
                fn(X[3][:, :, :], X[3][:, :, :], ACT.Sqrt).then_inc(sem("lru_root"), 1)
                fn(A[4][:, :, :], A[4][:, :, :], ACT.Gelu_apprx_tanh).then_inc(sem("gelu_ready"), 1)
                for x in range(5):
                    w = P if x < 4 else NS
                    act.wait_ge(sem("kv_turned"), x + 1)
                    for n in range(2):
                        dst = (vtm, ktm)[n][:, x, :] if x < 4 else (vs8o, ks8)[n][:, :]
                        fn(dst, psum[0:w, 2 * (x % 2) + n, :], ACT.Copy).then_inc(sem("kv_copied"), 1)
                act.wait_ge(sem("qs_turned"), 1)
                fn(qs8[:, :], psum[0:NS, 4, :], ACT.Copy).then_inc(sem("qs_copied"), 1)
                act.wait_ge(sem("lruh_turned"), 1)
                fn(lhst[:, :], psum[0:9, 5, :], ACT.Copy).then_inc(sem("lruh_copied"), 1)
                act.wait_ge(sem("lru_done"), 1)
                for b in range(POOLED):
                    act.wait_ge(sem("qb_ready"), b + 1)
                    fn(qb[:, b, :], bank(4 + b), ACT.Copy).then_inc(sem("qb_copied"), 1)
                def exps(n):
                    nk = (n // 4 + 1) * P
                    act.wait_ge(sem("mx_ready"), n + 1)
                    if n >= 2:
                        act.wait_ge(sem("wt_turned"), n - 1)
                    for m in range(2):
                        fn(probs[:, n % 2, m, 0:nk], psum[:, 2 * (n % 2) + m, 0:nk], ACT.Exp, bias=nb2s[n % 2][:, m:m + 1], scale=HD ** -0.5,
                           accum_out=l2s[n % 2][:, m:m + 1]).then_inc(sem("exp_done"), 1)

                def out(n):
                    i, j = n // 4, n % 4
                    act.wait_ge(sem("pv2_done"), n + 1)
                    fn(A[0][:, j, i * P:(i + 1) * P], psum[:, 6 + n % 2, 0:P], ACT.Copy).then_inc(sem("oc_copied"), 1)

                exps(0)
                exps(1)
                for n in range(16):
                    nk = (n // 4 + 1) * P
                    act.wait_ge(sem("wt_turned"), n + 1)
                    fn(wtp[:, n % 2, 0:nk], psum[:, 4 + n % 2, 0:nk], ACT.Copy).then_inc(sem("wt_copied"), 1)
                    if n >= 1:
                        out(n - 1)
                    if n < 14:
                        exps(n + 2)
                out(15)
                act.wait_ge(sem("mxn_ready"), 1)
                for m in range(2):
                    fn(pdec[:, m, :], psum[0:32, 2 + m, :], ACT.Exp, bias=mxn[0:32, m:m + 1], scale=HD ** -0.5,
                       accum_out=l2[0:32, m:m + 1]).then_inc(sem("expd_done"), 1)
                    fn(pn2[0:32, m:m + 1], psum[0:32, 4, m:m + 1], ACT.Exp, bias=mxn[0:32, m:m + 1], scale=HD ** -0.5).then_inc(sem("expd_done"), 1)
                act.wait_ge(sem("wd_turned"), 1)
                fn(wtz[:, :, :].rearrange("p x (b c) -> p x b c", c=36)[:, :, :, 0:4], psum[:, 5, 0:128].rearrange("p (x b c) -> p x b c", x=PAGES, b=NS), ACT.Copy).then_inc(sem("wtd_copied"), 1)
                act.wait_ge(sem("vd_used"), 1)
                fn(odec[:, :], psum[0:32, 4, :], ACT.Copy).then_inc(sem("wtd_copied"), 1)
                act.wait_ge(sem("os2_ready"), 1)
                fn(X[1][:, :, :], A[0][:, :, :], ACT.Square).then_inc(sem("oc_sq"), 1)
                for r in range(3):
                    ahead(UB[("mix_out", 1)] + r, r, 0)
                stat_root(3, 20, 1.0 / P, eps_col)
                for k in range(4, 8):
                    cat_hi(k, A[4])
                for k in range(4):
                    act.wait_ge(stat_used, 13 + k)
                    cat_hi(k, A[0])

            def just_ahead(name, n, stop=False):
                with act.Fori(0, n - stop) as it:
                    for m in range(4):
                        ahead(it * 4 + (UB[name] + m), m)
                if stop:
                    ahead(UB[name] + 4 * (n - 1), 0)

            def mix_out(i):
                name, n = ("mix_out", i), NORM[(i, 3)]

                def body(it):
                    for m in range(4):
                        ahead(it * 4 + (UB[name] + m), m)
                        act.wait_ge(psum_free[m % 2], it * 2 + (TB[name] // 2 + m // 2 + 1))
                        square(n, it * 4 + m, f if isinstance(it, int) else (f, m % 2))

                body(0)
                body(1)

            def gate(i):
                name = ("gate", i)
                with act.Fori(0, 2) as it:
                    for m in range(4):
                        ahead(it * 4 + (UB[name] + m), m)
                        act.wait_ge(psum_free[m % 2], it * 2 + (TB[name] // 2 + m // 2 + 1))
                        fn(one(f, it * 4 + m), one(f, it * 4 + m), ACT.Sigmoid).then_inc(sg_ready, 1)

            act.dma_start(cst[:, :], I["consts"]).then_inc(sem("x_loaded"), 16)
            for x in range(4):
                act.dma_start(stage[:, x, :], I["x_prompt"][0, x * P:(x + 1) * P]).then_inc(sem("x_loaded"), 16)
            act.dma_start(stage_s[:, :], I["x_sample"][:, 0, :]).then_inc(sem("x_loaded"), 16)
            for r in range(3):
                ahead(r, r, 0)
            act.wait_ge(sem("eps_set"), 2)
            for i in range(2):
                pre(NORM[(i, 0)])
                ffn(i, 0)
                root(NORM[(i, 1)])
                pre(NORM[(i, 2)])
                just_ahead(("mix_in", i), NT[("mix_in", i)] // 4, True)
                (even_mix if i == 0 else odd_mix)()
                mix_out(i)
                root(NORM[(i, 3)])
                pre(NORM[(i, 4)])
                ffn(i, 1)
                root(NORM[(i, 5)])
                pre(NORM[(i, 6)])
                gate(i)
                act.wait_ge(sem("p_turned"), i + 1)
                for k in range(2):
                    b = (2 + 4 * k) * 512
                    fn(phi[:, k, :], flat[:, b:b + T], ACT.Copy).then_inc(sem("phi_ready"), 1)
                for e in range(4):
                    ahead(UB[("ple", i)] + e, e)
                    for m in range(2):
                        act.wait_ge(psum_free[m], TB[("ple", i)] // 2 + e + 1)
                        square(NORM[(i, 7)], 2 * e + m, f)
                root(NORM[(i, 7)])

        @block.vector
        def _(dve):
            own = Steps(dve, sem("dve_steps"))
            tt, ts, stt = nc.vector.tensor_tensor, nc.vector.tensor_scalar, nc.vector.scalar_tensor_tensor

            def ahead(u, r, lead=3):
                u, r = u + lead, r + lead
                if isinstance(u, int) and u >= NU:
                    return
                s, w = r % 4, raw_cols(u)
                dve.wait_ge(hi_ready, u + 1)
                tt(wlo[s][:, 0:w], raw[s][:, 0:w], whi[s][:, 0:w].bitcast(F32), ALU.subtract).then_inc(lo_ready, 1)

            def ffn(i, a):
                for r in range(2):
                    name = ("in", i, a, r)
                    u0, p0 = UB[name], PAIRS[name]
                    with dve.Fori(0, 8) as it:
                        for p in range(2):
                            for g in range(2):
                                ahead(it * 4 + (u0 + 2 * p + g), 2 * p + g)
                            pr = it * 2 + (p0 + p)
                            dve.wait_ge(unit_used, it * 4 + (u0 + 2 * p + 1))
                            tt(tok(sgt[:, p, :]), halves(4 * p), tok(rbk), ALU.mult).then_inc(gate_scaled, 1)
                            dve.wait_ge(unit_used, it * 4 + (u0 + 2 * p + 2))
                            tt(tok(sgt[:, 2 + p, :]), halves(4 * p + 2), tok(rbk), ALU.mult).then_inc(hid_ready, 1)
                            dve.wait_ge(sg_ready, it * 2 + (SG[name] + p + 1))
                            dve.wait_ge(hid_ready, pr * 2 + 1)
                            tt(sgt[:, 2 + p, :], sgt[:, p, :], sgt[:, 2 + p, :], ALU.mult).then_inc(hid_ready, 1)
                            dve.wait_ge(hhi_ready, pr + 1)
                            tt(one(glo, it * 2 + p), sgt[:, 2 + p, :], one(ghi, it * 2 + p).bitcast(F32), ALU.subtract).then_inc(psum_free[p], 1)
                    name = ("out", i, a, r)
                    uo = UB[name]
                    with dve.Fori(0, 4) as it:
                        for m in range(2):
                            for g in range(2):
                                ahead(it * 4 + (uo + 2 * m + g), 2 * m + g)
                            dve.wait_ge(unit_used, it * 4 + (uo + 2 * m + 2))
                            dst = one2(f, it * 2 + m)
                            if r == 0:
                                ins = nc.vector.tensor_copy(dst, halves(4 * m))
                            else:
                                ins = tt(dst, halves(4 * m), dst, ALU.add)
                            ins.then_inc(psum_free[m], 1)

            RB = flat[:, 6 * 512:6 * 512 + T]

            def rstd(n):
                dve.wait_ge(sd_ready, n + 1)
                nc.vector.reciprocal(rs5b, rs5).then_inc(rs_ready, 1)
                dve.wait_ge(rb_ready, n + 1)

            def gained_lo(n, k):
                dve.wait_ge(xh_ready, 8 * (n // 2) + k + 1)
                stt(xlo[:, k, :], h[:, k, :], gcol[:, n * 8 + k:n * 8 + k + 1], xhi[:, k, :].bitcast(F32), ALU.mult, ALU.subtract).then_inc(xn_ready, 1)

            def keep_rate(n):
                rstd(n)
                nc.vector.tensor_copy(rbk, RB).then_inc(rb_kept, 1)
                dve.wait_ge(rb_kept, n // 2 + 1)

            def post(n, last=False):
                rstd(n)
                for k in range(KT + 2):
                    if k < KT:
                        own(stt(f[:, k, :], f[:, k, :], gcol[:, n * 8 + k:n * 8 + k + 1], RB, ALU.mult, ALU.mult))
                    if 1 <= k <= KT:
                        dve.wait_ge(own.sem, own.n - (1 if k < KT else 0))
                        tt(h[:, k - 1, :], h[:, k - 1, :], f[:, k - 1, :], ALU.add).then_inc(h_ready, 1)
                    if k >= 2 and not last:
                        gained_lo(n + 1, k - 2)

            def stat_rate(g, n):
                dve.wait_ge(stat_rooted, g + 1)
                nc.vector.reciprocal(st_rs[:, 0:n], st_sd[:, 0:n]).then_inc(stat_ready, 1)

            def spread_mul(g, dst, src, gain=None):
                for j in range(GT):
                    dve.wait_ge(stat_spread, 4 * g + j + 1)
                    rb = flat[:, 4 * (j % 2) * 512:4 * (j % 2) * 512 + T]
                    if gain is None:
                        tt(dst[:, j, :], src[:, j, :], rb, ALU.mult).then_inc(stat_used, 1)
                    else:
                        stt(dst[:, j, :], src[:, j, :], gain, rb, ALU.mult, ALU.mult).then_inc(stat_used, 1)
                dve.wait_ge(stat_used, 4 * (g + 1))

            def cat_lo(i, k, src):
                dve.wait_ge(cath_ready, 8 * i + CAT_ORDER[i].index(k) + 1)
                tt(xlo[:, k, :], src[:, k % 4, :], xhi[:, k, :].bitcast(F32), ALU.subtract).then_inc(cat_ready, 1)

            def even_mix():
                q, k, v = A[0], A[1], A[2]
                dve.wait_ge(sem("tables_loaded"), 32)
                for n in range(8):
                    j, x = n % 4, A[n // 4]
                    dve.wait_ge(sem("rot_ready"), n + 1)
                    tt(tok(X[1][:, j, :]), halves(4 * (n % 2)), tok(rope[:, 1, :]), ALU.mult).then_inc(sem("rot_used"), 1)
                    own(tt(x[:, j, :], x[:, j, :], rope[:, 0, :], ALU.mult))
                    own.settle()
                    dve.wait_ge(sem("rot_used"), n + 1)
                    own(tt(x[:, j, :], x[:, j, :], X[1][:, j, :], ALU.add))
                    own.settle()
                    tt(x[:, j, :], x[:, j, :], decay[:, n // 4, j, :], ALU.mult).then_inc(sem("qk_ready"), 1)
                r_, k_, v_, z_ = A[4], A[5], A[6], A[7]

                def shift(x, n, d):
                    own(ts(d[:, :, 0:1], x[:, :, 0:1], -1.0, None, ALU.mult))
                    own(tt(d[:, :, 1:SEQ], x[:, :, 0:SEQ - 1], x[:, :, 1:SEQ], ALU.subtract))
                    own(tt(d[:, :, SEQ:T], shcol[:, :].rearrange("p (b j) -> p j b", b=NS)[:, 4 * n:4 * n + 4, :], x[:, :, SEQ:T], ALU.subtract))
                    own.settle()

                def lerp(dst, x, d, mu, signal):
                    for j in range(GT):
                        stt(dst[:, j, :], d[:, j, :], V("mu", 4 * mu + j), x[:, j, :], ALU.mult, ALU.add).then_inc(signal, 1)

                dve.wait_ge(sem("qk_ready"), 8)
                for i in range(4):
                    dve.wait_ge(sem("sc_ready"), i + 1)
                    if i:
                        dve.wait_ge(sem("pv_done"), i)
                    for hh in range(2):
                        tt(att[:, hh, :, :], psum[:, 2 + hh, :].rearrange("p (a b) -> p a b", a=GT),
                           C("causal_t").rearrange("p (o b) -> p o b", o=1).to_broadcast([P, GT, P]), ALU.mult).then_inc(sem("att_ready"), 1)
                    if i < 3:
                        x, dst = ((r_, X[0]), (k_, X[1]), (v_, X[2]))[i]
                        shift(x, i, FA[0])
                        for j in range(GT):
                            own(stt(dst[:, j, :], FA[0][:, j, :], V("mu", 4 * i + j), x[:, j, :], ALU.mult, ALU.add))
                        own.settle()
                    else:
                        shift(z_, 3, FA[0])
                        lerp(FA[1], z_, FA[0], 3, sem("z_ready"))
                        lerp(X[3], z_, FA[0], 4, sem("z_ready"))
                    dve.wait_ge(sem("pv_done"), i + 1)
                    dve.wait_ge(sem("ubd_ready"), i + 1)
                    for hh in range(2):
                        hp = slice(hh * HD, (hh + 1) * HD)
                        ins = tt(ubd[hp, :, hp], ubd[hp, :, hp], psum[hp, 5, :].rearrange("p (a b) -> p a b", a=GT)[:, :, hp], ALU.add)
                        own(ins) if hh == 0 else ins.then_inc(sem("ubd_ready"), 1)
                    own.settle()
                dve.wait_ge(sem("ubd_ready"), 5)
                for hh in range(2):
                    hp = slice(hh * HD, (hh + 1) * HD)
                    tt(uout[hp, :, :], ubd[hp, :, hp], C("g511")[hp].rearrange("p (a o) -> p a o", o=1).to_broadcast([HD, GT, HD]), ALU.mult).then_inc(sem("uout_ready"), 1)
                dve.wait_ge(sem("sret_loaded"), 16 * GT)
                for j in range(GT):
                    dve.wait_ge(sem("vb_ready"), j + 1)
                    if j:
                        dve.wait_ge(sem("sret_ready"), j)
                    tt(kvt[:, :, :], psum[:, j % 2, :].rearrange("p (b v) -> p b v", b=NS),
                       k[:, j, SEQ:T].rearrange("p (b o) -> p b o", o=1).to_broadcast([P, NS, HD]), ALU.mult).then_inc(sem("vb_used"), 1)
                    dve.wait_ge(sem("vb_used"), j + 1)
                    stt(s_ret[:, j, :, :], s_ret[:, j, :, :], C("gam")[:, j:j + 1], kvt[:, :, :], ALU.mult, ALU.add).then_inc(sem("sret_ready"), 1)
                stat_rate(0, 40)
                lerp(A[1], z_, FA[0], 5, sem("z_ready"))
                spread_mul(0, A[2], A[2])
                dve.wait_ge(sem("silu_ready"), 1)
                tt(A[0][:, :, :], A[2][:, :, :], A[3][:, :, :], ALU.mult).then_inc(sem("oa_ready"), 1)
                dve.wait_ge(sem("oa_ready"), 1)
                nc.vector.memset(small[:, 190:191], 0.0).then_inc(sem("rkv_ready"), 3)
                for j in range(GT):
                    dve.wait_ge(sem("z_ready"), 12)
                    ts(FA[0][:, j, :], X[1][:, j, :], V("kk", j), None, ALU.mult).then_inc(sem("kk_raw"), 1)
                dve.wait_ge(stat_summed, 2)
                own(ts(st_in[:, 0:40], psum[:, 7, 0:40], 1e-24, None, ALU.max))
                own.settle()
                nc.vector.memset(small[:, 190:191], 0.0).then_inc(sem("kk_clamped"), 1)
                own(ts(omka, vcol[:, VEC["ka"][0]:VEC["ka"][0] + 4], -1.0, 1.0, ALU.mult, ALU.add))
                own.settle()
                dve.wait_ge(sem("l2_copied"), 8)
                for j in range(GT):
                    own(ts(A[4][:, j, :], FA[1][:, j, :], V("ka", j), omka[:, j:j + 1], ALU.mult, ALU.add))
                own.settle()
                own(tt(X[1][:, :, :], X[1][:, :, :], A[4][:, :, :], ALU.mult))
                stat_rate(1, 40)
                spread_mul(1, FA[0], FA[0])
                own(tt(FA[1][:, :, :], FA[1][:, :, :], FA[0][:, :, :], ALU.mult))
                dve.wait_ge(sem("tables_loaded"), 48)
                for j in range(GT):
                    own(nc.vector.tensor_tensor_scan(A[5][:, j, 0:SEQ], reset[:, :], A[2][:, j, 0:SEQ], 0.0, ALU.mult, ALU.add))
                own(nc.vector.tensor_copy(A[5][:, :, SEQ:T], A[2][:, :, SEQ:T]))
                own.settle()
                own(tt(A[2][:, :, :], A[5][:, :, :], A[2][:, :, :], ALU.subtract))
                own.settle()
                dve.wait_ge(sem("l2_copied"), 12)
                nc.vector.memset(small[:, 190:191], 0.0).then_inc(sem("cs_ready"), 1)
                dve.wait_ge(sem("dec_ready"), 3)
                nc.vector.memset(small[:, 190:191], 0.0).then_inc(sem("rw_ready"), 1)
                tt(FA[0][:, :, 0:SEQ], FA[0][:, :, 0:SEQ], A[2][:, :, 0:SEQ], ALU.mult).then_inc(sem("products_ready"), 1)
                tt(FA[1][:, :, 0:SEQ], FA[1][:, :, 0:SEQ], A[3][:, :, 0:SEQ], ALU.mult).then_inc(sem("products_ready"), 1)
                nc.vector.tensor_copy(dcol, A[5][:, :, CH - 1:SEQ:CH]).then_inc(sem("products_ready"), 1)
                dve.wait_ge(sem("srw_loaded"), 16 * GT)
                bcn = [0]

                def bc():
                    bcn[0] += 1
                    dve.wait_ge(sem("bc_ready"), bcn[0])
                    return psum[:, (bcn[0] - 1) % 6, :].rearrange("p (b k) -> p b k", b=NS)

                def col(x):
                    return x.rearrange("p (b o) -> p b o", o=1).to_broadcast([P, NS, HD])

                for j in range(GT):
                    S = s_rw[:, j, :, :]
                    t0, t1 = swt[0][:, :, :], swt[1][:, :, :]

                    def step(ins):
                        ins.then_inc(sem("bc_used"), 1)
                        dve.wait_ge(sem("bc_used"), bcn[0])

                    def mine(ins):
                        own(ins)
                        own.settle()

                    step(tt(t0, S, bc(), ALU.mult))
                    mine(nc.vector.tensor_reduce(sa8[:, :], t0, axis=AX.X, op=ALU.add))
                    step(tt(S, S, bc(), ALU.mult))
                    step(tt(t1, bc(), col(sa8[:, :]), ALU.mult))
                    mine(tt(S, S, t1, ALU.subtract))
                    step(tt(t0, bc(), col(X[2][:, j, SEQ:T]), ALU.mult))
                    mine(tt(S, S, t0, ALU.add))
                    step(tt(t1, S, bc(), ALU.mult))
                    mine(nc.vector.tensor_reduce(X[3][:, j, SEQ:T], t1, axis=AX.X, op=ALU.add))
                nc.vector.memset(small[:, 190:191], 0.0).then_inc(sem("srw_ready"), 1)
                nc.vector.memset(uc[:, :, :], 0.0)

                def chunks(it, q):
                    wide = lambda name: C(name).rearrange("p (o b) -> p o b", o=1).to_broadcast([P, 2 * GT, HD])

                    def need(who, step):
                        after(dve, who, it, step)

                    def done(ins):
                        ins.then_inc(step_sem["inv.dve"], 1)

                    def masked(src, diag, mask, op=ALU.mult):
                        for hp in HP:
                            ins = tt(diag[hp, :, hp], src[hp], wide(mask)[hp], op)
                        done(ins)

                    def blocks(src, diag):
                        for hp in HP:
                            ins = nc.vector.tensor_copy(diag[hp, :, hp], src[hp])
                        return ins

                    def solution(c):
                        if q is not None:
                            after(dve, "rec.pe", q, f"z{c}")
                            nc.vector.tensor_copy(zc[:, :, :], four(bank(5, 256))).then_inc(step_sem["rec.dve"], 1)

                    def state(c):
                        if q is not None:
                            after(dve, "rec.pe", q, f"st{c}")
                            tt(uc[:, :, :], uc[:, :, :], four(bank(7, 256)), ALU.add).then_inc(step_sem["rec.dve"], 1)
                            after(dve, "rec.dve", q, f"u{c}")
                            k = q * 2 + c
                            d = dcol[:, :, k:k + 1] if isinstance(k, int) else dcol[:, :, bass.ds(k, 1)]
                            tt(uc[:, :, :], uc[:, :, :], d.to_broadcast([P, GT, HD]), ALU.mult).then_inc(step_sem["rec.dve"], 1)

                    def stage(x, src):
                        for hp in HP:
                            ins = ts(diagonal(bd[x], hp), by_chunk(src[hp, :, pair_cols(it, 0, 2 * CH)]), 1.0, None, ALU.mult)
                        done(ins)

                    if it is not None:
                        if not isinstance(it, int):
                            after(dve, "inv.pe", it - 1, "rb")
                        stage("be", FA[1])
                        stage("al", FA[0])
                        need("inv.pe", "at")
                        done(tt(cm["mt"][:, :, :], eight(bank(1)), wide("m_at"), ALU.mult))
                        need("inv.pe", "a")
                        done(tt(cm["m"][:, :, :], eight(bank(0)), wide("m_a"), ALU.mult))
                        need("inv.dve", "m")
                        for hp in HP:
                            ins = nc.vector.tensor_copy(bd["m"][hp, :, hp], cm["m"][hp, :, :])
                        done(ins)
                        done(tt(cm["e"], eight(bank(0)), wide("m_e"), ALU.mult))
                        done(tt(cm["x1"], cm["mt"][:, :, :], wide("stack"), ALU.add))
                        for n, src in enumerate((FA[0], X[0])):
                            ins = nc.vector.tensor_copy(mv[:, n].rearrange("p (c j) t -> p j c t", c=2), by_chunk(src[:, :, pair_cols(it, 0, 2 * CH)]))
                        done(ins)
                    if it is not None:
                        need("inv.pe", "m2t")
                        blocks(eight(bank(3)), bd["m2t"])
                        done(nc.vector.tensor_copy(cm["m2t"], eight(bank(3))))
                    solution(0)
                    if it is not None:
                        need("inv.pe", "x2")
                        done(blocks(two_banks(2, 0), bd["mt"]))
                        done(tt(cm["mt"][:, :, :], two_banks(2, 1), cm["x1"], ALU.add))
                    state(0)
                    if it is not None:
                        need("inv.pe", "x4")
                        need("inv.dve", "x2")
                        done(tt(cm["x1"], eight(bank(0)), cm["mt"][:, :, :], ALU.add))
                        need("inv.pe", "x8")
                        need("inv.dve", "x4")
                        done(tt(cm["m2"][:, :, :], eight(bank(2)), cm["x1"], ALU.add))
                        need("inv.dve", "xt")
                        done(nc.vector.tensor_copy(bd["m2t"][HP[1], :, HP[1]], cm["m2"][HP[1], :, :]))
                    if it is not None:
                        need("inv.pe", "ft")
                        done(blocks(eight(bank(3)), bd["m"]))
                    solution(1)
                    if it is not None:
                        done(tt(cm["m"][:, :, :], wide("stack"), eight(bank(3)), ALU.subtract))
                    state(1)
                    if it is not None:
                        if q is not None:
                            after(dve, "rec.pe", q, "pre1")
                        stage("alu", FA[0])
                        stage("rh", X[0])
                        need("inv.pe", "h")
                        need("inv.dve", "ift")
                        done(tt(cm["mt"][:, :, :], eight(bank(1)), cm["m"][:, :, :], ALU.add))
                        need("inv.pe", "rb")
                        if q is not None:
                            after(dve, "rec.pe", q, "o1")
                        masked(two_banks(2, 0), bd["rbt"], "m_i")
                        need("inv.pe", "ak")
                        masked(two_banks(0, 0), bd["akt"], "m_s")
                        masked(two_banks(0, 1), bd["rkt"], "m_i")

                dve.wait_ge(sem("bd_zeroed"), 14)
                chunks(0, None)
                with dve.Fori(1, NCH // 2) as it:
                    chunks(it, it - 1)
                chunks(None, NCH // 2 - 1)
                for r in range(3):
                    ahead(UB[("mix_out", 0)] + r, r, 0)
                dve.wait_ge(sem("products_ready"), 6)
                for j in range(GT):
                    own(ts(A[2][:, j, :], A[2][:, j, :], V("rk", j), None, ALU.mult))
                own.settle()
                nc.vector.memset(small[:, 190:191], 0.0).then_inc(sem("rkk_ready"), 1)
                stat_rate(2, 40)
                spread_mul(2, X[3], FA[0])
                for j in range(GT):
                    own(ts(X[3][:, j, :], X[3][:, j, :], V("ln", j), V("ln", 4 + j), ALU.mult, ALU.add))
                for j in range(GT):
                    dve.wait_ge(sem("bonus_ready"), j + 1)
                    tt(tok(X[2][:, j, :]), tok(X[2][:, j, :]), halves(4 * (j % 2)), ALU.mult).then_inc(sem("bonus_used"), 1)
                dve.wait_ge(sem("bonus_used"), 4)
                own.settle()
                own(tt(X[3][:, :, :], X[3][:, :, :], X[2][:, :, :], ALU.add))
                own.settle()
                for j in range(GT):
                    tt(A[7][:, j, :], A[7][:, j, :], X[3][:, j, :], ALU.mult).then_inc(sem("ob_ready"), 1)
                    cat_lo(0, j, A[0])
                dve.wait_ge(sem("ob_ready"), 4)
                for k in range(4, 8):
                    cat_lo(0, k, A[7])
                dve.wait_ge(sem("rows_stored"), 64)

            def odd_mix():
                xr, xc = A[3], X[0]
                lam = vcol[:, VEC["lam"][0]:VEC["lam"][0] + 4]

                def mine(ins):
                    own(ins)
                    own.settle()

                mine(ts(lt[:, 16:20], lam, -1.0, None, ALU.mult))
                tt(lt[:, 0:4], lt[:, 16:20], lam, ALU.max).then_inc(sem("lam_abs"), 1)
                dve.wait_ge(sem("lam_pages_loaded"), 32)
                mine(tt(dlam[:, 0, :], dlam[:, 0, :], dlam[:, 1, :], ALU.mult))
                nc.vector.tensor_reduce(lamt[:, 0:1], dlam[:, 0, :], axis=AX.X, op=ALU.add).then_inc(sem("dlam_sums"), 1)
                mine(tt(dlam[:, 2, :], dlam[:, 2, :], dlam[:, 3, :], ALU.mult))
                nc.vector.tensor_reduce(lamt[:, 1:2], dlam[:, 2, :], axis=AX.X, op=ALU.add).then_inc(sem("dlam_sums"), 1)
                dve.wait_ge(psum_free[0], TB[("mix_in", 1)] // 2 + 10)
                own.settle()
                for j in range(GT):
                    own(ts(xc[:, j, :], xr[:, j, :], V("conv_w", 12 + j), V("conv_b", j), ALU.mult, ALU.add))
                own.settle()
                buf = lrucol[:, 0:96].rearrange("p (b t j) -> p j t b", b=NS, t=3)
                for d in range(1, 4):
                    for j in range(GT):
                        w = V("conv_w", 4 * (3 - d) + j)
                        own(stt(xc[:, j, d:SEQ], xr[:, j, 0:SEQ - d], w, xc[:, j, d:SEQ], ALU.mult, ALU.add))
                        own(stt(xc[:, j, SEQ:T], buf[:, j, 3 - d, :], w, xc[:, j, SEQ:T], ALU.mult, ALU.add))
                    own.settle()
                nc.vector.memset(small[:, 190:191], 0.0).then_inc(sem("xc_ready"), 1)
                dve.wait_ge(sem("lam_ln1p"), 2)
                mine(ts(lt[:, 0:4], lt[:, 4:8], 1.0, None, ALU.add))
                mine(ts(lt[:, 0:4], lt[:, 0:4], 1.0, None, ALU.subtract))
                mine(ts(lt[:, 12:16], lt[:, 0:4], 0.0, None, ALU.is_equal))
                mine(tt(lt[:, 12:16], lt[:, 12:16], lt[:, 4:8], ALU.mult))
                mine(ts(lt[:, 0:4], lt[:, 0:4], 1e-30, None, ALU.max))
                mine(nc.vector.reciprocal(lt[:, 0:4], lt[:, 0:4]))
                mine(tt(lt[:, 8:12], lt[:, 8:12], lt[:, 4:8], ALU.mult))
                mine(tt(lt[:, 8:12], lt[:, 8:12], lt[:, 0:4], ALU.mult))
                mine(tt(lt[:, 8:12], lt[:, 8:12], lt[:, 12:16], ALU.add))
                mine(ts(lt[:, 16:20], lt[:, 16:20], 0.0, None, ALU.max))
                mine(tt(lt[:, 8:12], lt[:, 8:12], lt[:, 16:20], ALU.add))
                mine(ts(lru_sp, lt[:, 8:12], 8.0, None, ALU.mult))
                ts(lru_nsp, lt[:, 8:12], -8.0, None, ALU.mult).then_inc(sem("lru_sp_ready"), 1)
                dve.wait_ge(sem("dlam_exp"), 1)
                mine(tt(neglam, lamt[:, 3:4], lamt[:, 2:3], ALU.subtract))
                mine(ts(neglam, neglam, LAM_INIT, None, ALU.subtract))
                dve.wait_ge(sem("gates_copied"), 8)
                own(tt(FA[0][:, :, :], X[2][:, :, :], X[0][:, :, :], ALU.mult))
                dve.wait_ge(sem("lru_decays"), 8)
                mine(tt(FA[1][:, :, :], X[1][:, :, :], X[1][:, :, :], ALU.mult))
                for j in range(GT):
                    own(stt(X[3][:, j, :], FA[1][:, j, :], 1.0, X[3][:, j, :], ALU.add, ALU.mult))
                own.settle()
                nc.vector.memset(small[:, 190:191], 0.0).then_inc(sem("lru_v"), 1)
                dve.wait_ge(sem("lru_root"), 1)
                mine(tt(FA[1][:, :, :], FA[0][:, :, :], X[3][:, :, :], ALU.mult))
                for j in range(GT):
                    own(nc.vector.tensor_tensor_scan(FA[0][:, j, 0:SEQ], X[1][:, j, 0:SEQ], FA[1][:, j, 0:SEQ], 0.0, ALU.mult, ALU.add))
                mine(tt(FA[0][:, :, SEQ:T], X[1][:, :, SEQ:T], lrucol[:, 96:128].rearrange("p (b j) -> p j b", b=NS), ALU.mult))
                mine(tt(FA[0][:, :, SEQ:T], FA[0][:, :, SEQ:T], FA[1][:, :, SEQ:T], ALU.add))
                nc.vector.memset(small[:, 190:191], 0.0).then_inc(sem("lruh_ready"), 1)
                dve.wait_ge(sem("gelu_ready"), 1)
                mine(tt(A[4][:, :, :], A[4][:, :, :], FA[0][:, :, :], ALU.mult))
                dve.wait_ge(sem("lruh_turned"), 1)
                nc.vector.memset(small[:, 190:191], 0.0).then_inc(sem("lru_done"), 1)
                def maxima(n):
                    i = n // 4
                    nk = (i + 1) * P
                    ps = psum[:, 2 * (n % 2):2 * (n % 2) + 2, :]
                    dve.wait_ge(sem("qk2_ready"), n + 1)
                    mine(tt(ps[:, :, i * P:nk], ps[:, :, i * P:nk], C("causal_add").rearrange("p (o b) -> p o b", o=1).to_broadcast([P, 2, P]), ALU.add))
                    mine(nc.vector.tensor_reduce(mx2s[n % 2], ps[:, :, 0:nk], axis=AX.X, op=ALU.max))
                    ts(nb2s[n % 2], mx2s[n % 2], -HD ** -0.5, None, ALU.mult).then_inc(sem("mx_ready"), 1)

                maxima(0)
                maxima(1)
                for n in range(16):
                    nk = (n // 4 + 1) * P
                    dve.wait_ge(sem("exp_done"), 2 * (n + 1))
                    if n:
                        dve.wait_ge(sem("w_ready"), n)
                    mine(nc.vector.reciprocal(rl2, l2s[n % 2]))
                    mine(tt(rl2[:, 1:2], rl2[:, 1:2], neglam, ALU.mult))
                    mine(ts(probs[:, n % 2, 0, 0:nk], probs[:, n % 2, 0, 0:nk], rl2[:, 0:1], None, ALU.mult))
                    stt(probs[:, n % 2, 0, 0:nk], probs[:, n % 2, 1, 0:nk], rl2[:, 1:2], probs[:, n % 2, 0, 0:nk], ALU.mult, ALU.add).then_inc(sem("w_ready"), 1)
                    if n < 14:
                        maxima(n + 2)
                dve.wait_ge(sem("lru_stored"), 80)
                tt(prodn[:, :, :].rearrange("p b h -> p h b"), A[0][:, :, SEQ:T], A[1][:, :, SEQ:T], ALU.mult).then_inc(sem("sdec_ready"), 1)
                dve.wait_ge(sem("pool_keys"), 7 * POOLED)
                for b in range(POOLED, NS):
                    dve.wait_ge(sem(f"kd_loaded{b % 2}"), 64 * (b // 2 + 1))
                    dve.wait_ge(sem("qb_ready"), b + 1)
                    dve.wait_ge(sem("sdec_ready"), b - POOLED + 1)
                    tt(kprod[:, :, :], kd[b % 2][:, :, :], bank(b % 2).rearrange("p (o n) -> p o n", o=1).to_broadcast([P, PAGES, GW]), ALU.mult).then_inc(sem("qb_used"), 1)
                    dve.wait_ge(sem("qb_used"), b - POOLED + 1)
                    for x in range(PAGES):
                        ins = nc.vector.tensor_reduce(sdec[:, :, x, b, :].rearrange("p m h -> p h m"), kprod[:, x, :].rearrange("p (h m d) -> p h m d", h=4, m=2), axis=AX.X, op=ALU.add)
                    ins.then_inc(sem("sdec_ready"), 1)
                dve.wait_ge(sem("sdec_ready"), NS - POOLED + 1)
                nc.vector.memset(wtz[:, :, :], 0.0)
                dve.wait_ge(sem("sd_turned"), 1)
                ps = psum[0:32, 2:4, :]
                mine(nc.vector.tensor_reduce(mxn[0:32], ps, axis=AX.X, op=ALU.max))
                mine(tt(mxn[0:32], mxn[0:32], psum[0:32, 4, 0:2], ALU.max))
                ts(mxn[0:32], mxn[0:32], -HD ** -0.5, None, ALU.mult).then_inc(sem("mxn_ready"), 1)
                dve.wait_ge(sem("expd_done"), 4)
                mine(tt(l2[0:32], l2[0:32], pn2[0:32], ALU.add))
                mine(nc.vector.reciprocal(rl2[0:32], l2[0:32]))
                mine(tt(rl2[0:32, 1:2], rl2[0:32, 1:2], neglam[0:32], ALU.mult))
                mine(ts(pdec[:, 0, :], pdec[:, 0, :], rl2[0:32, 0:1], None, ALU.mult))
                mine(stt(pdec[:, 0, :], pdec[:, 1, :], rl2[0:32, 1:2], pdec[:, 0, :], ALU.mult, ALU.add))
                mine(tt(wn2[0:32], pn2[0:32], rl2[0:32], ALU.mult))
                mine(tt(wn2[0:32, 0:1], wn2[0:32, 0:1], wn2[0:32, 1:2], ALU.add))
                ts(wdiag[:, :], ident[0:32, 0:32], wn2[0:32, 0:1], None, ALU.mult).then_inc(sem("wd_ready"), 1)
                dve.wait_ge(sem("vd_used"), 2)
                tmp = dlam[:, 0, 0:32].rearrange("p (b h) -> p h b", b=NS)
                mine(tt(tmp, A[2][:, :, SEQ:T], psum[:, 6, 0:32].rearrange("p (b h) -> p h b", b=NS), ALU.mult))
                for j in range(4):
                    ins = tt(A[0][:, j, SEQ:T], tmp[:, j], psum[:, 7, j * 33:j * 33 + 29:4], ALU.add)
                ins.then_inc(sem("os2_ready"), 1)
                own(ts(small[:, 188:189], V("subln"), 1.0 - LAM_INIT, None, ALU.mult))
                own.settle()
                for r in range(3):
                    ahead(UB[("mix_out", 1)] + r, r, 0)
                stat_rate(3, 20)
                for k in range(4, 8):
                    cat_lo(1, k, A[4])
                spread_mul(3, A[0], A[0], small[:, 188:189])
                for k in range(4):
                    cat_lo(1, k, A[0])

            def mix_in(i):
                name = ("mix_in", i)

                def body(it, stop):
                    for m in range(4):
                        if not (stop and m):
                            ahead(it * 4 + (UB[name] + m), m)
                        dve.wait_ge(unit_used, it * 4 + (UB[name] + m + 1))
                        tt(one2(u, it * 4 + m), halves(4 * (m % 2)), tok(rbk), ALU.mult).then_inc(psum_free[m % 2], 1)

                n = NT[name] // 4
                with dve.Fori(0, n - 1) as it:
                    body(it, False)
                body(n - 1, True)

            def mix_out(i):
                u0 = UB[("mix_out", i)]
                with dve.Fori(0, 2) as it:
                    for m in range(4):
                        ahead(it * 4 + (u0 + m), m)
                        dve.wait_ge(unit_used, it * 4 + (u0 + m + 1))
                        nc.vector.tensor_copy(one2(f, it * 4 + m), halves(4 * (m % 2))).then_inc(psum_free[m % 2], 1)

            nc.vector.memset(eps_col, EPS).then_inc(sem("eps_set"), 1)
            nc.vector.memset(gn_eps_col, GN_EPS).then_inc(sem("eps_set"), 1)
            dve.wait_ge(sem("rows_turned"), 1)
            for n, (dst, rows) in enumerate(row_tables):
                w = rows.shape[0]
                own(nc.vector.tensor_copy(dst[:, 0:w], psum[:, 6, n * P:n * P + w]))
            own.settle()
            for i in range(2):
                for k in (1, 5):
                    x = (i * 8 + k) * 8
                    own(ts(gcol[:, x:x + 8], gcol[:, x:x + 8], 0.5, None, ALU.mult))
            for k in range(KT):
                dve.wait_ge(sem("xt_turned"), k + 1)
                b = 4 * (k % 2)
                nc.vector.tensor_copy(h[:, k, :], flat[:, b * 512:b * 512 + T]).then_inc(h_ready, 1)
            for r in range(3):
                ahead(r, r, 0)
            own.settle()
            for k in range(KT):
                gained_lo(0, k)
            for i in range(2):
                keep_rate(NORM[(i, 0)])
                ffn(i, 0)
                post(NORM[(i, 1)])
                keep_rate(NORM[(i, 2)])
                mix_in(i)
                (even_mix if i == 0 else odd_mix)()
                mix_out(i)
                post(NORM[(i, 3)])
                keep_rate(NORM[(i, 4)])
                ffn(i, 1)
                post(NORM[(i, 5)])
                keep_rate(NORM[(i, 6)])
                with dve.Fori(0, 2) as it:
                    for m in range(4):
                        ahead(it * 4 + (UB[("gate", i)] + m), m)
                        dve.wait_ge(unit_used, it * 4 + (UB[("gate", i)] + m + 1))
                        tt(one2(f, it * 4 + m), halves(4 * (m % 2)), tok(rbk), ALU.mult).then_inc(psum_free[m % 2], 1)
                for k in range(2):
                    dve.wait_ge(sem("phi_ready"), 2 * i + k + 1)
                    b = (2 + 4 * k) * 512
                    tt(plo[:, k, :], flat[:, b:b + T], phi[:, k, :].bitcast(F32), ALU.subtract).then_inc(sem("plo_ready"), 1)
                dve.wait_ge(sg_ready, SG[("gate", i)] + 8)
                for e in range(4):
                    ahead(UB[("ple", i)] + e, e)
                    for m in range(2):
                        dve.wait_ge(unit_used, UB[("ple", i)] + e + 1)
                        dst = tok(f[:, 2 * e + m, :])
                        tt(dst, halves(4 * m), dst, ALU.mult).then_inc(psum_free[m], 1)
                post(NORM[(i, 7)], i == 1)
            for x in range(5):
                w = P if x < 4 else NS
                dve.wait_ge(sem("y_turned"), x + 1)
                b = 4 * (x % 2) * 512
                dst = stage[:, x, :] if x < 4 else stage_s[:, :]
                nc.vector.tensor_copy(dst, flat[0:w, b:b + D]).then_inc(sem("y_copied"), 1)

        @block.gpsimd
        def _(pool):
            dma = pool.dma_start

            def zero(x, signal):
                nc.gpsimd.memset(x, 0.0).then_inc(signal, 1)

            for dst, src in ROWS[10:]:
                dma(dst, src).then_inc(sem("inputs_loaded"), 16)

            def p_load(i):
                dma(pst[:, :, :], I["p_prompt"][i, 0].rearrange("(x p) d -> p x d", p=P)).then_inc(sem("p_loaded"), 16)
                dma(pss[:, :], I["p_sample"][i, :, 0, :]).then_inc(sem("p_loaded"), 16)

            def squares(*norms):
                for n in norms:
                    for k in range(1, KT - 1):
                        pool.wait_ge(sq_ready, KT * n + k + 1)
                        if k > 1:
                            pool.wait_ge(sq_used, (KT - 2) * n + k - 1)
                        nc.gpsimd.tensor_tensor(sgt[:, 0, :], sgt[:, 0, :], sq[:, k % 2, :], ALU.add).then_inc(sq_used, 1)

            squares(0, 1, 2)
            pool.wait_ge(rb_kept, 2)
            dma(rope[:, :, :], I["rope"].rearrange("p (a t) -> p a t", a=2)).then_inc(sem("tables_loaded"), 16)
            dma(decay[:, :, :, :], I["decay"].rearrange("p (a j t) -> p a j t", a=2, j=GT)).then_inc(sem("tables_loaded"), 16)
            for s in range(2):
                pool.wait_ge(psum_free[s], TB[("mix_in", 0)] // 2 + 16)
            zero(ubd[:, :, :], sem("ubd_ready"))
            for j in range(GT):
                dma(s_ret[:, j, :, :], I["state_ret"][0, :, 2 * j:2 * j + 2].rearrange("b h d v -> (h d) b v")).then_inc(sem("sret_loaded"), 16)
            dma(lw1[:, :, :], I["rwkv_w1"][0].rearrange("(k p) n -> p k n", p=P)).then_inc(sem("lora_loaded"), 16)
            dma(la1[:, :, :], I["rwkv_a1"][0].rearrange("(k p) n -> p k n", p=P)).then_inc(sem("lora_loaded"), 16)
            dma(lg1[:, :, :], I["rwkv_g1"][0].rearrange("(k p) n -> p k n", p=P)).then_inc(sem("lora_loaded"), 16)
            dma(lw2[:, :], I["rwkv_w2"][0]).then_inc(sem("lora_loaded"), 16)
            dma(la2[:, :], I["rwkv_a2"][0]).then_inc(sem("lora_loaded"), 16)
            dma(lg2[:, :], I["rwkv_g2"][0]).then_inc(sem("lora_loaded"), 16)
            pool.wait_ge(sem("shift_copied"), 4)
            dma(O["shift_prompt"][0, 0], shst[0:1, :, :].rearrange("p a b -> p (a b)")).then_inc(sem("rows_stored"), 16)
            dma(O["shift_sample"][0, :, 0, :], shst[1:9, :, :].rearrange("p a b -> p (a b)")).then_inc(sem("rows_stored"), 16)
            pool.wait_ge(sem("qk_ready"), 8)
            dma(reset[:, :], I["reset"]).then_inc(sem("tables_loaded"), 16)
            pool.wait_ge(sem("uout_ready"), 2)
            dma(O["ret_prompt"][0, 0].rearrange("(j h) d v -> (h d) j v", h=2), uout[:, :, :]).then_inc(sem("rows_stored"), 16)
            for j in range(GT):
                pool.wait_ge(sem("sret_ready"), j + 1)
                dma(O["ret_sample"][0, :, 2 * j:2 * j + 2].rearrange("b h d v -> (h d) b v"), s_ret[:, j, :, :]).then_inc(sem("states_stored"), 16)
            pool.wait_ge(sem("l1_ready"), 3)
            pool.wait_ge(sem("rows_stored"), 48)
            pool.wait_ge(sem("states_stored"), 64)
            for x in ("al", "be", "m", "mt", "m2", "m2t", "e", "ka"):
                zero(bd[x][:, :, :], sem("bd_zeroed"))
            nc.gpsimd.tensor_copy(mv[:, 2, :, :], C("stack").rearrange("p (o b) -> p o b", o=1).to_broadcast([P, 2 * GT, HD])).then_inc(sem("bd_zeroed"), 1)
            pool.wait_ge(sem("cs_ready"), 1)
            for j in range(GT):
                dma(s_rw[:, j, :, :], I["state_rwkv"][0, :, 2 * j:2 * j + 2].rearrange("b h v k -> (h v) b k")).then_inc(sem("srw_loaded"), 16)
            ptt = nc.gpsimd.tensor_tensor
            pool.wait_ge(sem("products_ready"), 1)
            ptt(A[2][:, :, :], X[0][:, :, :], X[1][:, :, :], ALU.mult).then_inc(sem("products_ready"), 1)
            pool.wait_ge(sem("products_ready"), 4)
            ptt(X[1][:, :, 0:SEQ], X[1][:, :, 0:SEQ], A[3][:, :, 0:SEQ], ALU.mult).then_inc(sem("products_ready"), 1)
            ptt(X[0][:, :, 0:SEQ], X[0][:, :, 0:SEQ], A[5][:, :, 0:SEQ], ALU.mult).then_inc(sem("products_ready"), 1)
            pool.wait_ge(sem("products_ready"), 6)
            pool.wait_ge(sem("rw_turned"), 1)
            for x in ("alu", "rh", "akt", "rbt", "rkt"):
                zero(bd[x][:, :, :], sem("bd_zeroed"))
            pool.wait_ge(sem("srw_ready"), 1)
            zero(ob[:, :, :], sem("bd_zeroed"))
            for j in range(GT):
                dma(O["rwkv_sample"][0, :, 2 * j:2 * j + 2].rearrange("b h v k -> (h v) b k"), s_rw[:, j, :, :]).then_inc(sem("states_stored"), 16)
            pool.wait_ge(sem("states_stored"), 128)
            for x in ("wt", "bt", "kt"):
                zero(bd[x][:, :, :], sem("bd_zeroed"))
            pool.wait_ge(sem("rwst_ready"), 1)
            dma(O["rwkv_prompt"][0, 0].rearrange("(j h) v k -> v j h k", h=2), rwst[:, :, :].rearrange("p j (h k) -> p j h k", h=2)).then_inc(sem("rows_stored"), 16)
            pool.wait_ge(sem("ob_ready"), 4)
            pool.wait_ge(cat_ready, 8)
            p_load(0)
            squares(3, 4, 5, 6, 7, 8, 9, 10)
            pool.wait_ge(rb_kept, 6)
            dma(dlam[:, :, :], I["diff_lam"][0].rearrange("a (o d) -> o a d", o=1).to_broadcast([P, 4, HD])).then_inc(sem("lam_pages_loaded"), 16)
            dma(pages[:, :], I["page_table"].rearrange("(o b) g -> o (b g)", o=1)).then_inc(sem("lam_pages_loaded"), 16)
            for s in range(2):
                pool.wait_ge(psum_free[s], TB[("mix_in", 1)] // 2 + 10)
            zero(wabd[:, :, :], sem("lruw_zeroed"))
            zero(wibd[:, :, :], sem("lruw_zeroed"))
            pool.wait_ge(sem("lruw_zeroed"), 2)
            for hh, hp in enumerate(HP):
                dma(wabd[hp, :, hp], I["lru_wa"][0, hh::2].rearrange("j d e -> d j e")).then_inc(sem("lruw_loaded"), 16)
                dma(wibd[hp, :, hp], I["lru_wi"][0, hh::2].rearrange("j d e -> d j e")).then_inc(sem("lruw_loaded"), 16)
            pool.wait_ge(sem("lconv_copied"), 1)
            dma(O["lru_conv_prompt"][0, 0], lcst[0:3, :]).then_inc(sem("lru_stored"), 16)
            dma(O["lru_conv_sample"][0, :, 2, :], lcst[3:11, :]).then_inc(sem("lru_stored"), 16)
            dma(O["lru_conv_sample"][0, :, 0:2, :], I["state_lru_conv"][0, :, 1:3, :]).then_inc(sem("lru_stored"), 16)
            pool.wait_ge(sem("lruh_copied"), 1)
            dma(O["lru_h_prompt"][0], lhst[0:1, :]).then_inc(sem("lru_stored"), 16)
            dma(O["lru_h_sample"][0], lhst[1:9, :]).then_inc(sem("lru_stored"), 16)
            pool.wait_ge(sem("kv_copied"), 10)
            dma(O["v_prompt"][0, 0].rearrange("(x p) h d -> p x (h d)", p=P), vtm[:, :, :]).then_inc(sem("kv_y_stored"), 16)
            dma(O["k_prompt"][0, 0].rearrange("(x p) h d -> p x (h d)", p=P), ktm[:, :, :]).then_inc(sem("kv_y_stored"), 16)
            dma(O["v_sample"][0, :, 0].rearrange("b h d -> b (h d)"), vs8o[:, :]).then_inc(sem("kv_y_stored"), 16)
            dma(O["k_sample"][0, :, 0].rearrange("b h d -> b (h d)"), ks8[:, :]).then_inc(sem("kv_y_stored"), 16)
            pool.wait_ge(sem("lru_stored"), 80)
            for b in range(POOLED):
                pool.wait_ge(sem(f"kd_loaded{b % 2}"), 64 * (b // 2 + 1))
                pool.wait_ge(sem("qb_copied"), b + 1)
                if b:
                    pool.wait_ge(sem("pool_keys"), 7 * b)
                nc.gpsimd.tensor_tensor(kprod[:, :, :], kd[b % 2][:, :, :], qb[:, b:b + 1, :].to_broadcast([P, PAGES, GW]), ALU.mult).then_inc(sem("pool_keys"), 1)
                terms = kprod[:, :, :].rearrange("p x (g d) -> p (x g) d", d=HD)
                for n in range(6):
                    pool.wait_ge(sem("pool_keys"), 7 * b + n + 1)
                    w = HD >> (n + 1)
                    if n < 5:
                        ins = nc.gpsimd.tensor_tensor(terms[:, :, 0:w], terms[:, :, 0:w], terms[:, :, w:2 * w], ALU.add)
                    else:
                        t = kprod[:, :, :].rearrange("p x (h m d) -> p m x h d", h=4, m=2)
                        for m in range(2):
                            ins = nc.gpsimd.tensor_tensor(sdec[:, m, :, b, :], t[:, m, :, :, 0], t[:, m, :, :, 1], ALU.add)
                    ins.then_inc(sem("pool_keys"), 1)
            pool.wait_ge(sem("kv_y_stored"), 64)
            pool.wait_ge(cat_ready, 16)
            p_load(1)
            squares(11, 12, 13, 14, 15)
            pool.wait_ge(sem("y_copied"), 5)
            dma(O["y_prompt"][0].rearrange("(x p) d -> p x d", p=P), stage[:, :, :]).then_inc(sem("kv_y_stored"), 16)
            dma(O["y_sample"][:, 0, :], stage_s[:, :]).then_inc(sem("kv_y_stored"), 16)
            pool.wait_ge(sem("rows_stored"), 64)
            pool.wait_ge(sem("states_stored"), 128)
            pool.wait_ge(sem("lru_stored"), 80)
            pool.wait_ge(sem("kv_y_stored"), 64)
            pool.wait_ge(sem("kv_y_stored"), 96)


INS = ["x_prompt", "x_sample", "cache_k", "cache_v", "state_ret", "state_rwkv", "state_rwkv_shift", "state_lru_h",
       "state_lru_conv", "page_table", "p_prompt", "p_sample", "norm_g", "ffn_w_in", "ffn_w_out", "ple_w",
       "ple_gate_w", "ab_w_in", "ab_w_out", "rwkv_mu", "rwkv_w0", "rwkv_w1", "rwkv_w2", "rwkv_a0", "rwkv_a1",
       "rwkv_a2", "rwkv_g1", "rwkv_g2", "rwkv_kk", "rwkv_ka", "rwkv_rk", "rwkv_ln", "cd_w_in", "cd_w_out",
       "diff_lam", "diff_subln", "lru_conv_w", "lru_conv_b", "lru_wa", "lru_ba", "lru_wi", "lru_bi", "lru_lambda"]
OUTS = [("y_prompt", (1, SEQ, D)), ("y_sample", (NS, 1, D)), ("k_prompt", (1, 1, SEQ, 4, 128)),
        ("v_prompt", (1, 1, SEQ, 4, 128)), ("ret_prompt", (1, 1, 8, HD, HD)), ("rwkv_prompt", (1, 1, 8, HD, HD)),
        ("shift_prompt", (1, 1, 1, 4 * GW)), ("lru_h_prompt", (1, 1, GW)), ("lru_conv_prompt", (1, 1, 3, GW)),
        ("k_sample", (1, NS, 1, 4, 128)), ("v_sample", (1, NS, 1, 4, 128)), ("ret_sample", (1, NS, 8, HD, HD)),
        ("rwkv_sample", (1, NS, 8, HD, HD)), ("shift_sample", (1, NS, 1, 4 * GW)), ("lru_h_sample", (1, NS, GW)),
        ("lru_conv_sample", (1, NS, 3, GW))]


def kernel(**inputs):
    import concourse.bacc as bacc
    from concourse.bass_utils import run_bass_kernel_spmd

    nc = bacc.Bacc("TRN2", target_bir_lowering=False, num_devices=1)
    arrays = {f"in_{n}": np.ascontiguousarray(inputs[n]) for n in INS}
    for n, a in zip(("consts", "rope", "decay", "reset"), host_constants()):
        arrays[f"in_{n}"] = a
    I = {n[3:]: nc.dram_tensor(n, a.shape, mybir.dt.from_np(a.dtype), kind="ExternalInput").ap() for n, a in arrays.items()}
    O = {n: nc.dram_tensor(f"out_{n}", s, F32, kind="ExternalOutput").ap() for n, s in OUTS}
    build(nc, I, O)
    r = run_bass_kernel_spmd(nc, [arrays], core_ids=[0])
    return tuple(r.results[0][f"out_{n}"] for n, _ in OUTS)
```
